# Optimizing a Trainium2 kernel written in Bass

```python
import math
import jax, jax.numpy as jnp
from jax import lax
import numpy as np

D_MODEL = 2048
BATCH = 1
SEQ = 256
DEPTH = 1

HEAD_DIM = 128
GRID_W = 64
Q_BLOCK = 128
A_Q_HEADS = 8
A_KV_HEADS = 2
A_GROUP = A_Q_HEADS // A_KV_HEADS
B_HEADS = 8
WIN_ROWS_MAX = 8
WIN_COLS = 16
A_WIDTH = A_Q_HEADS * HEAD_DIM
B_WIDTH = B_HEADS * HEAD_DIM
MIX_WIDTH = A_WIDTH + B_WIDTH
A_KV_WIDTH = A_KV_HEADS * HEAD_DIM
IN_WIDTH = A_WIDTH + 2 * A_KV_WIDTH + 3 * B_WIDTH
D_FF = 4 * D_MODEL
PLE_DIM = 256
ROPE_THETA = 10000.0
ROPE_AXIS_DIM = HEAD_DIM // 2
NORM_EPS = 1e-6


def rms_norm(x, g):
    xf = x.astype(jnp.float32)
    y = xf * lax.rsqrt(jnp.mean(xf * xf, axis=-1, keepdims=True) + NORM_EPS)
    return (y * g.astype(jnp.float32)).astype(x.dtype)

def rope_half(x, ang):
    n = ang.shape[-1]
    shape = (1, ang.shape[0]) + (1,) * (x.ndim - 3) + (n,)
    cos = jnp.cos(ang).reshape(shape)
    sin = jnp.sin(ang).reshape(shape)
    xf = x.astype(jnp.float32)
    x1, x2 = xf[..., :n], xf[..., n:]
    return jnp.concatenate([x1 * cos - x2 * sin, x2 * cos + x1 * sin], axis=-1).astype(x.dtype)

def axial_rope(x, ang_row, ang_col):
    return jnp.concatenate([rope_half(x[..., :ROPE_AXIS_DIM], ang_row),
                            rope_half(x[..., ROPE_AXIS_DIM:], ang_col)], axis=-1)

def to_blocks(a):
    b, s = a.shape[0], a.shape[1]
    a = a.reshape((b, s // Q_BLOCK, Q_BLOCK) + a.shape[2:])
    return jnp.moveaxis(a, 1, 0)

def from_blocks(a):
    a = jnp.moveaxis(a, 0, 1)
    return a.reshape((a.shape[0], a.shape[1] * a.shape[2]) + a.shape[3:])

def global_gqa(q, k, v):
    scale = 1.0 / math.sqrt(HEAD_DIM)

    def block(qb):
        s = jnp.einsum('bqkgd,bskd->bkgqs', qb, k).astype(jnp.float32) * scale
        w = jax.nn.softmax(s, axis=-1).astype(v.dtype)
        return jnp.einsum('bkgqs,bskd->bqkgd', w, v)

    o = lax.map(block, to_blocks(q))
    return from_blocks(o)

def neighbourhood_attn(q, k, v, rpb, rows):
    s_len = q.shape[1]
    win_r = min(WIN_ROWS_MAX, rows)
    scale = 1.0 / math.sqrt(HEAD_DIM)
    t_blocks = jnp.arange(s_len, dtype=jnp.int32).reshape(s_len // Q_BLOCK, Q_BLOCK)
    ar_r = jnp.arange(win_r, dtype=jnp.int32)
    ar_c = jnp.arange(WIN_COLS, dtype=jnp.int32)

    def block(args):
        qb, t = args
        r = t // GRID_W
        c = t % GRID_W
        r0 = jnp.clip(r - win_r // 2, 0, rows - win_r)
        c0 = jnp.clip(c - WIN_COLS // 2, 0, GRID_W - WIN_COLS)
        kr = r0[:, None] + ar_r[None, :]
        kc = c0[:, None] + ar_c[None, :]
        idx = (kr[:, :, None] * GRID_W + kc[:, None, :]).reshape(Q_BLOCK, win_r * WIN_COLS)
        dr = kr - r[:, None] + (WIN_ROWS_MAX - 1)
        dc = kc - c[:, None] + (WIN_COLS - 1)
        bias = rpb[:, dr[:, :, None], dc[:, None, :]].reshape(B_HEADS, Q_BLOCK, win_r * WIN_COLS)
        kg = k[:, idx]
        vg = v[:, idx]
        s = jnp.einsum('bqhd,bqnhd->bhqn', qb, kg).astype(jnp.float32) * scale
        s = s + bias.astype(jnp.float32)[None]
        w = jax.nn.softmax(s, axis=-1).astype(vg.dtype)
        return jnp.einsum('bhqn,bqnhd->bqhd', w, vg)

    o = lax.map(block, (to_blocks(q), t_blocks))
    return from_blocks(o)

def first_inputs(seed: int = 0) -> dict:
    key = jax.random.key(seed)
    ks = jax.random.split(key, 20)
    f32 = jnp.float32

    def w(k, shape, fan_in):
        return jax.random.normal(k, shape, f32) * (fan_in ** -0.5)

    def gain(k, shape):
        return 1.0 + 0.05 * jax.random.normal(k, shape, f32)

    return {
        "x": jax.random.normal(ks[0], (BATCH, SEQ, D_MODEL), f32),
        "p": jax.random.normal(ks[1], (DEPTH, BATCH, SEQ, PLE_DIM), f32),
        "pre_mix_norm": gain(ks[2], (DEPTH, D_MODEL)),
        "w_in": w(ks[3], (DEPTH, D_MODEL, IN_WIDTH), D_MODEL),
        "q_norm": gain(ks[4], (DEPTH, HEAD_DIM)),
        "k_norm": gain(ks[5], (DEPTH, HEAD_DIM)),
        "rel_pos_bias": 0.1 * jax.random.normal(ks[6], (DEPTH, B_HEADS, 2 * WIN_ROWS_MAX - 1, 2 * WIN_COLS - 1), f32),
        "w_o": w(ks[7], (DEPTH, MIX_WIDTH, D_MODEL), MIX_WIDTH),
        "post_mix_norm": gain(ks[8], (DEPTH, D_MODEL)),
        "pre_mlp_norm": gain(ks[9], (DEPTH, D_MODEL)),
        "w_up": w(ks[10], (DEPTH, D_MODEL, D_FF), D_MODEL),
        "w_down": w(ks[11], (DEPTH, D_FF, D_MODEL), D_FF),
        "post_mlp_norm": gain(ks[12], (DEPTH, D_MODEL)),
        "pre_ple_norm": gain(ks[13], (DEPTH, D_MODEL)),
        "w_ple_gate": w(ks[14], (DEPTH, D_MODEL, D_MODEL), D_MODEL),
        "w_ple_proj": w(ks[15], (DEPTH, PLE_DIM, D_MODEL), PLE_DIM),
        "post_ple_norm": gain(ks[16], (DEPTH, D_MODEL)),
    }

def first_block(x, p, pre_mix_norm, w_in, q_norm, k_norm, rel_pos_bias, w_o, post_mix_norm,
              pre_mlp_norm, w_up, w_down, post_mlp_norm, pre_ple_norm, w_ple_gate, w_ple_proj,
              post_ple_norm):
    b, s_len, _ = x.shape
    rows = s_len // GRID_W
    t = jnp.arange(s_len, dtype=jnp.int32)
    row = (t // GRID_W).astype(jnp.float32)
    col = (t % GRID_W).astype(jnp.float32)
    n_freq = ROPE_AXIS_DIM // 2
    freqs = ROPE_THETA ** (-jnp.arange(n_freq, dtype=jnp.float32) / n_freq)
    ang_row = row[:, None] * freqs[None, :]
    ang_col = col[:, None] * freqs[None, :]

    h = x
    for i in range(DEPTH):
        xn = rms_norm(h, pre_mix_norm[i])
        proj = xn @ w_in[i]
        o0 = A_WIDTH
        o1 = o0 + A_KV_WIDTH
        o2 = o1 + A_KV_WIDTH
        o3 = o2 + B_WIDTH
        o4 = o3 + B_WIDTH
        qa = proj[..., :o0].reshape(b, s_len, A_KV_HEADS, A_GROUP, HEAD_DIM)
        ka = proj[..., o0:o1].reshape(b, s_len, A_KV_HEADS, HEAD_DIM)
        va = proj[..., o1:o2].reshape(b, s_len, A_KV_HEADS, HEAD_DIM)
        qb = proj[..., o2:o3].reshape(b, s_len, B_HEADS, HEAD_DIM)
        kb = proj[..., o3:o4].reshape(b, s_len, B_HEADS, HEAD_DIM)
        vb = proj[..., o4:].reshape(b, s_len, B_HEADS, HEAD_DIM)

        qa = axial_rope(rms_norm(qa, q_norm[i]), ang_row, ang_col)
        ka = axial_rope(rms_norm(ka, k_norm[i]), ang_row, ang_col)
        out_a = global_gqa(qa, ka, va).reshape(b, s_len, A_WIDTH)
        out_b = neighbourhood_attn(qb, kb, vb, rel_pos_bias[i], rows).reshape(b, s_len, B_WIDTH)

        mix = jnp.concatenate([out_a, out_b], axis=-1) @ w_o[i]
        h = h + rms_norm(mix, post_mix_norm[i])

        m = rms_norm(h, pre_mlp_norm[i]) @ w_up[i]
        m = jnp.square(jax.nn.relu(m)) @ w_down[i]
        h = h + rms_norm(m, post_mlp_norm[i])

        gate = jax.nn.sigmoid(rms_norm(h, pre_ple_norm[i]) @ w_ple_gate[i])
        e = (p[i] @ w_ple_proj[i]) * gate
        h = h + rms_norm(e, post_ple_norm[i])
    return h


CTX_LEN = 256
D_CONV = D_MODEL // 2
CONV_WIDTH = 31
CONV_PAD = (CONV_WIDTH - 1) // 2
D_HGRN = D_MODEL // 2
HGRN_HEAD_DIM = 128
HGRN_HEADS = D_HGRN // HGRN_HEAD_DIM
HGRN_CHUNK = 64
D_FF_2 = 4 * D_MODEL
N_MOD = 6
EPS = 1e-6
D_IN = 5 * D_HGRN + 2 * D_CONV + 2 * D_MODEL


def rms_norm_2(x, g):
    xf = x.astype(jnp.float32)
    y = xf * lax.rsqrt(jnp.mean(xf * xf, axis=-1, keepdims=True) + EPS)
    return (y * g.astype(jnp.float32)).astype(x.dtype)

def layer_norm(x, g, b):
    xf = x.astype(jnp.float32)
    mu = jnp.mean(xf, axis=-1, keepdims=True)
    var = jnp.mean(jnp.square(xf - mu), axis=-1, keepdims=True)
    y = (xf - mu) * lax.rsqrt(var + EPS)
    return (y * g.astype(jnp.float32) + b.astype(jnp.float32)).astype(x.dtype)

def modulate(h, shift, scale):
    return h * (1 + scale) + shift

def split_proj(p):
    cuts = [D_HGRN, 2 * D_HGRN, 3 * D_HGRN, 4 * D_HGRN, 5 * D_HGRN,
            5 * D_HGRN + D_CONV, 5 * D_HGRN + 2 * D_CONV, 5 * D_HGRN + 2 * D_CONV + D_MODEL]
    return jnp.split(p, cuts, axis=-1)

def dwconv1d(u, w, b):
    ch = u.shape[-1]
    y = lax.conv_general_dilated(u, w[:, None, :].astype(u.dtype), window_strides=(1,),
                                 padding=[(CONV_PAD, CONV_PAD)],
                                 dimension_numbers=('NWC', 'WIO', 'NWC'),
                                 feature_group_count=ch)
    return y + b

def axial_dwconv(u, w, b, rows):
    bsz, seq, ch = u.shape
    half = ch // 2
    uh = u[..., :half].reshape(bsz * rows, GRID_W, half)
    yh = dwconv1d(uh, w[:, :half], b[:half]).reshape(bsz, seq, half)
    uv = u[..., half:].reshape(bsz, rows, GRID_W, ch - half).transpose(0, 2, 1, 3)
    uv = uv.reshape(bsz * GRID_W, rows, ch - half)
    yv = dwconv1d(uv, w[:, half:], b[half:]).reshape(bsz, GRID_W, rows, ch - half)
    yv = yv.transpose(0, 2, 1, 3).reshape(bsz, seq, ch - half)
    return jnp.concatenate([yh, yv], axis=-1)

def conformer_branch(val, gate, w_dw, b_dw, ln_g, ln_b, w_pw, rows):
    u = val * jax.nn.sigmoid(gate)
    u = dwconv1d(u, w_dw, b_dw) if rows is None else axial_dwconv(u, w_dw, b_dw, rows)
    u = jax.nn.silu(layer_norm(u, ln_g, ln_b))
    return u @ w_pw

def to_heads(t):
    return t.reshape(t.shape[:-1] + (HGRN_HEADS, HGRN_HEAD_DIM))

def hgrn_forget(f_raw, lb):
    f = lb + (1.0 - lb) * jax.nn.sigmoid(f_raw.astype(jnp.float32))
    return to_heads(jnp.log(f)), to_heads(1.0 - f)

def q_prep(p_q):
    return to_heads(jax.nn.silu(p_q.astype(jnp.float32))) * (HGRN_HEAD_DIM ** -0.5)

def hgrn_chunk_scan(q, k, v, logf, s0):
    bsz, seq = q.shape[:2]
    n_chunks = seq // HGRN_CHUNK

    def to_chunks(t):
        return t.reshape(bsz, n_chunks, HGRN_CHUNK, HGRN_HEADS, t.shape[-1]).transpose(1, 0, 3, 2, 4)

    tri = jnp.tril(jnp.ones((HGRN_CHUNK, HGRN_CHUNK), dtype=bool))

    def step(s, xs):
        qc, kc, vc, gc = xs
        a = jnp.cumsum(gc, axis=2)
        a_last = a[:, :, -1:, :]
        inter = jnp.einsum('bhtk,bhkv->bhtv', qc * jnp.exp(a), s)
        diff = a[:, :, :, None, :] - a[:, :, None, :, :]
        decay = jnp.exp(jnp.where(tri[:, :, None], diff, -jnp.inf))
        scores = jnp.einsum('bhtk,bhsk,bhtsk->bhts', qc, kc, decay)
        intra = jnp.einsum('bhts,bhsv->bhtv', scores, vc)
        s_new = jnp.exp(a_last[:, :, 0, :])[..., None] * s + \
            jnp.einsum('bhsk,bhsv->bhkv', kc * jnp.exp(a_last - a), vc)
        return s_new, inter + intra

    s_fin, out = lax.scan(step, s0, (to_chunks(q), to_chunks(k), to_chunks(v), to_chunks(logf)))
    out = out.transpose(1, 0, 3, 2, 4).reshape(bsz, seq, HGRN_HEADS, HGRN_HEAD_DIM)
    return out, s_fin

def hgrn_final_state(k, v, logf):
    a = jnp.cumsum(logf, axis=1)
    return jnp.einsum('blhk,blhv->bhkv', k * jnp.exp(a[:, -1:] - a), v)

def hgrn_bidir(q, v, gf, gb, s0f, s0b):
    o_f, s_f = hgrn_chunk_scan(q, gf[1], v, gf[0], s0f)
    fl = lambda t: jnp.flip(t, axis=1)
    o_b, s_b = hgrn_chunk_scan(fl(q), fl(gb[1]), fl(v), fl(gb[0]), s0b)
    return o_f + fl(o_b), s_f, s_b

def hgrn_readout(o, g, norm_g, w_o):
    o = rms_norm_2(o, norm_g.reshape(HGRN_HEADS, HGRN_HEAD_DIM))
    o = o.reshape(o.shape[:2] + (D_HGRN,)).astype(g.dtype) * jax.nn.silu(g)
    return o @ w_o

def gated_merge(y_conv, y_hgrn, p_gc, p_gh, w_o):
    return (jax.nn.sigmoid(p_gc) * y_conv + jax.nn.sigmoid(p_gh) * y_hgrn) @ w_o

def sq_relu_mlp(h, w1, w2):
    return jnp.square(jax.nn.relu(h @ w1)) @ w2

def second_inputs(seed: int = 0) -> dict:
    key = jax.random.key(seed)
    ks = jax.random.split(key, 24)
    f32 = jnp.float32

    def nrm(k, shape, scale):
        return jax.random.normal(k, shape, f32) * scale

    def gain(k, shape):
        return 1.0 + 0.05 * jax.random.normal(k, shape, f32)

    return {
        'x': nrm(ks[0], (BATCH, SEQ, D_MODEL), 1.0),
        'c': nrm(ks[1], (BATCH, D_MODEL), 1.0),
        'ctx': nrm(ks[2], (BATCH, CTX_LEN, D_MODEL), 1.0),
        'c_ctx': nrm(ks[3], (D_MODEL,), 1.0),
        'w_mod': nrm(ks[4], (DEPTH, D_MODEL, N_MOD * D_MODEL), 0.5 * D_MODEL ** -0.5),
        'b_mod': nrm(ks[5], (DEPTH, N_MOD * D_MODEL), 0.02),
        'norm_pre_mix': gain(ks[6], (DEPTH, D_MODEL)),
        'norm_post_mix': gain(ks[7], (DEPTH, D_MODEL)),
        'norm_pre_mlp': gain(ks[8], (DEPTH, D_MODEL)),
        'norm_post_mlp': gain(ks[9], (DEPTH, D_MODEL)),
        'w_in': nrm(ks[10], (DEPTH, D_MODEL, D_IN), D_MODEL ** -0.5),
        'conv_dw_w': nrm(ks[11], (DEPTH, CONV_WIDTH, D_CONV), CONV_WIDTH ** -0.5),
        'conv_dw_b': nrm(ks[12], (DEPTH, D_CONV), 0.02),
        'conv_ln_g': gain(ks[13], (DEPTH, D_CONV)),
        'conv_ln_b': nrm(ks[14], (DEPTH, D_CONV), 0.02),
        'conv_pw_w': nrm(ks[15], (DEPTH, D_CONV, D_MODEL), D_CONV ** -0.5),
        'hgrn_lb_logits': nrm(ks[16], (2, DEPTH + 1, D_HGRN), 0.5),
        'hgrn_norm_g': gain(ks[17], (DEPTH, D_HGRN)),
        'hgrn_out_w': nrm(ks[18], (DEPTH, D_HGRN, D_MODEL), D_HGRN ** -0.5),
        'w_out': nrm(ks[19], (DEPTH, D_MODEL, D_MODEL), D_MODEL ** -0.5),
        'mlp_w1': nrm(ks[20], (DEPTH, D_MODEL, D_FF_2), D_MODEL ** -0.5),
        'mlp_w2': nrm(ks[21], (DEPTH, D_FF_2, D_MODEL), D_FF_2 ** -0.5),
    }

def second_block(x, c, ctx, c_ctx, w_mod, b_mod, norm_pre_mix, norm_post_mix, norm_pre_mlp, norm_post_mlp,
              w_in, conv_dw_w, conv_dw_b, conv_ln_g, conv_ln_b, conv_pw_w, hgrn_lb_logits, hgrn_norm_g,
              hgrn_out_w, w_out, mlp_w1, mlp_w2):
    f32 = jnp.float32
    rows = x.shape[1] // GRID_W
    lb_all = jnp.cumsum(jax.nn.softmax(hgrn_lb_logits.astype(f32), axis=1), axis=1)
    xc = ctx
    for l in range(DEPTH):
        last = l == DEPTH - 1
        mod = jax.nn.silu(c) @ w_mod[l] + b_mod[l]
        sh_m, sc_m, ga_m, sh_f, sc_f, ga_f = [m[:, None, :] for m in jnp.split(mod, N_MOD, axis=-1)]
        mod_c = jax.nn.silu(c_ctx) @ w_mod[l] + b_mod[l]
        shc_m, scc_m, gac_m, shc_f, scc_f, gac_f = jnp.split(mod_c, N_MOD, axis=-1)
        lb_f, lb_b = lb_all[0, l], lb_all[1, l]

        hc = modulate(rms_norm_2(xc, norm_pre_mix[l]), shc_m, scc_m)
        if last:
            pc_i, pc_ff, pc_fb = jnp.split(hc @ w_in[l][:, :3 * D_HGRN], 3, axis=-1)
            vc = to_heads(pc_i.astype(f32))
            lfc_f, kc_f = hgrn_forget(pc_ff, lb_f)
            lfc_b, kc_b = hgrn_forget(pc_fb, lb_b)
            s_f = hgrn_final_state(kc_f, vc, lfc_f)
            s_b = hgrn_final_state(jnp.flip(kc_b, 1), jnp.flip(vc, 1), jnp.flip(lfc_b, 1))
        else:
            pc = split_proj(hc @ w_in[l])
            vc = to_heads(pc[0].astype(f32))
            zeros = jnp.zeros((xc.shape[0], HGRN_HEADS, HGRN_HEAD_DIM, HGRN_HEAD_DIM), f32)
            oc, s_f, s_b = hgrn_bidir(q_prep(pc[3]), vc, hgrn_forget(pc[1], lb_f),
                                      hgrn_forget(pc[2], lb_b), zeros, zeros)
            yc_h = hgrn_readout(oc, pc[4], hgrn_norm_g[l], hgrn_out_w[l])
            yc_c = conformer_branch(pc[5], pc[6], conv_dw_w[l], conv_dw_b[l], conv_ln_g[l], conv_ln_b[l],
                                    conv_pw_w[l], None)
            yc = gated_merge(yc_c, yc_h, pc[7], pc[8], w_out[l])
            xc_next = xc + gac_m * rms_norm_2(yc, norm_post_mix[l])
            hc2 = modulate(rms_norm_2(xc_next, norm_pre_mlp[l]), shc_f, scc_f)
            xc_next = xc_next + gac_f * rms_norm_2(sq_relu_mlp(hc2, mlp_w1[l], mlp_w2[l]), norm_post_mlp[l])

        h = modulate(rms_norm_2(x, norm_pre_mix[l]), sh_m, sc_m)
        p_i, p_ff, p_fb, p_q, p_g, p_cv, p_cg, p_gc, p_gh = split_proj(h @ w_in[l])
        o, _, _ = hgrn_bidir(q_prep(p_q), to_heads(p_i.astype(f32)), hgrn_forget(p_ff, lb_f),
                             hgrn_forget(p_fb, lb_b), s_f, s_b)
        y_h = hgrn_readout(o, p_g, hgrn_norm_g[l], hgrn_out_w[l])
        y_c = conformer_branch(p_cv, p_cg, conv_dw_w[l], conv_dw_b[l], conv_ln_g[l], conv_ln_b[l],
                               conv_pw_w[l], rows)
        y = gated_merge(y_c, y_h, p_gc, p_gh, w_out[l])
        x = x + ga_m * rms_norm_2(y, norm_post_mix[l])
        h2 = modulate(rms_norm_2(x, norm_pre_mlp[l]), sh_f, sc_f)
        x = x + ga_f * rms_norm_2(sq_relu_mlp(h2, mlp_w1[l], mlp_w2[l]), norm_post_mlp[l])

        if not last:
            xc = xc_next
    return x


def setup_inputs(seed=0):
    out = dict(first_inputs(seed))
    for name, value in second_inputs(seed + 1).items():
        if name != "x":
            out[name + "_2"] = value
    return out


def reference(
    x, p, pre_mix_norm, w_in, q_norm, k_norm, rel_pos_bias, w_o, post_mix_norm, pre_mlp_norm,
    w_up, w_down, post_mlp_norm, pre_ple_norm, w_ple_gate, w_ple_proj, post_ple_norm, c_2,
    ctx_2, c_ctx_2, w_mod_2, b_mod_2, norm_pre_mix_2, norm_post_mix_2, norm_pre_mlp_2,
    norm_post_mlp_2, w_in_2, conv_dw_w_2, conv_dw_b_2, conv_ln_g_2, conv_ln_b_2, conv_pw_w_2,
    hgrn_lb_logits_2, hgrn_norm_g_2, hgrn_out_w_2, w_out_2, mlp_w1_2, mlp_w2_2,
):
    x = first_block(
        x, p, pre_mix_norm, w_in, q_norm, k_norm, rel_pos_bias, w_o, post_mix_norm,
        pre_mlp_norm, w_up, w_down, post_mlp_norm, pre_ple_norm, w_ple_gate, w_ple_proj,
        post_ple_norm,
    )
    return second_block(
        x, c_2, ctx_2, c_ctx_2, w_mod_2, b_mod_2, norm_pre_mix_2, norm_post_mix_2,
        norm_pre_mlp_2, norm_post_mlp_2, w_in_2, conv_dw_w_2, conv_dw_b_2, conv_ln_g_2,
        conv_ln_b_2, conv_pw_w_2, hgrn_lb_logits_2, hgrn_norm_g_2, hgrn_out_w_2, w_out_2,
        mlp_w1_2, mlp_w2_2,
    )


_drawn_inputs = setup_inputs


def setup_inputs(seed=0):
    import zlib

    import numpy as np

    out = dict(_drawn_inputs(seed))
    spreads = {}
    factors = {'q_norm': 3.73,
     'k_norm': 3.203,
     'pre_ple_norm': 5.635,
     'ctx_2': 8.0,
     'c_ctx_2': 8.0,
     'b_mod_2': 3.637,
     'norm_pre_mix_2': 5.952,
     'norm_post_mix_2': 7.9,
     'norm_pre_mlp_2': 6.643,
     'norm_post_mlp_2': 7.849,
     'conv_dw_b_2': 64.0,
     'conv_ln_g_2': 64.0,
     'conv_ln_b_2': 200.0,
     'hgrn_lb_logits_2': 8.0,
     'hgrn_norm_g_2': 8.0}
    for name, (base, spread) in spreads.items():
        noise = np.random.default_rng([zlib.crc32(name.encode()), seed]).standard_normal(out[name].shape)
        drawn = base * np.exp(spread * noise) if base else spread * noise
        out[name] = __import__('jax').numpy.asarray(drawn.astype(out[name].dtype))
    for name, factor in factors.items():
        out[name] = (out[name] * factor).astype(out[name].dtype)
    return out
```

```python
from contextlib import ExitStack

import numpy as np

import concourse.bass as bass
from concourse import mybir

ALU = mybir.AluOpType
ACT = mybir.ActivationFunctionType
F32 = mybir.dt.float32
F32R = mybir.dt.float32r
I8 = mybir.dt.int8
AX_X = mybir.AxisListType.X

P = 128
T = 256
TH = T // P
D = 2048
KT = D // P
NCH = 512
HD = 128
GRID = 64
ROWS = T // GRID
A_Q, A_KV, B_H = 8, 2, 8
IN1 = (A_Q + 2 * A_KV + 3 * B_H) * HD
DFF = 4 * D
PLE = 256
RPB_R, RPB_C = 15, 31
WIN = 16
EPS = 1e-6
SCALE = float(HD) ** -0.5
DH = 1024
HH = DH // HD
TAPS = 31
NSLOT = 4
NMOD = 6
FAR = -1e30

VEC_GROUPS = [
    [("pre_mix_norm", 16), ("pre_mlp_norm", 16), ("pre_ple_norm", 16), ("norm_pre_mix_2", 16),
     ("norm_pre_mlp_2", 16), ("norm_post_mix_2", 16), ("norm_post_mlp_2", 16)],
    [("b_mod_2", 96), ("c_2", 16), ("c_ctx_2", 16)],
    [("conv_dw_w_2a", 128)],
    [("conv_dw_w_2b", 120)],
    [("conv_dw_b_2", 8), ("conv_ln_g_2", 8), ("conv_ln_b_2", 8)],
]
COL = {}
_n = 0
for _g in VEC_GROUPS:
    for _name, _rows in _g:
        COL[_name] = _n
        _n += _rows
NCOL = _n

LEVELS = [64, 32, 16, 8, 4, 2, 1]
NHEAD = B_H + A_Q
HEAD_KT = [A_Q + h for h in range(B_H)] + list(range(A_Q))
MODS = ["normc", "norm3", "norm4"]
NORMS = ["norm0", "norm1", "norm2"] + MODS
POSTS = ["post0", "post1", "post2", "post3", "post4"]
N_CONV = HH + (HH // 2) * 2 * (TAPS // 2) + (HH // 2) * 2 * (ROWS - 1)


def shape_constants():
    t = np.arange(T)
    n = HD // 4
    freq = (np.float32(10000.0) ** (-np.arange(n, dtype=np.float32) / np.float32(n))).astype(np.float32)
    ar = (t // GRID).astype(np.float32)[:, None] * freq[None]
    ac = (t % GRID).astype(np.float32)[:, None] * freq[None]
    cos = np.concatenate([np.cos(ar), np.cos(ar), np.cos(ac), np.cos(ac)], 1)
    sin = np.concatenate([-np.sin(ar), np.sin(ar), -np.sin(ac), np.sin(ac)], 1)
    rope = np.stack([cos, sin]).astype(np.float32)
    rope = rope.reshape(2, TH, P, HD).transpose(2, 0, 1, 3).reshape(P, -1)
    c = np.arange(P) % GRID
    c0 = np.clip(c - WIN // 2, 0, GRID - WIN)
    kc = np.arange(GRID)
    inside = (kc[None] >= c0[:, None]) & (kc[None] < c0[:, None] + WIN)
    colmask = np.where(inside, 0.0, FAR).astype(np.float32)
    ident = np.eye(P, dtype=np.float32)
    sel = np.zeros((P, 2), np.float32)
    sel[0, 0] = sel[2, 0] = sel[1, 1] = sel[3, 1] = 1.0
    small = np.concatenate([ident, np.ones((P, P), np.float32), sel], 1)
    j = np.arange(P)[:, None]
    q = np.arange(P)[None]
    sums, masks = [], []
    for m in LEVELS:
        mid = q // (2 * m) * (2 * m) + m
        second = q >= mid
        sums.append(np.where(second, (j >= mid) & (j <= q), (j > q) & (j < mid)))
    for m in LEVELS:
        mid = q // (2 * m) * (2 * m) + m
        second = q >= mid
        sums.append(np.where(second, (j >= mid) & (j < q), (j >= q) & (j < mid)))
    sums += [j <= q, j > q, j >= q, j < q]
    s, tt = j, q
    for m in LEVELS:
        same = s // (2 * m) == tt // (2 * m)
        masks.append(same & (s % (2 * m) < m) & (tt % (2 * m) >= m))
    for m in LEVELS:
        same = s // (2 * m) == tt // (2 * m)
        masks.append(same & (s % (2 * m) >= m) & (tt % (2 * m) < m))
    masks.append(s == tt)
    sums = np.concatenate([x.astype(np.float32) for x in sums], 1)
    masks = np.concatenate([x.astype(np.float32) for x in masks], 1)
    early = np.concatenate([rope, colmask], 1)
    return {"k_small": small, "k_early": np.ascontiguousarray(early),
            "k_sums": np.ascontiguousarray(sums), "k_masks": np.ascontiguousarray(masks)}


def build(nc, I, out):
    ctx = ExitStack()
    with ctx:
        base = nc.sbuf_base + (-nc.sbuf_base) % 64
        limit = nc.sbuf_usable_end
        cursor = [base]

        def at(name, shape, dt, offset):
            size = int(np.prod(shape[1:])) * (1 if dt == I8 else 4)
            assert offset + size <= limit, (name, offset + size, limit)
            return nc.alloc_sbuf_tensor_at(name, shape, dt, offset=offset)

        def sb(name, shape, dt):
            size = int(np.prod(shape[1:])) * (1 if dt == I8 else 4)
            t = at(name, shape, dt, cursor[0])
            cursor[0] += size + (-size) % 32
            return t

        def sem(name):
            return ctx.enter_context(nc.semaphore(name))

        K = 1024
        raw = sb("raw", [P, NSLOT, 2, NCH], F32)
        whi = sb("whi", [P, NSLOT, 2, NCH], F32R)
        wlo = sb("wlo", [P, NSLOT, 2, NCH], F32R)
        xhi_at = cursor[0]
        xhi = sb("xhi", [P, KT, T], F32R)
        xlo_at = cursor[0]
        xlo = sb("xlo", [P, KT, T], F32R)
        hhi_at = cursor[0]
        hhi = sb("hhi", [P, KT, T], F32R)
        hlo_at = cursor[0]
        hlo = sb("hlo", [P, KT, T], F32R)
        res_at = cursor[0]
        res = sb("res", [P, TH, D], F32)
        small = sb("small", [P, 2 * P + 2], F32)
        ident = small[:, 0:P]
        ones = small[:, P:2 * P]
        sel = small[:, 2 * P:2 * P + 2]
        cols = sb("cols", [P, NCOL], F32)
        mcol = sb("mcol", [P, 5, KT], F32)
        modT = sb("modT", [P, NMOD * KT, 2], F32)
        cst4 = sb("cst4", [P, KT, 4], F32R)
        lev_at = cursor[0]
        sums = sb("sums", [P, 2 * len(LEVELS) + 4, P], F32)
        masks = sb("masks", [P, 2 * len(LEVELS) + 1, P], I8)
        tcol = sb("tcol", [P, 2, 2, T], F32)
        stat = sb("stat", [P, 256], F32)
        mrow_at = cursor[0]
        mrow = sb("mrow", [P, NCH], F32)
        work_at = cursor[0]
        early = at("early", [P, 2 * TH * HD + GRID], F32, lev_at)
        rope = early[:, 0:2 * TH * HD].rearrange("p (s h d) -> p s h d", s=2, h=TH)
        colmask = early[:, 2 * TH * HD:]

        xs = at("xs", [P, TH, D], F32, work_at + 16 * K)
        yrow = at("yrow", [P, TH, D], F32, work_at)
        gbc = at("gbc", [P, D], F32, work_at + 32 * K)
        rrow = at("rrow", [P, TH, NCH], F32, work_at + 40 * K)
        sqrow = at("sqrow", [P, TH, NCH], F32, work_at + 44 * K)
        grow = at("grow", [P, TH, D], F32, work_at + 16 * K)
        prow = at("prow", [P, TH, PLE], F32, work_at + 48 * K)
        vecs = at("vecs", [P, len(VEC_GROUPS), P], F32, work_at + 48 * K)
        cst = at("cst", [P, KT, P], F32R, work_at + 48 * K)
        NA = A_Q + A_KV
        SET = NA // 2
        proj = at("proj", [P, TH, IN1], F32, work_at)
        bm = at("bm", [P, TH, B_H, T], F32, work_at + 36 * K)
        NB = B_H * RPB_R * RPB_C
        bias_rows = nc.dram_tensor("bias_rows", (GRID, NB), F32, kind="Internal").ap()
        qkT = at("qkT", [P, 26, T], F32, hhi_at)
        prob = at("prob", [P, 2, TH, T], F32, hhi_at + 26 * K)
        probT = [at("probT0", [P, TH, T], F32, hhi_at + 30 * K), at("probT1", [P, TH, T], F32, work_at + 52 * K)]
        gqk = at("gqk", [P, NA * HD], F32, xhi_at)
        rota = at("rota", [P, 2, SET * HD], F32, xlo_at)


        pctx = at("pctx", [P, 3, TH, DH], F32, work_at)
        lfc = at("lfc", [P, 2, TH, DH], F32, work_at + 24 * K)
        S0 = at("S0", [P, 2, DH], F32, work_at + 40 * K)
        lb = at("lb", [P, 2, DH], F32, work_at + 48 * K)
        lg = at("lg", [P, 2, 2, DH], F32, hhi_at)
        mask_rows = at("mask_rows", [P, 2 * len(LEVELS) + 1, P], F32, hhi_at)
        dctx = at("dctx", [P, 2, TH, DH], F32, hlo_at)
        rows5 = at("rows5", [P, 5, TH, DH], F32, work_at)
        RV, RF, RQ, RG = 0, 1, 3, 4
        urow = at("urow", [P, TH, DH], F32, res_at)
        cgrow = at("cgrow", [P, TH, DH], F32, res_at + 8 * K)
        uT = at("uT", [P, HH, T], F32, hlo_at + 8 * K)
        yT = at("yT", [P, HH, T], F32, hhi_at + 8 * K)
        ysq = at("ysq", [P, HH, T], F32, hhi_at)
        ysg = at("ysg", [P, HH, T], F32, hlo_at)
        lnm = at("lnm", [P, 2, T], F32, work_at + 48 * K)
        GW = NCH
        lf = at("lf", [P, 2, TH, GW], F32, res_at)
        qT = at("qT", [P, 4, T], F32, res_at + 8 * K)
        kfT = at("kfT", [P, 4, T], F32, res_at + 12 * K)
        kbT = at("kbT", [P, 4, T], F32, work_at + 48 * K)
        kD = at("kD", [P, 2, 2, T], F32, work_at + 52 * K)
        sc = at("sc", [P, 2, 2, TH, P], F32, hhi_at)
        cross = at("cross", [P, 2, 2, 2, P], F32, hhi_at + 4 * K)
        dec = at("dec", [P, 2, 2, T], F32, hlo_at)
        qD = at("qD", [P, 2, 2, T], F32, hlo_at + 4 * K)
        ngain = at("ngain", [P, GW], F32, mrow_at)
        scratch = nc.dram_tensor("x_mid", (P, TH, D), F32, kind="Internal").ap()

        UNITS = []
        n_e = n_s = 0
        for pair in range(HH // 2):
            kinds = [("diag", 0, 0)] + [("level", d, m) for m in LEVELS for d in (0, 1)]
            kinds += [("cross", 0, P), ("cross", 1, P), ("init", 0, 0), ("init", 1, 0)]
            for kind, d, m in kinds:
                has_e, has_s = kind != "diag", kind != "init"
                UNITS.append((kind, d, m, pair, n_e if has_e else None, n_s if has_s else None))
                n_e += has_e
                n_s += has_s
        PER = len(UNITS) // (HH // 2)
        N_E, N_S = [], []
        a = b = 0
        for u in UNITS:
            N_E.append(a)
            N_S.append(b)
            a += u[4] is not None
            b += u[5] is not None
        LV = {m: k for k, m in enumerate(LEVELS)}
        PRE_IN, SUF_EX, SUF_IN, PRE_EX = (2 * len(LEVELS) + k for k in range(4))

        ps = ctx.enter_context(nc.psum_tensor("ps", [P, 8, NCH], F32))
        TB = [4, 5]
        MB = 6

        landed = [sem(f"landed{i}") for i in range(NSLOT)]
        hi_done = sem("hi_done")
        lo_done = sem("lo_done")
        pe_done = sem("pe_done")
        acc_free = sem("acc_free")
        t_done = sem("t_done")
        t_free = sem("t_free")
        t_hi = sem("t_hi")
        x_lo = sem("x_lo")
        dve_step = sem("dve_step")
        small_in = sem("small_in")
        early_in = sem("early_in")
        x_in = sem("x_in")
        vec_in = sem("vec_in")
        vec_turned = sem("vec_turned")
        vec_cols = sem("vec_cols")
        c_exp = sem("c_exp")
        cst_done = sem("cst_done")
        bias_copied = sem("bias_copied")
        bias_in = sem("bias_in")
        bias_done = sem("bias_done")
        gqk_in = sem("gqk_in")
        qk_ss = sem("qk_ss")
        qk_rstd = sem("qk_rstd")
        rope_done = sem("rope_done")
        sc_done = sem("sc_done")
        sc_free = sem("sc_free")
        mx_done = sem("mx_done")
        exp_done = sem("exp_done")
        p_done = sem("p_done")
        pt_done = sem("pt_done")
        pt_copied = sem("pt_copied")
        o_done = sem("o_done")
        o_hi = sem("o_hi")
        o_lo = sem("o_lo")
        sq_done = sem("sq_done")
        m_sel = sem("m_sel")
        m_out = sem("m_out")
        macc_clear = sem("macc_clear")
        p_in = sem("p_in")
        out_done = sem("out_done")

        mcol_done = sem("mcol_done")
        lg_in = sem("lg_in")
        lb_diff = sem("lb_diff")
        lb_exp = sem("lb_exp")
        lb_done = sem("lb_done")
        ctx_in = sem("ctx_in")
        ctx_f = sem("ctx_f")
        ctx_ln = sem("ctx_ln")
        ctx_k = sem("ctx_k")
        cs_done = sem("cs_done")
        cs_exp = sem("cs_exp")
        cs_dec = sem("cs_dec")
        st_done = sem("st_done")
        st_out = sem("st_out")
        spill = sem("spill")
        sums_in = sem("sums_in")
        sig_done = sem("sig_done")
        x_f = sem("x_f")
        u_done = sem("u_done")
        lf_done = sem("lf_done")
        k_done = sem("k_done")
        e_done = sem("e_done")
        d_done = sem("d_done")
        qk_done = sem("qk_done")
        s_done = sem("s_done")
        s_free = sem("s_free")
        o2_done = sem("o2_done")
        oc_done = sem("oc_done")
        on_ms = sem("on_ms")
        on_rstd = sem("on_rstd")
        on_done = sem("on_done")
        ng_in = sem("ng_in")
        conv_done = sem("conv_done")
        clr = sem("clr")
        ln_sum = sem("ln_sum")
        ln_mean = sem("ln_mean")
        ln_cent = sem("ln_cent")
        ln_sq = sem("ln_sq")
        ln_var = sem("ln_var")
        ln_ms = sem("ln_ms")
        ln_pow = sem("ln_pow")
        ln_norm = sem("ln_norm")
        ln_z = sem("ln_z")
        ln_s = sem("ln_s")
        ln_u = sem("ln_u")
        c_hi = sem("c_hi")
        c_lo = sem("c_lo")
        merged = sem("merged")
        reload = sem("reload")
        masks_in = sem("masks_in")
        masks_done = sem("masks_done")
        gb_done = sem("gb_done")
        pool_own = sem("pool_own")
        S = {}
        for k in NORMS:
            for w in ("ss", "ms", "rstd", "xs"):
                S[w, k] = sem(f"{w}_{k}")
        for k in POSTS:
            for w in ("ss", "ms", "rstd", "gain", "scaled", "res"):
                S[w, k] = sem(f"{w}_{k}")

        def pieces(w):
            return w.rearrange("(q k p) n -> p q k n", p=P, k=2)

        w_in, w_o, w_up, w_down = (pieces(I[n][0]) for n in ("w_in", "w_o", "w_up", "w_down"))
        w_gate, w_ple, w_mod = (pieces(I[n][0]) for n in ("w_ple_gate", "w_ple_proj", "w_mod_2"))

        MLP1 = [("U", 0), ("M", 0), ("U", 1), ("M", 1), ("U", 2), ("M", 2), ("U", 3), ("M", 3),
                ("D", 0), ("M", 4), ("D", 1), ("D", 2), ("M", 5), ("D", 3)]
        MLP2 = [("U", c) for c in range(4)] + [("D", c) for c in range(4)]
        NSB = DFF // D
        plan = {}
        pc = [0, 0]

        def stage(name, chunks, per):
            plan[name] = (pc[0], pc[1])
            pc[0] += chunks * per
            pc[1] += chunks

        stage("in", IN1 // NCH, 8)
        stage("o", 4, 8)
        stage("mlp1", len(MLP1) * NSB, 8)
        stage("gate", 4, 8)
        stage("ple", 4, 1)
        stage("ctx", 6, 8)
        stage("x2", 14, 8)
        stage("gc", 4, 8)
        stage("pw", 4, 4)
        stage("gh", 4, 8)
        stage("ho", 4, 4)
        stage("wo2", 4, 8)
        stage("mlp2", len(MLP2) * NSB, 8)
        stage("end", 0, 0)
        n_pieces = pc[0]

        def bank(g):
            return 2 * (g % 2)

        def col(name, n=KT):
            return cols[:, COL[name]:COL[name] + n]

        def rows_of(x):
            return x.rearrange("(h p) n -> p h n", p=P)

        TG = {}
        tc = [0, 0]
        for name, groups, counted in (("norm0", 8, 1), ("attention", 13, 0), ("norm1", 8, 1), ("mlp1", 8 * NSB, 1),
                                      ("norm2", 8, 1), ("ple", 1, 1), ("normc", 8, 1), ("norm3", 8, 1), ("u", 4, 0),
                                      ("qk0", 6, 0), ("qk1", 6, 0), ("o2", 4, 1), ("y", 8, 1), ("norm4", 8, 1),
                                      ("mlp2", 8 * NSB, 1)):
            TG[name] = tuple(tc)
            tc = [tc[0] + groups, tc[1] + groups * counted]

        block = ctx.enter_context(nc.Block())

        @block.sync
        def _(sp):
            sp.dma_start(small[:], I["k_small"]).then_inc(small_in, 16)
            for gi, group in enumerate(VEC_GROUPS):
                r = 0
                for name, rows in group:
                    if name == "conv_dw_w_2a":
                        src = I["conv_dw_w_2"][0].rearrange("a (b p) -> (a b) p", p=P)[0:128]
                    elif name == "conv_dw_w_2b":
                        src = I["conv_dw_w_2"][0].rearrange("a (b p) -> (a b) p", p=P)[128:248]
                    elif name == "c_ctx_2":
                        src = I[name].rearrange("(b p) -> b p", p=P)
                    else:
                        src = I[name][0].rearrange("(b p) -> b p", p=P)
                    sp.dma_start(vecs[r:r + rows, gi, :], src).then_inc(vec_in, 16)
                    r += rows
            sp.dma_start(early[:], I["k_early"]).then_inc(early_in, 16)

            def load(src, p, s):
                if not (isinstance(p, int) and p < NSLOT):
                    sp.wait_ge(lo_done, p - (NSLOT - 1))
                sp.dma_start(raw[:, s % NSLOT], src).then_inc(landed[s % NSLOT], 16)

            def chunk(w, p, col, n=8, s=0):
                for u in range(n):
                    load(w[:, u, :, bass.ds(col, NCH)], p + u, s + u)

            chunk(w_in, 0, 0)
            with sp.Fori(1, IN1 // NCH) as i:
                chunk(w_in, i * 8, i * NCH)
            with sp.Fori(0, 4) as i:
                chunk(w_o, i * 8 + plan["o"][0], i * NCH)

            def mlp(seq, up, down, p0):
                with sp.Fori(0, NSB) as i:
                    for j, (kind, c) in enumerate(seq):
                        p = i * (8 * len(seq)) + (p0 + 8 * j)
                        if kind == "U":
                            chunk(up, p, i * D + c * NCH)
                        elif kind == "M":
                            chunk(w_mod, p, i * (6 * NCH) + c * NCH)
                        else:
                            for u in range(8):
                                src = down[:, bass.ds(i * 8 + u, 1), :, c * NCH:(c + 1) * NCH]
                                load(src.rearrange("p a k n -> p (a k) n"), p + u, u)

            mlp(MLP1, w_up, w_down, plan["mlp1"][0])
            with sp.Fori(0, 4) as i:
                chunk(w_gate, i * 8 + plan["gate"][0], i * NCH)
            for c in range(4):
                chunk(w_ple, plan["ple"][0] + c, c * NCH, n=1, s=c)

            w_x2, w_pw, w_ho, w_wo2 = (pieces(I[n][0]) for n in ("w_in_2", "conv_pw_w_2", "hgrn_out_w_2", "w_out_2"))
            w_up2, w_down2 = pieces(I["mlp_w1_2"][0]), pieces(I["mlp_w2_2"][0])
            c_gate, c_half = 7 * DH, 7 * DH + D

            def loop(w, name, chunks, col, n=8):
                with sp.Fori(0, chunks) as i:
                    chunk(w, i * n + plan[name][0], i * NCH + col, n=n)
            loop(w_x2, "ctx", 6, 0)
            loop(w_x2, "x2", 14, 0)
            loop(w_x2, "gc", 4, c_gate)
            loop(w_pw, "pw", 4, 0, n=4)
            loop(w_x2, "gh", 4, c_half)
            loop(w_ho, "ho", 4, 0, n=4)
            loop(w_wo2, "wo2", 4, 0)
            mlp(MLP2, w_up2, w_down2, plan["mlp2"][0])
            chunk(w_down2, n_pieces, 0, n=3)

        @block.scalar
        def _(act):
            def split(p, s):
                if isinstance(p, int) and p >= n_pieces:
                    return
                act.wait_ge(landed[s % NSLOT], (p - s % NSLOT) * 4 + 16)
                if not (isinstance(p, int) and p < NSLOT):
                    act.wait_ge(pe_done, p - (NSLOT - 1))
                nc.scalar.activation(whi[:, s % NSLOT], raw[:, s % NSLOT], ACT.Copy).then_inc(hi_done, 1)

            def chunk(p, evac=None, n=8, mid=None, s=0):
                for u in range(n):
                    if mid and u == 5:
                        mid()
                    split(p + (3 + u), s + 3 + u)
                if evac:
                    act.wait_ge(pe_done, p + n)
                    evac()

            def evac_to(dst, col, g, func=ACT.Copy, scale=1.0):
                def f():
                    for th in range(TH):
                        ins = nc.scalar.activation(dst[:, th, bass.ds(col, NCH)], ps[:, bank(g) + th], func, scale=scale)
                    ins.then_inc(acc_free, 1)
                return f

            def norm(k, src, wait_src, gain):
                wait_src(act)
                nc.scalar.activation(xs[:, 0], src[:, 0], ACT.Square, accum_out=stat[:, 0:1]).then_inc(S["ss", k], 1)
                act.wait_ge(S["rstd", k], 1)
                nc.scalar.activation(xs[:, 0], src[:, 0], ACT.Copy, scale=stat[:, 8:9]).then_inc(S["xs", k], 1)
                t0, h0 = TG[k]
                for g in range(KT // 2):
                    act.wait_ge(t_done, t0 + g + 1)
                    for j in range(2):
                        ins = nc.scalar.activation(xhi[:, 2 * g + j], ps[:, TB[(t0 + g) % 2], j * T:(j + 1) * T], ACT.Copy,
                                                   scale=gain[:, 2 * g + j:2 * g + j + 1])
                    ins.then_inc(t_hi, 1)

            def postnorm(k, row, wait_row, gain):
                wait_row(act)
                act.dma_start(gbc[:], gain.partition_broadcast(P)).then_inc(S["gain", k], 16)
                nc.scalar.activation(xs[:, 0], row[:, 0], ACT.Square, accum_out=stat[:, 0:1]).then_inc(S["ss", k], 1)

            act.dma_start(res[:], rows_of(I["x"][0])).then_inc(x_in, 16)
            act.dma_start(bias_rows, bass.AP(I["rel_pos_bias"].tensor, 0, [[0, GRID], [1, NB]])).then_inc(bias_copied, 16)
            for u in range(3):
                split(u, u)
            act.wait_ge(vec_cols, 1)
            nc.scalar.activation(stat[:, 64:96], cols[:, COL["c_2"]:COL["c_2"] + 32], ACT.Exp, scale=-1.0).then_inc(c_exp, 1)
            norm("norm0", res, lambda e: e.wait_ge(x_in, 16), col("pre_mix_norm"))
            act.wait_ge(bias_copied, 16)
            for r in range(ROWS):
                for h in range(B_H):
                    src = bass.AP(bias_rows.tensor, h * RPB_R * RPB_C + (7 - r) * RPB_C + 15,
                                  [[NB - 1, GRID], [RPB_C, ROWS], [1, GRID]])
                    dst = bm[GRID * (r % 2):GRID * (r % 2) + GRID, r // 2, h].rearrange("p (a b) -> p a b", a=ROWS)
                    act.dma_start(dst, src).then_inc(bias_in, 16)

            p0, g0 = plan["in"]
            with act.Fori(0, 4) as i:
                for c in range(2):
                    chunk(i * 16 + (8 * c + p0), evac_to(proj, i * (2 * NCH) + c * NCH, g0 + c))
            chunk(p0 + 64, evac_to(proj, 8 * NCH, g0 + 8))

            act.wait_ge(pe_done, plan["o"][0])
            act.dma_start(gqk[:, 0:A_Q * HD].rearrange("p (h d) -> p h d", d=HD),
                          bass.AP(I["q_norm"].tensor, 0, [[0, P], [0, A_Q], [1, HD]])).then_inc(gqk_in, 16)
            act.dma_start(gqk[:, A_Q * HD:].rearrange("p (h d) -> p h d", d=HD),
                          bass.AP(I["k_norm"].tensor, 0, [[0, P], [0, A_KV], [1, HD]])).then_inc(gqk_in, 16)
            t0 = TG["attention"][0]

            def turn_out(g):
                act.wait_ge(t_done, t0 + g + 1)
                nc.scalar.activation(qkT[:, 2 * g:2 * g + 2], ps[:, TB[(t0 + g) % 2]].rearrange("p (a b) -> p a b", a=2), ACT.Copy)\
                    .then_inc(t_free, 1)

            def softmax_exp(i):
                act.wait_ge(mx_done, i + 1)
                for th in range(TH):
                    if i < B_H:
                        src, sc = prob[:, i % 2, th], 1.0
                    else:
                        src, sc = ps[:, i % 2, th * T:(th + 1) * T], SCALE
                        if th == 0 and i >= 2:
                            act.wait_ge(pt_done, i - 1)
                    k = 2 * (i % 2) + th
                    ins = nc.scalar.activation(prob[:, i % 2, th], src, ACT.Exp, bias=stat[:, 32 + k:33 + k], scale=sc,
                                               accum_out=stat[:, 36 + k:37 + k])
                ins.then_inc(exp_done, 1)

            def prob_copy(i):
                act.wait_ge(pt_done, i + 1)
                if i >= 2:
                    act.wait_ge(o_done, i - 1)
                nc.scalar.activation(probT[i % 2][:], ps[:, 2 + i % 2].rearrange("p (a b) -> p a b", a=TH), ACT.Copy)\
                    .then_inc(pt_copied, 1)

            def out_hi(i):
                act.wait_ge(o_done, i + 1)
                nc.scalar.activation(xhi[:, HEAD_KT[i]], ps[:, 6 + i % 2, 0:T], ACT.Copy).then_inc(o_hi, 1)

            for g in range(8):
                turn_out(g)
            for i in range(NHEAD + 2):
                if i == B_H:
                    for g in range(8, 13):
                        turn_out(g)
                if 1 <= i <= NHEAD:
                    prob_copy(i - 1)
                if i < NHEAD:
                    softmax_exp(i)
                if i >= 2:
                    out_hi(i - 2)

            p0, g0 = plan["o"]
            with act.Fori(0, 2) as i:
                for c in range(2):
                    chunk(i * 16 + (8 * c + p0), evac_to(yrow, i * (2 * NCH) + c * NCH, g0 + c))
            postnorm("post0", yrow, lambda e: e.wait_ge(acc_free, plan["mlp1"][1] + 2), I["post_mix_norm"][0])
            norm("norm1", res, lambda e: e.wait_ge(S["res", "post0"], 2), col("pre_mlp_norm"))

            def mlp(i, seq, p0, g0, u0, k):
                t0 = TG[k][0]
                for j, (kind, c) in enumerate(seq):
                    def turned(c=seq[j - 1][1]):
                        for h in range(2):
                            act.wait_ge(t_done, i * 8 + (t0 + 2 * c + h + 1))
                            nc.scalar.activation(hhi[:, 4 * c + 2 * h:4 * c + 2 * h + 2],
                                                 ps[:, TB[(t0 + h) % 2]].rearrange("p (a b) -> p a b", a=2), ACT.Copy)\
                                .then_inc(t_hi, 1)

                    def relu(c=c, j=j):
                        act.wait_ge(sq_done, i * 8 + (2 * (u0 + c) + 2))
                        for th in range(TH):
                            ins = nc.scalar.activation(rrow[:, th], ps[:, bank(g0 + j) + th], ACT.Relu)
                        ins.then_inc(acc_free, 1)
                    chunk(i * (8 * len(seq)) + (p0 + 8 * j), relu if kind == "U" else None,
                          mid=turned if j and seq[j - 1][0] == "U" else None)

            with act.Fori(0, NSB) as i:
                mlp(i, MLP1, *plan["mlp1"], 0, "mlp1")
            postnorm("post1", yrow, lambda e: e.wait_ge(acc_free, plan["gate"][1] + 2), I["post_mlp_norm"][0])
            act.dma_start(prow[:], rows_of(I["p"][0, 0])).then_inc(p_in, 16)
            norm("norm2", res, lambda e: e.wait_ge(S["res", "post1"], 2), col("pre_ple_norm"))
            t0 = TG["ple"][0]
            act.wait_ge(t_done, t0 + 1)
            nc.scalar.activation(hhi[:, 0:2], ps[:, TB[t0 % 2]].rearrange("p (a b) -> p a b", a=2), ACT.Copy).then_inc(t_hi, 1)
            p0, g0 = plan["gate"]
            with act.Fori(0, 2) as i:
                for c in range(2):
                    chunk(i * 16 + (8 * c + p0), evac_to(grow, i * (2 * NCH) + c * NCH, g0 + c, ACT.Sigmoid))
            for c in range(4):
                chunk(plan["ple"][0] + c, n=1, s=c)
            postnorm("post2", yrow, lambda e: e.wait_ge(acc_free, plan["ctx"][1] + 2), I["post_ple_norm"][0])

            act.wait_ge(S["res", "post2"], 2)
            act.dma_start(yrow[:], rows_of(I["ctx_2"][0])).then_inc(ctx_in, 16)
            act.dma_start(lg[:].rearrange("p a b c -> p (a b c)"),
                          I["hgrn_lb_logits_2"].rearrange("a b c -> (a b c)").partition_broadcast(P)).then_inc(lg_in, 16)
            act.dma_start(sums[:].rearrange("p a b -> p (a b)"), I["k_sums"]).then_inc(sums_in, 16)

            def norm_mod(k, src, wait_src):
                wait_src(act)
                nc.scalar.activation(xs[:, 0], src[:, 0], ACT.Square, accum_out=stat[:, 0:1]).then_inc(S["ss", k], 1)
                act.wait_ge(S["rstd", k], 1)
                nc.scalar.activation(xs[:, 0], src[:, 0], ACT.Copy, scale=stat[:, 8:9]).then_inc(S["xs", k], 1)
                t0, h0 = TG[k]
                for g in range(KT // 2):
                    act.wait_ge(t_free, t0 + g + 1)
                    nc.scalar.activation(xhi[:, 2 * g:2 * g + 2], tcol[:, g % 2], ACT.Copy).then_inc(t_hi, 1)

            norm_mod("normc", yrow, lambda e: e.wait_ge(ctx_in, 16))
            p0, g0 = plan["ctx"]

            def lb_exps():
                act.wait_ge(lb_diff, 2)
                nc.scalar.activation(lg[:], lg[:], ACT.Exp).then_inc(lb_exp, 1)
            for c in range(6):
                chunk(p0 + 8 * c, evac_to(pctx[:, c // 2], c % 2 * NCH, g0 + c, *((ACT.Copy, 1.0) if c < 2 else (ACT.Exp, -1.0))),
                      mid=lb_exps if c == 0 else None)
            act.wait_ge(ctx_f, 4)
            for d in range(2):
                nc.scalar.activation(lfc[:, d], pctx[:, 1 + d], ACT.Ln).then_inc(ctx_ln, 1)
            for n in range(4):
                act.wait_ge(cs_done, n + 1)
                nc.scalar.activation(dctx[:, n // 2, :, n % 2 * NCH:(n % 2 + 1) * NCH], ps[:, bank(n):bank(n) + 2], ACT.Exp)\
                    .then_inc(cs_exp, 1)
            for n in range(4):
                act.wait_ge(st_done, n + 1)
                nc.scalar.activation(S0[:, n // 2, n % 2 * NCH:(n % 2 + 1) * NCH], ps[:, 6 + n % 2], ACT.Copy).then_inc(st_out, 1)

            norm_mod("norm3", res, lambda e: e.wait_ge(st_out, 4))
            act.wait_ge(S["xs", "norm3"], 2)
            act.dma_start(scratch, res[:]).then_inc(spill, 16)
            act.wait_ge(lb_done, 1)
            act.dma_start(mask_rows[:].rearrange("p a b -> p (a b)"), I["k_masks"]).then_inc(masks_in, 16)
            p0, g0 = plan["x2"]

            def sig_only(dst, col, g):
                def f():
                    for th in range(TH):
                        ins = nc.scalar.activation(dst[:, th, col:col + NCH], ps[:, bank(g) + th], ACT.Sigmoid)
                    ins.then_inc(sig_done, 1)
                return f
            for c in range(14):
                col_, g = c % 2 * NCH, g0 + c
                if c < 2:
                    f = evac_to(rows5[:, RV], col_, g)
                elif c < 6:
                    f = evac_to(rows5[:, RF + (c - 2) // 2], col_, g, ACT.Exp, -1.0)
                elif c < 10:
                    f = sig_only(rows5[:, RQ + (c - 6) // 2], col_, g)
                elif c < 12:
                    if c == 10:
                        act.wait_ge(spill, 16)
                    f = evac_to(urow, col_, g)
                else:
                    f = evac_to(cgrow, col_, g, ACT.Sigmoid)
                chunk(p0 + 8 * c, f)
            t0 = TG["u"][0]
            for g in range(4):
                act.wait_ge(t_done, t0 + g + 1)
                nc.scalar.activation(uT[:, 2 * g:2 * g + 2], ps[:, TB[(t0 + g) % 2]].rearrange("p (a b) -> p a b", a=2), ACT.Copy)\
                    .then_inc(t_free, 1)

            def exp_unit(n):
                kind, d, m, pair, ne, ns = UNITS[n]
                if ne is None:
                    return
                act.wait_ge(e_done, ne + 1)
                if n >= 2:
                    act.wait_ge(qk_done, n - 1)
                nc.scalar.activation(dec[:, n % 2], ps[:, ne % 2].rearrange("p (a b) -> p a b", a=2), ACT.Exp).then_inc(d_done, 1)

            for hg in range(2):
                cs = slice(hg * GW, (hg + 1) * GW)
                if hg == 0:
                    act.wait_ge(x_f, 4)
                    act.wait_ge(t_done, t0 + 4)
                else:
                    act.wait_ge(e_done, N_E[2 * PER])
                for d in range(2):
                    nc.scalar.activation(lf[:, d], rows5[:, RF + d, :, cs], ACT.Ln).then_inc(lf_done, 1)
                if hg:
                    act.wait_ge(on_done, 2)
                act.dma_start(ngain[:], I["hgrn_norm_g_2"][0, cs].partition_broadcast(P)).then_inc(ng_in, 16)
                t0 = TG["qk%d" % hg][0]
                if hg:
                    act.wait_ge(qk_done, 2 * PER)
                    act.wait_ge(s_done, N_S[2 * PER])
                for g in range(6):
                    act.wait_ge(t_done, t0 + g + 1)
                    dst = (qT, kfT, kbT)[g // 2]
                    nc.scalar.activation(dst[:, g % 2 * 2:g % 2 * 2 + 2], ps[:, TB[(t0 + g) % 2]].rearrange("p (a b) -> p a b", a=2),
                                         ACT.Copy).then_inc(t_free, 1)
                for pair in (2 * hg, 2 * hg + 1):
                    for n in range(pair * PER, (pair + 1) * PER):
                        exp_unit(n)
                    act.wait_ge(o2_done, pair + 1)
                    nc.scalar.activation(rows5[:, RQ, :, pair * 2 * HD:(pair + 1) * 2 * HD],
                                         ps[:, 6 + pair % 2].rearrange("p (a b) -> p a b", a=TH), ACT.Copy).then_inc(oc_done, 1)

            act.wait_ge(ln_sum, 1)
            nc.scalar.activation(lnm[:, 0], ps[:, 2, 0:T], ACT.Copy, scale=1.0 / DH).then_inc(ln_mean, 1)
            act.wait_ge(ln_cent, 1)
            nc.scalar.activation(ysq[:], yT[:], ACT.Square).then_inc(ln_sq, 1)
            act.wait_ge(ln_norm, 1)
            for c in range(HH):
                g1, b1 = (cols[:, COL[x] + c:COL[x] + c + 1] for x in ("conv_ln_g_2", "conv_ln_b_2"))
                nc.scalar.activation(ysg[:, c], yT[:, c], ACT.Sigmoid, bias=b1, scale=g1).then_inc(ln_s, 1)
            for c in range(HH):
                g1, b1 = (cols[:, COL[x] + c:COL[x] + c + 1] for x in ("conv_ln_g_2", "conv_ln_b_2"))
                nc.scalar.activation(ysq[:, c], yT[:, c], ACT.Identity, bias=b1, scale=g1).then_inc(ln_z, 1)
            act.wait_ge(ln_u, 1)
            nc.scalar.activation(hhi[:, HH:KT], ysq[:], ACT.Copy).then_inc(c_hi, 1)
            act.wait_ge(c_lo, 1)
            t0, h0 = TG["o2"]
            for g in range(4):
                act.wait_ge(t_done, t0 + g + 1)
                nc.scalar.activation(hhi[:, 2 * g:2 * g + 2], ps[:, TB[(t0 + g) % 2]].rearrange("p (a b) -> p a b", a=2), ACT.Copy)\
                    .then_inc(t_hi, 1)

            def pairs_of(name, dst, n=8, func=None, last=False):
                p0, g0 = plan[name]
                with act.Fori(0, 2) as i:
                    for c in range(2):
                        chunk(i * (2 * n) + (n * c + p0), func and evac_to(dst, i * (2 * NCH) + c * NCH, g0 + c, func), n=n)
            pairs_of("gc", yrow, func=ACT.Sigmoid)
            pairs_of("pw", None, n=4)
            pairs_of("gh", grow, func=ACT.Sigmoid)
            pairs_of("ho", None, n=4)
            act.wait_ge(on_done, 4)
            act.dma_start(res[:], scratch).then_inc(reload, 16)
            t0, h0 = TG["y"]
            for g in range(8):
                act.wait_ge(t_done, t0 + g + 1)
                nc.scalar.activation(xhi[:, 2 * g:2 * g + 2], ps[:, TB[(t0 + g) % 2]].rearrange("p (a b) -> p a b", a=2), ACT.Copy)\
                    .then_inc(t_hi, 1)
            pairs_of("wo2", yrow, func=ACT.Copy)

            def postnorm_gated(k, n, row, wait_row):
                wait_row(act)
                nc.scalar.activation(xs[:, 0], row[:, 0], ACT.Square, accum_out=stat[:, 0:1]).then_inc(S["ss", k], 1)
                act.wait_ge(gb_done, n + 1)
                nc.scalar.activation(gbc[:], ps[:, 0:4].rearrange("p a b -> p (a b)"), ACT.Copy).then_inc(S["gain", k], 16)

            act.wait_ge(reload, 16)
            postnorm_gated("post3", 0, yrow, lambda e: e.wait_ge(acc_free, plan["mlp2"][1] + 2))
            norm_mod("norm4", res, lambda e: e.wait_ge(S["res", "post3"], 2))
            with act.Fori(0, NSB) as i:
                mlp(i, MLP2, *plan["mlp2"], 16, "mlp2")
            postnorm_gated("post4", 1, yrow, lambda e: e.wait_ge(acc_free, plan["end"][1] + 2))
            for th in range(TH):
                act.wait_ge(S["res", "post4"], 2)
                act.dma_start(rows_of(out[0])[:, th], res[:, th]).then_inc(out_done, 16)
            act.wait_ge(out_done, 32)

        @block.tensor
        def _(pe):
            def turn(t, parts):
                if t >= 2:
                    pe.wait_ge(t_free, t - 1)
                for c, src in parts:
                    ins = nc.tensor.transpose(ps[:, TB[t % 2], c:c + P], src, ident)
                ins.then_inc(t_done, 1)

            def norm(k):
                pe.wait_ge(S["xs", k], 2)
                for g in range(KT // 2):
                    turn(TG[k][0] + g, [(j * T + th * P, xs[:, th, (2 * g + j) * P:(2 * g + j + 1) * P])
                                        for j in range(2) for th in range(TH)])

            def chunk(p, g, hi, lo, n=8, s=0, par=None, inserts=None, before=None):
                par = g if par is None else par
                pe.wait_ge(acc_free, g + 1)
                for u in range(n):
                    if inserts and u in inserts:
                        inserts[u]()
                    pe.wait_ge(lo_done, p + (u + 1))
                    for th in range(TH):
                        for k in range(2):
                            kt = 2 * u + k
                            for m, (a, b) in enumerate(((hi, whi), (hi, wlo), (lo, whi))):
                                ins = nc.tensor.matmul(ps[:, bank(par) + th], a[:, kt, th * P:(th + 1) * P],
                                                       b[:, (s + u) % NSLOT, k], start=(kt == 0 and m == 0),
                                                       stop=(kt == 2 * n - 1 and m == 2))
                    ins.then_inc(pe_done, 1)

            def mod_chunk(p, g, par, inserts):
                pe.wait_ge(acc_free, g + 1)
                for u in range(8):
                    if inserts and u in inserts:
                        inserts[u]()
                    pe.wait_ge(lo_done, p + (u + 1))
                    for k in range(2):
                        kt = 2 * u + k
                        for m, b in enumerate((whi, wlo)):
                            ins = nc.tensor.matmul(ps[:, bank(par)], cst[:, kt], b[:, u % NSLOT, k],
                                                   start=(kt == 0 and m == 0), stop=(kt == KT - 1 and m == 1))
                    ins.then_inc(pe_done, 1)

            pe.wait_ge(small_in, 16)
            pe.wait_ge(vec_in, 16 * sum(len(g) for g in VEC_GROUPS))
            c = 0
            for gi, group in enumerate(VEC_GROUPS):
                rows = sum(n for _, n in group)
                ins = nc.tensor.transpose(ps[:, MB, c:c + rows], vecs[0:rows, gi, :], ident[0:rows, 0:rows])
                c += rows
            ins.then_inc(vec_turned, 1)

            norm("norm0")
            pe.wait_ge(t_free, 8)
            p0, g0 = plan["in"]
            with pe.Fori(0, 4) as i:
                for c in range(2):
                    chunk(i * 16 + (8 * c + p0), i * 2 + (g0 + c), xhi, xlo, par=g0 + c)
            chunk(p0 + 64, g0 + 8, xhi, xlo)

            pe.wait_ge(acc_free, plan["o"][1] + 2)
            o_q, o_k = (A_Q + 2 * A_KV) * HD, (A_Q + 2 * A_KV + B_H) * HD
            o_v = o_k + B_H * HD
            t0 = TG["attention"][0]

            def turn_heads(g, a, b):
                turn(t0 + g, [(j * T + th * P, proj[:, th, c:c + HD]) for j, c in enumerate((a, b)) for th in range(TH)])

            def scores(i):
                if i >= 2:
                    pe.wait_ge(sc_free if i - 2 < B_H else exp_done, i - 1)
                q, k = (2 * i, 2 * i + 1) if i < B_H else (16 + i - B_H, 16 + A_Q + (i - B_H) // (A_Q // A_KV))
                for th in range(TH):
                    ins = nc.tensor.matmul(ps[:, i % 2, th * T:(th + 1) * T], qkT[:, q, th * P:(th + 1) * P], qkT[:, k],
                                           start=True, stop=True)
                ins.then_inc(sc_done, 1)

            def prob_turn(i):
                pe.wait_ge(p_done, i + 1)
                if i >= 2:
                    pe.wait_ge(pt_copied, i - 1)
                for kt in range(TH):
                    for th in range(TH):
                        ins = nc.tensor.transpose(ps[:, 2 + i % 2, kt * T + th * P:kt * T + (th + 1) * P],
                                                  prob[:, i % 2, th, kt * P:(kt + 1) * P], ident)
                ins.then_inc(pt_done, 1)

            def values(i):
                pe.wait_ge(pt_copied, i + 1)
                if i >= 2:
                    pe.wait_ge(o_lo, i - 1)
                c = o_v + i * HD if i < B_H else (A_Q + A_KV + (i - B_H) // (A_Q // A_KV)) * HD
                for kt in range(TH):
                    ins = nc.tensor.matmul(ps[:, 6 + i % 2, 0:T], proj[:, kt, c:c + HD], probT[i % 2][:, kt],
                                           start=kt == 0, stop=kt == TH - 1)
                ins.then_inc(o_done, 1)

            for h in range(B_H):
                turn_heads(h, o_q + h * HD, o_k + h * HD)
            pe.wait_ge(t_free, t0 + 8)
            for i in range(NHEAD + 2):
                if i == B_H:
                    pe.wait_ge(rope_done, 4)
                    for g in range(NA // 2):
                        turn_heads(8 + g, 2 * g * HD, (2 * g + 1) * HD)
                    pe.wait_ge(t_free, t0 + 13)
                if i < NHEAD:
                    scores(i)
                if 1 <= i <= NHEAD:
                    prob_turn(i - 1)
                if i >= 2:
                    values(i - 2)
            pe.wait_ge(o_lo, NHEAD)

            p0, g0 = plan["o"]
            with pe.Fori(0, 2) as i:
                for c in range(2):
                    chunk(i * 16 + (8 * c + p0), i * 2 + (g0 + c), xhi, xlo, par=g0 + c)
            norm("norm1")
            pe.wait_ge(t_free, TG["mlp1"][0])
            pe.wait_ge(cst_done, 1)

            def mlp(i, seq, p0, g0, u0, k):
                t0 = TG[k][0]
                nm = sum(kind == "M" for kind, _ in seq)
                for j, (kind, c) in enumerate(seq):
                    def turn_hidden(c=seq[j - 1][1]):
                        pe.wait_ge(sq_done, i * 8 + (2 * (u0 + c) + 4))
                        for h in range(2):
                            pe.wait_ge(t_free, i * 8 + (t0 + 2 * c + h - 1))
                            for a in range(2):
                                for th in range(TH):
                                    f = (2 * h + a) * P
                                    ins = nc.tensor.transpose(ps[:, TB[(t0 + h) % 2], a * T + th * P:a * T + (th + 1) * P],
                                                              sqrow[:, th, f:f + P], ident)
                            ins.then_inc(t_done, 1)

                    def select(m=seq[j - 1][1], j=j):
                        pe.wait_ge(acc_free, i * len(seq) + (g0 + j + 2))
                        pe.wait_ge(m_out, i * nm + (m + 1))
                        for b in range(4):
                            ins = nc.tensor.matmul(ps[:, MB, 2 * b:2 * b + 2], mrow[0:4, b * P:(b + 1) * P], sel[0:4, :],
                                                   start=True, stop=True)
                        ins.then_inc(m_sel, 1)

                    def hidden_ready(c=c):
                        pe.wait_ge(t_free, i * 8 + (t0 + 8))
                    prev = seq[j - 1][0] if j else None
                    inserts = {3: turn_hidden} if prev == "U" else {3: select} if prev == "M" else {}
                    if kind == "D" and c == 0:
                        inserts[0 if prev != "U" else 6] = hidden_ready
                    p = i * (8 * len(seq)) + (p0 + 8 * j)
                    g = i * len(seq) + (g0 + j)
                    if kind == "M":
                        mod_chunk(p, g, g0 + j, inserts)
                    else:
                        st = (xhi, xlo) if kind == "U" else (hhi, hlo)
                        chunk(p, g, *st, par=g0 + j, inserts=inserts)

            with pe.Fori(0, NSB) as i:
                mlp(i, MLP1, *plan["mlp1"], 0, "mlp1")
            norm("norm2")
            pe.wait_ge(p_in, 16)
            turn(TG["ple"][0], [(j * T + th * P, prow[:, th, j * P:(j + 1) * P]) for j in range(2) for th in range(TH)])
            pe.wait_ge(t_free, TG["ple"][0] + 1)
            p0, g0 = plan["gate"]
            with pe.Fori(0, 2) as i:
                for c in range(2):
                    chunk(i * 16 + (8 * c + p0), i * 2 + (g0 + c), xhi, xlo, par=g0 + c)
            p0, g0 = plan["ple"]
            for c in range(4):
                chunk(p0 + c, g0 + c, hhi, hlo, n=1, s=c)

            norm("normc")
            pe.wait_ge(x_lo, 8)

            def straight(name, chunks, n=8, st=(xhi, xlo)):
                p0, g0 = plan[name]
                for c in range(chunks):
                    chunk(p0 + n * c, g0 + c, *st, n=n)

            def looped(name, pairs, n=8, st=(xhi, xlo)):
                p0, g0 = plan[name]
                with pe.Fori(0, pairs) as i:
                    for c in range(2):
                        chunk(i * (2 * n) + (n * c + p0), i * 2 + (g0 + c), *st, n=n, par=g0 + c)
            looped("ctx", 3)
            pe.wait_ge(acc_free, plan["x2"][1] + 2)
            pe.wait_ge(sums_in, 16)
            for n in range(4):
                d, cs = n // 2, slice(n % 2 * NCH, (n % 2 + 1) * NCH)
                pe.wait_ge(ctx_ln, d + 1)
                if n >= 2:
                    pe.wait_ge(cs_exp, n - 1)
                own = sums[:, SUF_EX if d == 0 else PRE_EX]
                far = 0 if d == 0 else 1
                for th in range(TH):
                    ins = nc.tensor.matmul(ps[:, bank(n) + th], own, lfc[:, d, th, cs], start=True, stop=th != far)
                    if th == far:
                        ins = nc.tensor.matmul(ps[:, bank(n) + th], ones, lfc[:, d, 1 - th, cs], start=False, stop=True)
                ins.then_inc(cs_done, 1)
            for n in range(4):
                d = n // 2
                pe.wait_ge(cs_dec, n + 1)
                if n >= 2:
                    pe.wait_ge(st_out, n - 1)
                for h in range(4):
                    c = (n % 2 * 4 + h) * HD
                    for th in range(TH):
                        ins = nc.tensor.matmul(ps[:, 6 + n % 2, h * HD:(h + 1) * HD], dctx[:, d, th, c:c + HD], pctx[:, 0, th, c:c + HD],
                                               start=th == 0, stop=th == TH - 1)
                ins.then_inc(st_done, 1)
            norm("norm3")
            pe.wait_ge(x_lo, 16)
            looped("x2", 7)

            def turn_pair(t, src, kt):
                turn(t, [(j * T + th * P, src[:, th, (kt + j) * P:(kt + j + 1) * P]) for j in range(2) for th in range(TH)])
            pe.wait_ge(u_done, 2)
            for g in range(4):
                turn_pair(TG["u"][0] + g, urow, 2 * g)

            def sums_unit(n):
                kind, d, m, pair, ne, ns = UNITS[n]
                if ne is None:
                    return
                if ne >= 2:
                    pe.wait_ge(d_done, ne - 1)
                for hh in range(2):
                    c = (pair % 2 * 2 + hh) * HD
                    for th in range(TH):
                        o = ps[:, ne % 2, hh * T + th * P:hh * T + (th + 1) * P]
                        w = lf[:, d, th, c:c + HD]
                        if kind == "level":
                            mat, more = LV[m] + d * len(LEVELS), False
                        elif kind == "cross":
                            mat = (SUF_EX, PRE_IN)[th] if d == 0 else (SUF_IN, PRE_EX)[th]
                            more = False
                        else:
                            mat, more = (PRE_IN, SUF_IN)[d], th != d
                        ins = nc.tensor.matmul(o, w, sums[:, mat], start=True, stop=not more)
                        if more:
                            ins = nc.tensor.matmul(o, lf[:, d, 1 - th, c:c + HD], ones, start=False, stop=True)
                ins.then_inc(e_done, 1)

            def score_unit(n):
                kind, d, m, pair, ne, ns = UNITS[n]
                if ns is None:
                    return
                pe.wait_ge(qk_done, n + 1)
                if ns >= 2:
                    pe.wait_ge(s_free, ns - 1)
                for hh in range(2):
                    if kind == "cross":
                        s, t = (0, 1) if d == 0 else (1, 0)
                        ins = nc.tensor.matmul(ps[:, 2 + ns % 2, hh * P:(hh + 1) * P], kD[:, n % 2, hh, s * P:(s + 1) * P],
                                               qD[:, n % 2, hh, t * P:(t + 1) * P], start=True, stop=True)
                        continue
                    for th in range(TH):
                        q = qT[:, pair % 2 * 2 + hh] if kind == "diag" else qD[:, n % 2, hh]
                        ins = nc.tensor.matmul(ps[:, 2 + ns % 2, (hh * 2 + th) * P:(hh * 2 + th + 1) * P],
                                               kD[:, n % 2, hh, th * P:(th + 1) * P], q[:, th * P:(th + 1) * P],
                                               start=True, stop=True)
                ins.then_inc(s_done, 1)

            def out_pair(pair):
                n = (pair + 1) * PER
                pe.wait_ge(qk_done, n)
                pe.wait_ge(s_free, N_S[n] if n < len(UNITS) else n_s)
                if pair >= 2:
                    pe.wait_ge(oc_done, pair - 1)
                for th in range(TH):
                    for hh in range(2):
                        c = (2 * pair + hh) * HD
                        o = ps[:, 6 + pair % 2, (th * 2 + hh) * HD:(th * 2 + hh + 1) * HD]
                        parts = [(qD[:, (n - 2) % 2, hh, th * P:(th + 1) * P], S0[:, 0, c:c + HD]),
                                 (qD[:, (n - 1) % 2, hh, th * P:(th + 1) * P], S0[:, 1, c:c + HD]),
                                 (sc[:, pair % 2, hh, th], rows5[:, RV, th, c:c + HD]),
                                 (cross[:, pair % 2, hh, 1 - th], rows5[:, RV, 1 - th, c:c + HD])]
                        for k, (w, v) in enumerate(parts):
                            ins = nc.tensor.matmul(o, w, v, start=k == 0, stop=k == 3)
                ins.then_inc(o2_done, 1)

            for hg in range(2):
                t0 = TG["qk%d" % hg][0]
                for g in range(6):
                    if g >= 2:
                        pe.wait_ge(k_done, 2 * hg + g // 2)
                    row = (RQ, RF, RF + 1)[g // 2]
                    turn_pair(t0 + g, rows5[:, row], hg * 4 + g % 2 * 2)
                pe.wait_ge(lf_done, 2 * hg + 2)
                pe.wait_ge(t_free, t0 + 6)
                first, last = 2 * hg * PER, 2 * (hg + 1) * PER
                sums_unit(first)
                for n in range(first, last):
                    if n + 1 < last:
                        sums_unit(n + 1)
                    score_unit(n)
                    if (n + 1) % PER == 0:
                        out_pair(n // PER)

            pe.wait_ge(conv_done, N_CONV)
            for c in range(HH):
                ins = nc.tensor.matmul(ps[:, 2, 0:T], ones, yT[:, c], start=c == 0, stop=c == HH - 1)
            ins.then_inc(ln_sum, 1)
            pe.wait_ge(ln_sq, 1)
            for c in range(HH):
                ins = nc.tensor.matmul(ps[:, 3, 0:T], ones, ysq[:, c], start=c == 0, stop=c == HH - 1)
            ins.then_inc(ln_var, 1)
            pe.wait_ge(on_done, 4)
            for g in range(4):
                turn_pair(TG["o2"][0] + g, rows5[:, RQ], 2 * g)
            pe.wait_ge(c_lo, 1)
            looped("gc", 2)
            looped("pw", 2, n=4, st=(hhi[:, HH:KT], hlo[:, HH:KT]))
            looped("gh", 2)
            pe.wait_ge(t_free, TG["o2"][0] + 4)
            looped("ho", 2, n=4, st=(hhi, hlo))
            pe.wait_ge(merged, 4)
            for g in range(8):
                turn_pair(TG["y"][0] + g, yrow, 2 * g)
            pe.wait_ge(t_free, TG["y"][0] + 8)
            looped("wo2", 2)

            def gate_rows(k, g_end):
                pe.wait_ge(mcol_done, 5)
                pe.wait_ge(acc_free, g_end + 2)
                for kt in range(KT):
                    ins = nc.tensor.matmul(ps[:, kt // 4, kt % 4 * P:(kt % 4 + 1) * P], mcol[:, k, kt:kt + 1].to_broadcast([P, P]),
                                           ident, start=True, stop=True)
                ins.then_inc(gb_done, 1)
            gate_rows(3, plan["mlp2"][1])
            norm("norm4")
            pe.wait_ge(x_lo, 24)
            with pe.Fori(0, NSB) as i:
                mlp(i, MLP2, *plan["mlp2"], 16, "mlp2")
            gate_rows(4, plan["end"][1])

        @block.vector
        def _(dve):
            steps = [0]

            def step(ins):
                steps[0] += 1
                ins.then_inc(dve_step, 1)
                dve.wait_ge(dve_step, steps[0])

            def split(p, s):
                if isinstance(p, int) and p >= n_pieces:
                    return
                dve.wait_ge(hi_done, p + 1)
                nc.vector.tensor_tensor(wlo[:, s % NSLOT], raw[:, s % NSLOT], whi[:, s % NSLOT].bitcast(F32), ALU.subtract)\
                    .then_inc(lo_done, 1)

            def chunk(p, evac=None, n=8, mid=None, s=0):
                for u in range(n):
                    if mid and u == 5:
                        mid()
                    split(p + (3 + u), s + 3 + u)
                if evac:
                    dve.wait_ge(pe_done, p + n)
                    evac()

            def mean_square(k, src, wait_src):
                wait_src(dve)
                nc.vector.tensor_tensor_reduce(out=xs[:, 1], in0=src[:, 1], in1=src[:, 1], scale=1.0, scalar=0.0,
                                               op0=ALU.mult, op1=ALU.add, accum_out=stat[:, 1:2]).then_inc(S["ss", k], 1)
                dve.wait_ge(S["ss", k], 2)
                nc.vector.tensor_scalar(stat[:, 4:6], stat[:, 0:2], 1.0 / D, EPS, ALU.mult, ALU.add).then_inc(S["ms", k], 1)

            def norm(k, src, wait_src, gain):
                mean_square(k, src, wait_src)
                dve.wait_ge(S["rstd", k], 1)
                nc.vector.tensor_scalar(xs[:, 1], src[:, 1], stat[:, 9:10], None, ALU.mult).then_inc(S["xs", k], 1)
                t0, h0 = TG[k]
                for g in range(KT // 2):
                    dve.wait_ge(t_hi, h0 + g + 1)
                    for j in range(2):
                        kt = 2 * g + j
                        ins = nc.vector.scalar_tensor_tensor(out=xlo[:, kt], in0=ps[:, TB[(t0 + g) % 2], j * T:(j + 1) * T],
                                                             scalar=gain[:, kt:kt + 1], in1=xhi[:, kt].bitcast(F32),
                                                             op0=ALU.mult, op1=ALU.subtract)
                    ins.then_inc(t_free, 1)

            def postnorm(k, row, wait_row):
                mean_square(k, row, wait_row)
                dve.wait_ge(S["rstd", k], 1)
                dve.wait_ge(S["gain", k], 16)
                for th in range(TH):
                    nc.vector.scalar_tensor_tensor(out=xs[:, th], in0=row[:, th], scalar=stat[:, 8 + th:9 + th], in1=gbc[:],
                                                   op0=ALU.mult, op1=ALU.mult).then_inc(S["scaled", k], 1)
                dve.wait_ge(S["scaled", k], 2)
                nc.vector.tensor_tensor(res[:, 1], res[:, 1], xs[:, 1], ALU.add).then_inc(S["res", k], 1)

            for u in range(3):
                split(u, u)
            dve.wait_ge(vec_turned, 1)
            nc.vector.tensor_copy(cols[:], ps[:, MB]).then_inc(vec_cols, 1)
            norm("norm0", res, lambda e: e.wait_ge(x_in, 16), col("pre_mix_norm"))
            p0, g0 = plan["in"]
            with dve.Fori(0, 4) as i:
                for c in range(2):
                    chunk(i * 16 + (8 * c + p0))
            chunk(p0 + 64)

            dve.wait_ge(acc_free, plan["o"][1] + 2)
            dve.wait_ge(gqk_in, 32)
            dve.wait_ge(early_in, 16)
            for n in range(4):
                th, w = n // 2, (n % 2) * SET * HD
                pj = proj[:, th, w:w + SET * HD]
                ra, rb = rota[:, 0], rota[:, 1]
                step(nc.vector.tensor_tensor(ra, pj, pj, ALU.mult))
                step(nc.vector.tensor_reduce(stat[:, 16:16 + SET], ra.rearrange("p (h d) -> p h d", d=HD), AX_X, ALU.add))
                nc.vector.tensor_scalar(stat[:, 16:16 + SET], stat[:, 16:16 + SET], 1.0 / HD, EPS, ALU.mult, ALU.add)\
                    .then_inc(qk_ss, 1)
                dve.wait_ge(qk_rstd, n + 1)
                h3 = pj.rearrange("p (h d) -> p h d", d=HD)
                step(nc.vector.tensor_tensor(h3, h3, stat[:, 24:24 + SET].unsqueeze(2).to_broadcast([P, SET, HD]), ALU.mult))
                step(nc.vector.tensor_tensor(pj, pj, gqk[:, w:w + SET * HD], ALU.mult))
                nc.vector.tensor_tensor(ra.rearrange("p (h d) -> p h d", d=HD), h3,
                                        rope[:, 0, th].unsqueeze(1).to_broadcast([P, SET, HD]), ALU.mult)
                h4 = pj.rearrange("p (h b s c) -> p h b s c", b=2, s=2, c=HD // 4)
                r4 = rb.rearrange("p (h b s c) -> p h b s c", b=2, s=2, c=HD // 4)
                s4 = rope[:, 1, th].rearrange("p (b s c) -> p b s c", b=2, s=2)
                for s in range(2):
                    ins = nc.vector.tensor_tensor(r4[:, :, :, s], h4[:, :, :, 1 - s],
                                                  s4[:, :, s].unsqueeze(1).to_broadcast([P, SET, 2, HD // 4]), ALU.mult)
                step(ins)
                nc.vector.tensor_tensor(pj, ra, rb, ALU.add).then_inc(rope_done, 1)
                dve.wait_ge(rope_done, n + 1)

            def score_max(i):
                dve.wait_ge(sc_done, i + 1)
                k = 32 + 2 * (i % 2)
                if i < B_H:
                    if i >= 2:
                        dve.wait_ge(pt_done, i - 1)
                    ins = nc.vector.scalar_tensor_tensor(out=prob[:, i % 2], in0=ps[:, i % 2].rearrange("p (a b) -> p a b", a=TH),
                                                         scalar=SCALE, in1=bm[:, :, i], op0=ALU.mult, op1=ALU.add)
                    ins.then_inc(sc_free, 1)
                    dve.wait_ge(sc_free, i + 1)
                    step(nc.vector.tensor_reduce(stat[:, k:k + 2], prob[:, i % 2], AX_X, ALU.max))
                    s = -1.0
                else:
                    step(nc.vector.tensor_reduce(stat[:, k:k + 2], ps[:, i % 2].rearrange("p (a b) -> p a b", a=TH), AX_X, ALU.max))
                    s = -SCALE
                nc.vector.tensor_scalar(stat[:, k:k + 2], stat[:, k:k + 2], s, None, ALU.mult).then_inc(mx_done, 1)

            def normalise(i):
                dve.wait_ge(exp_done, i + 1)
                k = 36 + 2 * (i % 2)
                step(nc.vector.reciprocal(stat[:, k:k + 2], stat[:, k:k + 2]))
                for th in range(TH):
                    ins = nc.vector.tensor_scalar(prob[:, i % 2, th], prob[:, i % 2, th], stat[:, k + th:k + th + 1], None, ALU.mult)
                ins.then_inc(p_done, 1)

            def out_lo(i):
                dve.wait_ge(o_hi, i + 1)
                nc.vector.tensor_tensor(xlo[:, HEAD_KT[i]], ps[:, 6 + i % 2, 0:T], xhi[:, HEAD_KT[i]].bitcast(F32), ALU.subtract)\
                    .then_inc(o_lo, 1)

            dve.wait_ge(bias_done, 1)
            for i in range(NHEAD + 3):
                if 1 <= i <= NHEAD:
                    normalise(i - 1)
                if i < NHEAD:
                    score_max(i)
                if i >= 3:
                    out_lo(i - 3)

            p0, g0 = plan["o"]
            with dve.Fori(0, 2) as i:
                for c in range(2):
                    chunk(i * 16 + (8 * c + p0))
            dve.wait_ge(c_exp, 1)
            cc, ce = cols[:, COL["c_2"]:COL["c_2"] + 32], stat[:, 64:96]
            step(nc.vector.tensor_scalar(ce, ce, 1.0, None, ALU.add))
            step(nc.vector.reciprocal(ce, ce))
            step(nc.vector.tensor_tensor(ce, ce, cc, ALU.mult))
            ce2 = ce.rearrange("p (j k) -> p k j", j=2)
            step(nc.vector.tensor_copy(cst4[:, :, 0:2], ce2))
            step(nc.vector.tensor_tensor(cst4[:, :, 2:4], ce2, cst4[:, :, 0:2].bitcast(F32), ALU.subtract))
            nc.vector.tensor_copy(cst[:].rearrange("p k (r c) -> p k r c", c=4),
                                  cst4[:].bitcast(F32).unsqueeze(2).to_broadcast([P, KT, P // 4, 4])).then_inc(cst_done, 1)

            postnorm("post0", yrow, lambda e: e.wait_ge(acc_free, plan["mlp1"][1] + 2))
            norm("norm1", res, lambda e: e.wait_ge(S["res", "post0"], 2), col("pre_mlp_norm"))
            dve.wait_ge(macc_clear, 1)

            def mlp(i, seq, p0, g0, k):
                t0, h0 = TG[k]
                nm = sum(kind == "M" for kind, _ in seq)
                for j, (kind, c) in enumerate(seq):
                    def turned(c=seq[j - 1][1]):
                        for h in range(2):
                            dve.wait_ge(t_hi, i * 8 + (h0 + 2 * c + h + 1))
                            kt = 4 * c + 2 * h
                            nc.vector.tensor_tensor(hlo[:, kt:kt + 2], ps[:, TB[(t0 + h) % 2]].rearrange("p (a b) -> p a b", a=2),
                                                    hhi[:, kt:kt + 2].bitcast(F32), ALU.subtract).then_inc(t_free, 1)

                    def mod_cols(m=seq[j - 1][1]):
                        dve.wait_ge(m_sel, i * nm + (m + 2))
                        nc.vector.tensor_copy(modT[:, bass.ds(i * (4 * nm) + 4 * m, 4), :],
                                              ps[:, MB, 0:8].rearrange("p (a b) -> p a b", a=4)).then_inc(m_out, 1)

                    def mod_row(m=c, j=j):
                        dve.wait_ge(m_sel, i * nm + (m + 1))
                        nc.vector.tensor_copy(mrow[0:4, :], ps[0:4, bank(g0 + j)]).then_inc(acc_free, 1)

                    def down(c=c, j=j):
                        for th in range(TH):
                            y = yrow[:, th, c * NCH:(c + 1) * NCH]
                            ins = nc.vector.tensor_tensor(y, ps[:, bank(g0 + j) + th], y, ALU.add)
                        ins.then_inc(acc_free, 1)
                    prev = seq[j - 1][0] if j else None
                    chunk(i * (8 * len(seq)) + (p0 + 8 * j), {"U": None, "M": mod_row, "D": down}[kind],
                          mid={"U": turned, "M": mod_cols}.get(prev))

            with dve.Fori(0, NSB) as i:
                mlp(i, MLP1, *plan["mlp1"], "mlp1")
            postnorm("post1", yrow, lambda e: e.wait_ge(acc_free, plan["gate"][1] + 2))
            norm("norm2", res, lambda e: e.wait_ge(S["res", "post1"], 2), col("pre_ple_norm"))
            t0, h0 = TG["ple"]
            dve.wait_ge(t_hi, h0 + 1)
            nc.vector.tensor_tensor(hlo[:, 0:2], ps[:, TB[t0 % 2]].rearrange("p (a b) -> p a b", a=2),
                                    hhi[:, 0:2].bitcast(F32), ALU.subtract).then_inc(t_free, 1)
            p0, g0 = plan["gate"]
            with dve.Fori(0, 2) as i:
                for c in range(2):
                    chunk(i * 16 + (8 * c + p0))
            dve.wait_ge(acc_free, plan["ple"][1] + 2)
            p0, g0 = plan["ple"]
            for c in range(4):
                def gated(c=c):
                    for th in range(TH):
                        y = slice(c * NCH, (c + 1) * NCH)
                        ins = nc.vector.tensor_tensor(yrow[:, th, y], ps[:, bank(g0 + c) + th], grow[:, th, y], ALU.mult)
                    ins.then_inc(acc_free, 1)
                chunk(p0 + c, gated, n=1, s=c)
            postnorm("post2", yrow, lambda e: e.wait_ge(acc_free, plan["ctx"][1] + 2))

            step(nc.vector.tensor_tensor(modT[:], modT[:], col("b_mod_2", NMOD * KT).unsqueeze(2).to_broadcast([P, NMOD * KT, 2]), ALU.add))
            for n, (part, c, gain) in enumerate(((1, 0, "norm_pre_mix_2"), (1, 1, "norm_pre_mix_2"), (4, 0, "norm_pre_mlp_2"))):
                nc.vector.scalar_tensor_tensor(out=mcol[:, n], in0=modT[:, part * KT:(part + 1) * KT, c], scalar=1.0, in1=col(gain),
                                               op0=ALU.add, op1=ALU.mult).then_inc(mcol_done, 1)
            for n, (part, gain) in enumerate(((2, "norm_post_mix_2"), (5, "norm_post_mlp_2"))):
                nc.vector.tensor_tensor(mcol[:, 3 + n], modT[:, part * KT:(part + 1) * KT, 0], col(gain), ALU.mult).then_inc(mcol_done, 1)
            dve.wait_ge(mcol_done, 5)

            def norm_mod(k, src, wait_src, gain, shift):
                mean_square(k, src, wait_src)
                dve.wait_ge(S["rstd", k], 1)
                nc.vector.tensor_scalar(xs[:, 1], src[:, 1], stat[:, 9:10], None, ALU.mult).then_inc(S["xs", k], 1)
                t0, h0 = TG[k]

                def low(g):
                    dve.wait_ge(t_hi, h0 + g + 1)
                    nc.vector.tensor_tensor(xlo[:, 2 * g:2 * g + 2], tcol[:, g % 2], xhi[:, 2 * g:2 * g + 2].bitcast(F32), ALU.subtract)\
                        .then_inc(x_lo, 1)
                for g in range(KT // 2):
                    dve.wait_ge(t_done, t0 + g + 1)
                    if g >= 2:
                        dve.wait_ge(x_lo, 8 * MODS.index(k) + g - 1)
                    for j in range(2):
                        kt = 2 * g + j
                        ins = nc.vector.tensor_scalar(tcol[:, g % 2, j], ps[:, TB[(t0 + g) % 2], j * T:(j + 1) * T],
                                                      gain[:, kt:kt + 1], shift[:, kt:kt + 1], ALU.mult, ALU.add)
                    ins.then_inc(t_free, 1)
                    if g:
                        low(g - 1)
                low(KT // 2 - 1)

            norm_mod("normc", yrow, lambda e: e.wait_ge(ctx_in, 16), mcol[:, 1], modT[:, 0:KT, 1])

            def forget(f, d, c):
                l = lb[:, d, c:c + NCH].unsqueeze(1).to_broadcast([P, TH, NCH])
                step(nc.vector.tensor_scalar(f, f, 1.0, None, ALU.add))
                step(nc.vector.reciprocal(f, f))
                step(nc.vector.scalar_tensor_tensor(out=f, in0=l, scalar=-1.0, in1=f, op0=ALU.add, op1=ALU.mult))
                return nc.vector.tensor_tensor(f, l, f, ALU.subtract)

            p0, g0 = plan["ctx"]
            for c in range(6):
                def lower_bound():
                    dve.wait_ge(lb_exp, 1)
                    l0, l1 = lg[:, :, 0], lg[:, :, 1]
                    step(nc.vector.tensor_tensor(l1, l1, l0, ALU.add))
                    step(nc.vector.reciprocal(l1, l1))
                    step(nc.vector.tensor_tensor(l0, l0, l1, ALU.mult))
                    nc.vector.tensor_scalar(lb[:], l0, 2.0 ** -64, None, ALU.max).then_inc(lb_done, 1)
                    dve.wait_ge(lb_done, 1)

                def ctx_forget(c=c - 1):
                    dve.wait_ge(acc_free, g0 + c + 3)
                    forget(pctx[:, c // 2, :, c % 2 * NCH:(c % 2 + 1) * NCH], c // 2 - 1, c % 2 * NCH).then_inc(ctx_f, 1)
                chunk(p0 + 8 * c, mid=lower_bound if c == 1 else ctx_forget if c > 2 else None)
            ctx_forget(5)
            for n in range(4):
                d, cs = n // 2, slice(n % 2 * NCH, (n % 2 + 1) * NCH)
                dve.wait_ge(ctx_k, d + 1)
                dve.wait_ge(cs_exp, n + 1)
                nc.vector.tensor_tensor(dctx[:, d, :, cs], dctx[:, d, :, cs], pctx[:, 1 + d, :, cs], ALU.mult).then_inc(cs_dec, 1)

            norm_mod("norm3", res, lambda e: e.wait_ge(st_out, 4), mcol[:, 0], modT[:, 0:KT, 0])
            p0, g0 = plan["x2"]
            for c in range(14):
                col_, g = c % 2 * NCH, g0 + c

                def x_forget(c=c - 1):
                    dve.wait_ge(acc_free, g0 + c + 3)
                    forget(rows5[:, RF + (c - 2) // 2, :, c % 2 * NCH:(c % 2 + 1) * NCH], (c - 2) // 2, c % 2 * NCH).then_inc(x_f, 1)

                def gate_conv(c=c - 1):
                    dve.wait_ge(acc_free, g0 + c + 3)
                    s = slice(c % 2 * NCH, (c % 2 + 1) * NCH)
                    nc.vector.tensor_tensor(urow[:, :, s], urow[:, :, s], cgrow[:, :, s], ALU.mult).then_inc(u_done, 1)

                def silu(c=c, g=g, col_=col_):
                    row = rows5[:, RQ + (c - 6) // 2, :, col_:col_ + NCH]
                    dve.wait_ge(sig_done, c - 5)
                    ins = nc.vector.scalar_tensor_tensor(out=row, in0=ps[:, bank(g):bank(g) + 2], scalar=SCALE if c < 8 else 1.0,
                                                         in1=row, op0=ALU.mult, op1=ALU.mult)
                    ins.then_inc(acc_free, 1)
                chunk(p0 + 8 * c, silu if 6 <= c < 10 else None,
                      mid=x_forget if 3 <= c <= 6 else gate_conv if c == 13 else None)
            gate_conv(13)

            taps = []
            wcol = lambda tap, ct: cols[:, COL["conv_dw_w_2a"] + tap * HH + ct:COL["conv_dw_w_2a"] + tap * HH + ct + 1]
            mid_tap = TAPS // 2
            for ct in range(HH):
                taps.append((ct, 0))
            for dd in range(1, mid_tap + 1):
                for sg in (1, -1):
                    for ct in range(HH // 2):
                        taps.append((ct, sg * dd))
            for dd in range(1, ROWS):
                for sg in (1, -1):
                    for ct in range(HH // 2, HH):
                        taps.append((ct, sg * dd))
            assert len(taps) == N_CONV
            sent = [0]

            def conv(count):
                for _ in range(count):
                    n = sent[0]
                    if n >= N_CONV:
                        return
                    ct, dd = taps[n]
                    if n >= HH:
                        dve.wait_ge(conv_done, n - 3)
                    a, b = max(0, -dd), max(0, dd)
                    if dd == 0:
                        ins = nc.vector.tensor_scalar(yT[:, ct], uT[:, ct], wcol(mid_tap, ct),
                                                      cols[:, COL["conv_dw_b_2"] + ct:COL["conv_dw_b_2"] + ct + 1], ALU.mult, ALU.add)
                    elif ct < HH // 2:
                        y3, u3 = (x[:, ct].rearrange("p (r c) -> p r c", c=GRID) for x in (yT, uT))
                        y3, u3 = y3[:, :, a:GRID - b], u3[:, :, a + dd:GRID - b + dd]
                        ins = nc.vector.scalar_tensor_tensor(out=y3, in0=u3, scalar=wcol(mid_tap + dd, ct), in1=y3, op0=ALU.mult, op1=ALU.add)
                    else:
                        y2, u2 = yT[:, ct, a * GRID:T - b * GRID], uT[:, ct, (a + dd) * GRID:T + (dd - b) * GRID]
                        ins = nc.vector.scalar_tensor_tensor(out=y2, in0=u2, scalar=wcol(mid_tap + dd, ct), in1=y2, op0=ALU.mult, op1=ALU.add)
                    ins.then_inc(conv_done, 1)
                    sent[0] += 1

            def decay_unit(n):
                kind, d, m, pair, ne, ns = UNITS[n]
                if n >= 2:
                    if UNITS[n - 2][5] is not None:
                        dve.wait_ge(s_done, UNITS[n - 2][5] + 1)
                    else:
                        dve.wait_ge(o2_done, UNITS[n - 2][3] + 1)
                h = slice(pair % 2 * 2, pair % 2 * 2 + 2)
                kT = (kfT, kbT)[d]
                if kind == "diag":
                    nc.vector.tensor_tensor(kD[:, n % 2], kfT[:, h], kbT[:, h], ALU.add).then_inc(qk_done, 1)
                    return
                dve.wait_ge(d_done, ne + 1)
                if kind == "init":
                    nc.vector.tensor_tensor(qD[:, n % 2], qT[:, h], dec[:, n % 2], ALU.mult).then_inc(qk_done, 1)
                    return
                halves = lambda x, i: x.rearrange("p h (b s m) -> p (h b) s m", s=2, m=m)[:, :, i]
                nc.vector.tensor_tensor(halves(qD[:, n % 2], 1 - d), halves(qT[:, h], 1 - d), halves(dec[:, n % 2], 1 - d), ALU.mult)
                nc.vector.tensor_tensor(halves(kD[:, n % 2], d), halves(kT[:, h], d), halves(dec[:, n % 2], d), ALU.mult)\
                    .then_inc(qk_done, 1)

            def keep_unit(n):
                kind, d, m, pair, ne, ns = UNITS[n]
                if ns is None:
                    return
                dve.wait_ge(s_done, ns + 1)
                dve.wait_ge(s_free, ns)
                if kind == "diag" and pair >= 2:
                    dve.wait_ge(o2_done, pair - 1)
                b = ps[:, 2 + ns % 2].rearrange("p (a b) -> p a b", b=P)
                to = sc[:, pair % 2].rearrange("p h t n -> p (h t) n")
                if kind == "diag":
                    ins = nc.vector.tensor_copy(to, b)
                elif kind == "level":
                    ins = nc.vector.copy_predicated(to, masks[:, LV[m] + d * len(LEVELS)].unsqueeze(1).to_broadcast([P, 4, P]), b)
                else:
                    ins = nc.vector.tensor_copy(cross[:, pair % 2, :, d], b[:, 0:2])
                ins.then_inc(s_free, 1)

            def norm_pair(pair):
                dve.wait_ge(oc_done, pair + 1)
                o = rows5[:, RQ, :, pair * 2 * HD:(pair + 1) * 2 * HD]
                g = rows5[:, RG, :, pair * 2 * HD:(pair + 1) * 2 * HD]
                o3 = o.rearrange("p t (h d) -> p t h d", d=HD)
                sq = tcol[:, 0]
                step(nc.vector.tensor_tensor(sq, o, o, ALU.mult))
                step(nc.vector.tensor_reduce(stat[:, 40:44], sq.rearrange("p t (h d) -> p (t h) d", d=HD), AX_X, ALU.add))
                nc.vector.tensor_scalar(stat[:, 40:44], stat[:, 40:44], 1.0 / HD, EPS, ALU.mult, ALU.add).then_inc(on_ms, 1)
                step(nc.vector.tensor_tensor(g, g, ngain[:, pair % 2 * 2 * HD:(pair % 2 + 1) * 2 * HD].unsqueeze(1).to_broadcast([P, TH, 2 * HD]), ALU.mult))
                dve.wait_ge(on_rstd, pair + 1)
                step(nc.vector.tensor_tensor(o3, o3, stat[:, 44:48].rearrange("p (t h) -> p t h", h=2).unsqueeze(3).to_broadcast([P, TH, 2, HD]), ALU.mult))
                nc.vector.tensor_tensor(o, o, g, ALU.mult).then_inc(on_done, 1)

            dve.wait_ge(clr, 2)
            dve.wait_ge(t_free, TG["u"][0] + 4)
            dve.wait_ge(masks_done, 1)
            for hg in range(2):
                dve.wait_ge(t_free, TG["qk%d" % hg][0] + 6)
                first, last = 2 * hg * PER, 2 * (hg + 1) * PER
                for n in range(first, last + 1):
                    if n < last:
                        decay_unit(n)
                    if n > first:
                        keep_unit(n - 1)
                        if n % PER == 6 and n // PER >= 1 and n // PER % 2 == 1:
                            dve.wait_ge(ng_in, 16 * (hg + 1))
                            norm_pair(n // PER - 1)
                    conv(2)
                dve.wait_ge(ng_in, 16 * (hg + 1))
                norm_pair(2 * hg + 1)
            conv(N_CONV)

            bc = lambda x: x.unsqueeze(1).to_broadcast([P, HH, T])
            dve.wait_ge(ln_mean, 1)
            dve.wait_ge(conv_done, N_CONV)
            nc.vector.tensor_tensor(yT[:], yT[:], bc(lnm[:, 0]), ALU.subtract).then_inc(ln_cent, 1)
            dve.wait_ge(ln_var, 1)
            nc.vector.tensor_scalar(lnm[:, 1], ps[:, 3, 0:T], 1.0 / DH, EPS, ALU.mult, ALU.add).then_inc(ln_ms, 1)
            dve.wait_ge(ln_pow, 1)
            nc.vector.tensor_tensor(yT[:], yT[:], bc(lnm[:, 1]), ALU.mult).then_inc(ln_norm, 1)
            dve.wait_ge(ln_z, HH)
            nc.vector.tensor_tensor(ysq[:], ysq[:], ysg[:], ALU.mult).then_inc(ln_u, 1)
            dve.wait_ge(c_hi, 1)
            nc.vector.tensor_tensor(hlo[:, HH:KT], ysq[:], hhi[:, HH:KT].bitcast(F32), ALU.subtract).then_inc(c_lo, 1)
            t0, h0 = TG["o2"]
            dve.wait_ge(c_lo, 1)

            def low_parts(name, groups, hi, lo):
                t0, h0 = TG[name]
                for g in range(groups):
                    dve.wait_ge(t_hi, h0 + g + 1)
                    nc.vector.tensor_tensor(lo[:, 2 * g:2 * g + 2], ps[:, TB[(t0 + g) % 2]].rearrange("p (a b) -> p a b", a=2),
                                            hi[:, 2 * g:2 * g + 2].bitcast(F32), ALU.subtract).then_inc(t_free, 1)
            low_parts("o2", 4, hhi, hlo)

            def pairs_of(name, n=8):
                p0, g0 = plan[name]
                with dve.Fori(0, 2) as i:
                    for c in range(2):
                        chunk(i * (2 * n) + (n * c + p0), n=n)

            def gated_by(name, dst, add_to=None):
                p0, g0 = plan[name]
                dve.wait_ge(acc_free, g0 + 2)
                for c in range(4):
                    def f(c=c):
                        s = slice(c * NCH, (c + 1) * NCH)
                        nc.vector.tensor_tensor(dst[:, :, s], ps[:, bank(g0 + c):bank(g0 + c) + 2], dst[:, :, s], ALU.mult).then_inc(acc_free, 1)
                        if add_to is not None:
                            dve.wait_ge(acc_free, g0 + c + 3)
                            nc.vector.tensor_tensor(add_to[:, :, s], add_to[:, :, s], dst[:, :, s], ALU.add).then_inc(merged, 1)
                    chunk(p0 + 4 * c, f, n=4)
            pairs_of("gc")
            gated_by("pw", yrow)
            pairs_of("gh")
            gated_by("ho", grow, yrow)
            low_parts("y", 8, xhi, xlo)
            pairs_of("wo2")
            dve.wait_ge(reload, 16)
            postnorm("post3", yrow, lambda e: e.wait_ge(acc_free, plan["mlp2"][1] + 2))
            norm_mod("norm4", res, lambda e: e.wait_ge(S["res", "post3"], 2), mcol[:, 2], modT[:, 3 * KT:4 * KT, 0])
            dve.wait_ge(macc_clear, 2)
            with dve.Fori(0, NSB) as i:
                mlp(i, MLP2, *plan["mlp2"], "mlp2")
            postnorm("post4", yrow, lambda e: e.wait_ge(acc_free, plan["end"][1] + 2))

        @block.gpsimd
        def _(pool):
            half = stat[:, 128:144]
            nc.gpsimd.memset(half, -0.5).then_inc(m_sel, 1)
            nc.gpsimd.memset(stat[:, 208:209], 0.0).then_inc(m_out, 1)
            for n in range(2):
                nc.gpsimd.memset(stat[:, 200 + n:201 + n], 0.0).then_inc(acc_free, 1)
                nc.gpsimd.memset(stat[:, 204 + n:205 + n], 0.0).then_inc(sq_done, 1)

            def rstd(k):
                pool.wait_ge(S["ms", k], 1)
                nc.gpsimd.tensor_tensor(stat[:, 8:10], stat[:, 4:6], stat[:, 128:130], ALU.pow).then_inc(S["rstd", k], 1)

            def add_half(k):
                pool.wait_ge(S["scaled", k], 1)
                nc.gpsimd.tensor_tensor(res[:, 0], res[:, 0], xs[:, 0], ALU.add).then_inc(S["res", k], 1)

            pool.wait_ge(m_sel, 1)
            rstd("norm0")
            pool.wait_ge(bias_in, 16 * ROWS * B_H)
            pool.wait_ge(early_in, 16)
            b3 = bm[:].rearrange("p t h (a b) -> p (t h a) b", b=GRID)
            nc.gpsimd.tensor_tensor(b3, b3, colmask.unsqueeze(1).to_broadcast([P, TH * B_H * ROWS, GRID]), ALU.add)\
                .then_inc(bias_done, 1)
            for n in range(4):
                pool.wait_ge(qk_ss, n + 1)
                nc.gpsimd.tensor_tensor(stat[:, 24:24 + SET], stat[:, 16:16 + SET], stat[:, 128:128 + SET], ALU.pow)\
                    .then_inc(qk_rstd, 1)
            rstd("post0")
            add_half("post0")
            rstd("norm1")
            pool.wait_ge(S["res", "post0"], 2)
            nc.gpsimd.memset(yrow[:], 0.0).then_inc(macc_clear, 1)

            def mlp_squares(i, seq, g0, k):
                for j, (kind, c) in enumerate(seq):
                    for th in range(TH if kind == "U" else 0):
                        pool.wait_ge(acc_free, i * len(seq) + (g0 + j + 3))
                        pool.wait_ge(t_done, i * 8 + (TG[k][0] + 2 * c))
                        nc.gpsimd.tensor_tensor(sqrow[:, th], rrow[:, th], rrow[:, th], ALU.mult).then_inc(sq_done, 1)

            with pool.Fori(0, NSB) as i:
                mlp_squares(i, MLP1, plan["mlp1"][1], "mlp1")
            rstd("post1")
            add_half("post1")
            rstd("norm2")
            rstd("post2")
            add_half("post2")

            rstd("normc")
            pool.wait_ge(lg_in, 16)
            l0, l1 = lg[:, :, 0], lg[:, :, 1]
            nc.gpsimd.tensor_tensor(l1, l1, l0, ALU.subtract).then_inc(pool_own, 1)
            pool.wait_ge(pool_own, 1)
            nc.gpsimd.tensor_scalar(l0, l1, -1.0, 0.0, ALU.mult, ALU.min).then_inc(lb_diff, 1)
            pool.wait_ge(lb_diff, 1)
            nc.gpsimd.tensor_scalar(l1, l1, 0.0, None, ALU.min).then_inc(lb_diff, 1)
            for d in range(2):
                pool.wait_ge(ctx_ln, d + 1)
                nc.gpsimd.tensor_scalar(pctx[:, 1 + d], pctx[:, 1 + d], -1.0, 1.0, ALU.mult, ALU.add).then_inc(ctx_k, 1)
            rstd("norm3")
            pool.wait_ge(masks_in, 16)
            nc.gpsimd.tensor_copy(masks[:], mask_rows[:]).then_inc(masks_done, 1)
            pool.wait_ge(x_f, 4)
            nc.gpsimd.memset(kD[:], 0.0).then_inc(clr, 1)
            nc.gpsimd.memset(qD[:], 0.0).then_inc(clr, 1)
            for hg in range(2):
                for d in range(2):
                    pool.wait_ge(lf_done, 2 * hg + d + 1)
                    f = rows5[:, RF + d, :, hg * GW:(hg + 1) * GW]
                    nc.gpsimd.tensor_scalar(f, f, -1.0, 1.0, ALU.mult, ALU.add).then_inc(k_done, 1)
                for pair in (2 * hg, 2 * hg + 1):
                    pool.wait_ge(on_ms, pair + 1)
                    nc.gpsimd.tensor_tensor(stat[:, 44:48], stat[:, 40:44], stat[:, 128:132], ALU.pow).then_inc(on_rstd, 1)
            pool.wait_ge(ln_ms, 1)
            nc.gpsimd.tensor_tensor(lnm[:, 1], lnm[:, 1], stat[:, 128:129].to_broadcast([P, T]), ALU.pow).then_inc(ln_pow, 1)
            rstd("post3")
            add_half("post3")
            rstd("norm4")
            pool.wait_ge(S["res", "post3"], 2)
            nc.gpsimd.memset(yrow[:], 0.0).then_inc(macc_clear, 1)
            with pool.Fori(0, NSB) as i:
                mlp_squares(i, MLP2, plan["mlp2"][1], "mlp2")
            rstd("post4")
            add_half("post4")


INPUTS = ["x", "p", "pre_mix_norm", "w_in", "q_norm", "k_norm", "rel_pos_bias", "w_o", "post_mix_norm", "pre_mlp_norm",
          "w_up", "w_down", "post_mlp_norm", "pre_ple_norm", "w_ple_gate", "w_ple_proj", "post_ple_norm", "c_2", "ctx_2",
          "c_ctx_2", "w_mod_2", "b_mod_2", "norm_pre_mix_2", "norm_post_mix_2", "norm_pre_mlp_2", "norm_post_mlp_2",
          "w_in_2", "conv_dw_w_2", "conv_dw_b_2", "conv_ln_g_2", "conv_ln_b_2", "conv_pw_w_2", "hgrn_lb_logits_2",
          "hgrn_norm_g_2", "hgrn_out_w_2", "w_out_2", "mlp_w1_2", "mlp_w2_2"]


def kernel(**inputs):
    import concourse.bacc as bacc
    from concourse.bass_utils import run_bass_kernel_spmd

    nc = bacc.Bacc("TRN2", target_bir_lowering=False, num_devices=1)
    arrays = {name: np.ascontiguousarray(inputs[name]) for name in INPUTS}
    arrays.update(shape_constants())
    I = {name: nc.dram_tensor(name, a.shape, mybir.dt.from_np(a.dtype), kind="ExternalInput").ap()
         for name, a in arrays.items()}
    out = nc.dram_tensor("out", (1, T, D), F32, kind="ExternalOutput").ap()
    build(nc, I, out)
    result = run_bass_kernel_spmd(nc, [arrays], core_ids=[0])
    return result.results[0]["out"]
```

```python
from contextlib import ExitStack

import numpy as np

import concourse.bass as bass
from concourse import mybir

ALU = mybir.AluOpType
ACT = mybir.ActivationFunctionType
F32 = mybir.dt.float32
F32R = mybir.dt.float32r
I8 = mybir.dt.int8
AX_X = mybir.AxisListType.X

P = 128
T = 256
TH = T // P
D = 2048
KT = D // P
NCH = 512
HD = 128
GRID = 64
ROWS = T // GRID
A_Q, A_KV, B_H = 8, 2, 8
IN1 = (A_Q + 2 * A_KV + 3 * B_H) * HD
DFF = 4 * D
PLE = 256
RPB_R, RPB_C = 15, 31
WIN = 16
EPS = 1e-6
SCALE = float(HD) ** -0.5
DH = 1024
HH = DH // HD
TAPS = 31
NSLOT = 4
NMOD = 6
FAR = -1e30

VEC_GROUPS = [
    [("pre_mix_norm", 16), ("pre_mlp_norm", 16), ("pre_ple_norm", 16), ("norm_pre_mix_2", 16),
     ("norm_pre_mlp_2", 16), ("norm_post_mix_2", 16), ("norm_post_mlp_2", 16)],
    [("b_mod_2", 96), ("c_2", 16), ("c_ctx_2", 16)],
    [("conv_dw_w_2a", 128)],
    [("conv_dw_w_2b", 120)],
    [("conv_dw_b_2", 8), ("conv_ln_g_2", 8), ("conv_ln_b_2", 8)],
]
COL = {}
_n = 0
for _g in VEC_GROUPS:
    for _name, _rows in _g:
        COL[_name] = _n
        _n += _rows
NCOL = _n

LEVELS = [64, 32, 16, 8, 4, 2, 1]
NHEAD = B_H + A_Q
HEAD_KT = [A_Q + h for h in range(B_H)] + list(range(A_Q))
MODS = ["normc", "norm3", "norm4"]
NORMS = ["norm0", "norm1", "norm2"] + MODS
POSTS = ["post0", "post1", "post2", "post3", "post4"]
RMS = {k: n for n, k in enumerate(["norm0", "post0", "norm1", "post1", "norm2", "post2", "normc", "norm3", "post3", "norm4",
                                   "post4"])}


def shape_constants():
    t = np.arange(T)
    n = HD // 4
    freq = (np.float32(10000.0) ** (-np.arange(n, dtype=np.float32) / np.float32(n))).astype(np.float32)
    ar = (t // GRID).astype(np.float32)[:, None] * freq[None]
    ac = (t % GRID).astype(np.float32)[:, None] * freq[None]
    cos = np.concatenate([np.cos(ar), np.cos(ar), np.cos(ac), np.cos(ac)], 1)
    sin = np.concatenate([-np.sin(ar), np.sin(ar), -np.sin(ac), np.sin(ac)], 1)
    rope = np.stack([cos, sin]).astype(np.float32)
    rope = rope.reshape(2, TH, P, HD).transpose(2, 0, 1, 3).reshape(P, -1)
    c = np.arange(P) % GRID
    c0 = np.clip(c - WIN // 2, 0, GRID - WIN)
    kc = np.arange(GRID)
    inside = (kc[None] >= c0[:, None]) & (kc[None] < c0[:, None] + WIN)
    colmask = np.where(inside, 0.0, FAR).astype(np.float32)
    ident = np.eye(P, dtype=np.float32)
    small = np.concatenate([ident, np.ones((P, P), np.float32)], 1)
    j = np.arange(P)[:, None]
    q = np.arange(P)[None]
    sums, masks = [], []
    for m in LEVELS:
        mid = q // (2 * m) * (2 * m) + m
        second = q >= mid
        sums.append(np.where(second, (j >= mid) & (j <= q), (j > q) & (j < mid)))
    for m in LEVELS:
        mid = q // (2 * m) * (2 * m) + m
        second = q >= mid
        sums.append(np.where(second, (j >= mid) & (j < q), (j >= q) & (j < mid)))
    sums += [j <= q, j > q, j >= q, j < q]
    s, tt = j, q
    for m in LEVELS:
        same = s // (2 * m) == tt // (2 * m)
        masks.append(same & (s % (2 * m) < m) & (tt % (2 * m) >= m))
    for m in LEVELS:
        same = s // (2 * m) == tt // (2 * m)
        masks.append(same & (s % (2 * m) >= m) & (tt % (2 * m) < m))
    masks.append(s == tt)
    sums = np.concatenate([x.astype(np.float32) for x in sums], 1)
    masks = np.concatenate([x.astype(np.float32) for x in masks], 1)
    early = np.concatenate([rope, colmask], 1)
    return {"k_small": small, "k_early": np.ascontiguousarray(early),
            "k_sums": np.ascontiguousarray(sums), "k_masks": np.ascontiguousarray(masks)}


def build(nc, I, out):
    ctx = ExitStack()
    with ctx:
        base = nc.sbuf_base + (-nc.sbuf_base) % 64
        limit = nc.sbuf_usable_end
        cursor = [base]

        def at(name, shape, dt, offset):
            size = int(np.prod(shape[1:])) * (1 if dt == I8 else 4)
            assert offset + size <= limit, (name, offset + size, limit)
            return nc.alloc_sbuf_tensor_at(name, shape, dt, offset=offset)

        def sb(name, shape, dt):
            size = int(np.prod(shape[1:])) * (1 if dt == I8 else 4)
            t = at(name, shape, dt, cursor[0])
            cursor[0] += size + (-size) % 32
            return t

        def sem(name):
            return ctx.enter_context(nc.semaphore(name))

        K = 1024
        raw = sb("raw", [P, NSLOT, 2, NCH], F32)
        whi = sb("whi", [P, NSLOT, 2, NCH], F32R)
        wlo = sb("wlo", [P, NSLOT, 2, NCH], F32R)
        xhi_at = cursor[0]
        xhi = sb("xhi", [P, KT, T], F32R)
        xlo_at = cursor[0]
        xlo = sb("xlo", [P, KT, T], F32R)
        hhi_at = cursor[0]
        hhi = sb("hhi", [P, KT, T], F32R)
        hlo_at = cursor[0]
        hlo = sb("hlo", [P, KT, T], F32R)
        res_at = cursor[0]
        res = sb("res", [P, TH, D], F32)
        small = sb("small", [P, 2 * P], F32)
        ident = small[:, 0:P]
        ones = small[:, P:2 * P]
        cols = sb("cols", [P, NCOL], F32)
        mcol = sb("mcol", [P, 5, KT], F32)
        modT = sb("modT", [P, NMOD * KT, 2], F32)
        lev_at = cursor[0]
        sums = sb("sums", [P, 2 * len(LEVELS) + 4, P], F32)
        masks = sb("masks", [P, 2 * len(LEVELS) + 1, P], I8)
        tcol = sb("tcol", [P, 2, 2, T], F32)
        stat = sb("stat", [P, 216], F32)
        ngain = sb("ngain", [P, NCH], F32)
        work_at = cursor[0]
        early = at("early", [P, 2 * TH * HD + GRID], F32, lev_at)
        rope = early[:, 0:2 * TH * HD].rearrange("p (s h d) -> p s h d", s=2, h=TH)
        colmask = early[:, 2 * TH * HD:]

        xs = at("xs", [P, TH, D], F32, work_at + 16 * K)
        yrow = at("yrow", [P, TH, D], F32, work_at)
        gbc = at("gbc", [P, D], F32, work_at + 32 * K)
        rrow = at("rrow", [P, TH, NCH], F32, work_at + 32 * K)
        sqrow = at("sqrow", [P, TH, NCH], F32, work_at + 36 * K)
        grow = at("grow", [P, TH, D], F32, work_at + 16 * K)
        prow = at("prow", [P, TH, PLE], F32, work_at + 48 * K)
        vecs = at("vecs", [P, len(VEC_GROUPS), P], F32, work_at + 48 * K)
        MSLOT = 4
        mraw = at("mraw", [P, MSLOT, 2, NCH], F32, work_at + 40 * K)
        macc = at("macc", [P, 2, 3, NCH], F32, lev_at)
        NA = A_Q + A_KV
        SET = NA // 2
        proj = at("proj", [P, TH, IN1], F32, work_at)
        bm = at("bm", [P, TH, B_H, T], F32, work_at + 36 * K)
        NB = B_H * RPB_R * RPB_C
        bias_rows = nc.dram_tensor("bias_rows", (GRID, NB), F32, kind="Internal").ap()
        qkT = at("qkT", [P, 26, T], F32, hhi_at)
        prob = at("prob", [P, 2, TH, T], F32, hhi_at + 26 * K)
        probT = [at("probT0", [P, TH, T], F32, hhi_at + 30 * K), at("probT1", [P, TH, T], F32, work_at + 52 * K)]
        gqk = at("gqk", [P, NA * HD], F32, xhi_at)
        rota = at("rota", [P, 2, SET * HD], F32, xlo_at)


        pctx = at("pctx", [P, 3, TH, DH], F32, work_at)
        lfc = at("lfc", [P, 2, TH, DH], F32, work_at + 24 * K)
        S0 = at("S0", [P, 2, DH], F32, work_at + 40 * K)
        lb = at("lb", [P, 2, DH], F32, work_at + 48 * K)
        lg = at("lg", [P, 2, 2, DH], F32, hhi_at)
        mask_rows = at("mask_rows", [P, 2 * len(LEVELS) + 1, P], F32, hhi_at)
        dctx = at("dctx", [P, 2, TH, DH], F32, hlo_at)
        rows5 = at("rows5", [P, 5, TH, DH], F32, work_at)
        RV, RF, RQ, RG = 0, 1, 3, 4
        urow = at("urow", [P, TH, DH], F32, res_at)
        cgrow = at("cgrow", [P, TH, DH], F32, res_at + 8 * K)
        uT = at("uT", [P, HH, T], F32, hlo_at + 8 * K)
        yT = at("yT", [P, HH, T], F32, hhi_at + 8 * K)
        ysq = at("ysq", [P, HH, T], F32, hhi_at)
        ysg = at("ysg", [P, HH, T], F32, hlo_at)
        lnm = at("lnm", [P, T], F32, work_at + 48 * K)
        GW = NCH
        lf = at("lf", [P, 2, TH, GW], F32, res_at)
        qT = at("qT", [P, 4, T], F32, res_at + 8 * K)
        kfT = at("kfT", [P, 4, T], F32, res_at + 12 * K)
        kbT = at("kbT", [P, 4, T], F32, work_at + 48 * K)
        kD = at("kD", [P, 2, 2, T], F32, work_at + 52 * K)
        sc = at("sc", [P, 2, 2, TH, P], F32, hhi_at)
        cross = at("cross", [P, 2, 2, 2, P], F32, hhi_at + 4 * K)
        dec = at("dec", [P, 2, 2, T], F32, hlo_at)
        qD = at("qD", [P, 2, 2, T], F32, hlo_at + 4 * K)
        nsq = at("nsq", [P, TH, 2 * HD], F32, work_at + 56 * K)
        TAP_UNITS = [(ct, sg * dd) for dd in range(1, TAPS // 2 + 1) for sg in (1, -1) for ct in range(0, HH // 2, 2)]
        TAP_UNITS += [(ct, sg * dd) for dd in range(1, ROWS) for sg in (1, -1) for ct in range(HH // 2, HH, 2)]
        TAP_LAST = {}
        for n, (ct, dd) in enumerate(TAP_UNITS):
            TAP_LAST[n] = max([k for k in range(n) if TAP_UNITS[k][0] == ct], default=None)

        def tap_part(x, ct, dd, of_input):
            a, b = max(0, -dd), max(0, dd)
            off = dd if of_input else 0
            if ct < HH // 2:
                return x.rearrange("p (r c) -> p r c", c=GRID)[:, :, a + off:GRID - b + off]
            return x[:, (a + off) * GRID:T + (off - b) * GRID]

        def tap_two(x, ct, dd):
            a, b = max(0, -dd), max(0, dd)
            if ct < HH // 2:
                return x.rearrange("p k (r c) -> p (k r) c", c=GRID)[:, :, a:GRID - b]
            return x[:, :, a * GRID:T - b * GRID]

        scratch = nc.dram_tensor("x_mid", (P, TH, D), F32, kind="Internal").ap()

        UNITS = []
        n_e = n_s = 0
        for pair in range(HH // 2):
            kinds = [("diag", 0, 0)] + [("level", d, m) for m in LEVELS for d in (0, 1)]
            kinds += [("cross", 0, P), ("cross", 1, P), ("init", 0, 0), ("init", 1, 0)]
            for kind, d, m in kinds:
                has_e, has_s = kind != "diag", kind != "init"
                UNITS.append((kind, d, m, pair, n_e if has_e else None, n_s if has_s else None))
                n_e += has_e
                n_s += has_s
        PER = len(UNITS) // (HH // 2)
        N_E, N_S = [], []
        a = b = 0
        for u in UNITS:
            N_E.append(a)
            N_S.append(b)
            a += u[4] is not None
            b += u[5] is not None
        LV = {m: k for k, m in enumerate(LEVELS)}
        PRE_IN, SUF_EX, SUF_IN, PRE_EX = (2 * len(LEVELS) + k for k in range(4))

        ps = ctx.enter_context(nc.psum_tensor("ps", [P, 8, NCH], F32))
        TB = [4, 5]
        MB = 6

        landed = [sem(f"landed{i}") for i in range(NSLOT)]
        hi_done = sem("hi_done")
        lo_done = sem("lo_done")
        pe_done = sem("pe_done")
        acc_free = sem("acc_free")
        t_done = sem("t_done")
        t_free = sem("t_free")
        t_hi = sem("t_hi")
        x_lo = sem("x_lo")
        dve_step = sem("dve_step")
        small_in = sem("small_in")
        early_in = sem("early_in")
        x_in = sem("x_in")
        vec_in = sem("vec_in")
        vec_turned = sem("vec_turned")
        vec_cols = sem("vec_cols")
        c_exp = sem("c_exp")
        mod_out = sem("mod_out")
        half_set = sem("half_set")
        silu_done = sem("silu_done")
        m_landed = [sem(f"m_landed{i}") for i in range(MSLOT)]
        m_mul = sem("m_mul")
        m_red = sem("m_red")
        bias_copied = sem("bias_copied")
        bias_in = sem("bias_in")
        bias_done = sem("bias_done")
        gqk_in = sem("gqk_in")
        qk_ss = sem("qk_ss")
        qk_rstd = sem("qk_rstd")
        rope_done = sem("rope_done")
        sc_done = sem("sc_done")
        sc_free = sem("sc_free")
        mx_done = sem("mx_done")
        exp_done = sem("exp_done")
        p_done = sem("p_done")
        pt_done = sem("pt_done")
        pt_copied = sem("pt_copied")
        o_done = sem("o_done")
        o_hi = sem("o_hi")
        o_lo = sem("o_lo")
        sq_done = sem("sq_done")
        macc_clear = sem("macc_clear")
        p_in = sem("p_in")
        out_done = sem("out_done")
        ss_done = sem("ss_done")
        ms_done = sem("ms_done")
        rstd_done = sem("rstd_done")

        mcol_done = sem("mcol_done")
        lg_in = sem("lg_in")
        lb_diff = sem("lb_diff")
        lb_exp = sem("lb_exp")
        lb_done = sem("lb_done")
        ctx_in = sem("ctx_in")
        ctx_f = sem("ctx_f")
        ctx_ln = sem("ctx_ln")
        ctx_k = sem("ctx_k")
        cs_done = sem("cs_done")
        cs_exp = sem("cs_exp")
        cs_dec = sem("cs_dec")
        st_done = sem("st_done")
        st_out = sem("st_out")
        spill = sem("spill")
        sums_in = sem("sums_in")
        sig_done = sem("sig_done")
        x_f = sem("x_f")
        u_done = sem("u_done")
        lf_done = sem("lf_done")
        k_done = sem("k_done")
        e_done = sem("e_done")
        d_done = sem("d_done")
        qk_done = sem("qk_done")
        s_done = sem("s_done")
        s_free = sem("s_free")
        o2_done = sem("o2_done")
        oc_done = sem("oc_done")
        on_ms = sem("on_ms")
        on_rstd = sem("on_rstd")
        on_done = sem("on_done")
        ng_in = sem("ng_in")
        conv_done = sem("conv_done")
        tap_done = sem("tap_done")
        clr = sem("clr")
        ln_sum = sem("ln_sum")
        ln_mean = sem("ln_mean")
        ln_cent = sem("ln_cent")
        ln_sq = sem("ln_sq")
        ln_var = sem("ln_var")
        ln_ms = sem("ln_ms")
        ln_pow = sem("ln_pow")
        ln_rows = sem("ln_rows")
        ln_norm = sem("ln_norm")
        ln_z = sem("ln_z")
        ln_s = sem("ln_s")
        ln_u = sem("ln_u")
        c_hi = sem("c_hi")
        c_lo = sem("c_lo")
        merged = sem("merged")
        reload = sem("reload")
        masks_in = sem("masks_in")
        masks_done = sem("masks_done")
        gb_done = sem("gb_done")
        pool_own = sem("pool_own")
        S = {}
        for k in NORMS:
            S["xs", k] = sem(f"xs_{k}")
        for k in POSTS:
            for w in ("gain", "scaled", "res"):
                S[w, k] = sem(f"{w}_{k}")

        def pieces(w):
            return w.rearrange("(q k p) n -> p q k n", p=P, k=2)

        w_in, w_o, w_up, w_down = (pieces(I[n][0]) for n in ("w_in", "w_o", "w_up", "w_down"))
        w_gate, w_ple, w_mod = (pieces(I[n][0]) for n in ("w_ple_gate", "w_ple_proj", "w_mod_2"))

        SEQ = [("U", c) for c in range(4)] + [("D", c) for c in range(4)]
        MPER = {"mlp1": 5, "mlp2": 1}
        MCTX = (2 * D // NCH) // (DFF // D)
        M0 = {"mlp1": 0, "mlp2": 5 * (DFF // D)}
        MAT = {"mlp1": {j: (0, 2, 3, 5, 6) for j in range(8)}, "mlp2": {j: (2,) for j in range(8)}}
        NSB = DFF // D
        plan = {}
        pc = [0, 0]

        def stage(name, chunks, per):
            plan[name] = (pc[0], pc[1])
            pc[0] += chunks * per
            pc[1] += chunks

        stage("in", IN1 // NCH, 8)
        stage("o", 4, 8)
        stage("mlp1", len(SEQ) * NSB, 8)
        stage("gate", 4, 8)
        stage("ple", 4, 1)
        stage("ctx", 6, 8)
        stage("x2", 14, 8)
        stage("gc", 4, 8)
        stage("pw", 4, 4)
        stage("gh", 4, 8)
        stage("ho", 4, 4)
        stage("wo2", 4, 8)
        stage("mlp2", len(SEQ) * NSB, 8)
        stage("end", 0, 0)
        n_pieces = pc[0]
        N_MCH = NMOD * D // NCH

        def mod_chunk_of(i, k, m):
            if k == "mlp2":
                return i + M0[k]
            return i * MCTX + m if m < MCTX else i * (MPER[k] - MCTX) + (NSB * MCTX + m - MCTX)

        def mod_ops(i, k, q):
            ends = [0]
            for n in range(8 * MPER[k]):
                ends.append(ends[-1] + (4 if k == "mlp1" and n < 8 * MCTX else 2))
            at_q = ends[q + 1] if q >= 0 else ends[q] - ends[-1]
            return i * ends[-1] + (at_q + 16 + (NSB * 16 * (MPER["mlp1"] + MCTX) if k == "mlp2" else 0))

        TURN_U = 4
        def mod_extra(k, j, f):
            at_u = MAT[k][j]
            return {u: (lambda q=j * len(at_u) + r: f(q)) for r, u in enumerate(at_u)}

        def bank(g):
            return 2 * (g % 2)

        def col(name, n=KT):
            return cols[:, COL[name]:COL[name] + n]

        def rows_of(x):
            return x.rearrange("(h p) n -> p h n", p=P)

        TG = {}
        tc = [0, 0]
        for name, groups, counted in (("norm0", 8, 1), ("attention", 13, 0), ("norm1", 8, 1), ("mlp1", 8 * NSB, 1),
                                      ("norm2", 8, 1), ("ple", 1, 1), ("normc", 8, 1), ("norm3", 8, 1), ("u", 4, 0),
                                      ("qk0", 6, 0), ("qk1", 6, 0), ("o2", 4, 1), ("y", 8, 1), ("norm4", 8, 1),
                                      ("mlp2", 8 * NSB, 1)):
            TG[name] = tuple(tc)
            tc = [tc[0] + groups, tc[1] + groups * counted]

        block = ctx.enter_context(nc.Block())

        @block.sync
        def _(sp):
            sp.dma_start(small[:], I["k_small"]).then_inc(small_in, 16)
            for gi, group in enumerate(VEC_GROUPS):
                r = 0
                for name, rows in group:
                    if name == "conv_dw_w_2a":
                        src = I["conv_dw_w_2"][0].rearrange("a (b p) -> (a b) p", p=P)[0:128]
                    elif name == "conv_dw_w_2b":
                        src = I["conv_dw_w_2"][0].rearrange("a (b p) -> (a b) p", p=P)[128:248]
                    elif name == "c_ctx_2":
                        src = I[name].rearrange("(b p) -> b p", p=P)
                    else:
                        src = I[name][0].rearrange("(b p) -> b p", p=P)
                    sp.dma_start(vecs[r:r + rows, gi, :], src).then_inc(vec_in, 16)
                    r += rows
            sp.dma_start(early[:], I["k_early"]).then_inc(early_in, 16)

            def load(src, p, s):
                if not (isinstance(p, int) and p < NSLOT):
                    sp.wait_ge(lo_done, p - (NSLOT - 1))
                sp.dma_start(raw[:, s % NSLOT], src).then_inc(landed[s % NSLOT], 16)

            def chunk(w, p, col, n=8, s=0, extra=()):
                for u in range(n):
                    load(w[:, u, :, bass.ds(col, NCH)], p + u, s + u)
                    if u in extra:
                        extra[u]()

            chunk(w_in, 0, 0)
            with sp.Fori(1, IN1 // NCH) as i:
                chunk(w_in, i * 8, i * NCH)
            with sp.Fori(0, 4) as i:
                chunk(w_o, i * 8 + plan["o"][0], i * NCH)

            def mod_load(i, k, q):
                sp.wait_ge(m_mul, mod_ops(i, k, q - MSLOT))
                sp.dma_start(mraw[:, q % MSLOT], w_mod[:, q % 8, :, bass.ds(mod_chunk_of(i, k, q // 8) * NCH, NCH)])\
                    .then_inc(m_landed[q % MSLOT], 16)

            def mlp(k, up, down):
                p0 = plan[k][0]
                with sp.Fori(0, NSB) as i:
                    for j, (kind, c) in enumerate(SEQ):
                        p = i * (8 * len(SEQ)) + (p0 + 8 * j)
                        extra = mod_extra(k, j, lambda q: mod_load(i, k, q))
                        if kind == "U":
                            chunk(up, p, i * D + c * NCH, extra=extra)
                        else:
                            for u in range(8):
                                src = down[:, bass.ds(i * 8 + u, 1), :, c * NCH:(c + 1) * NCH]
                                load(src.rearrange("p a k n -> p (a k) n"), p + u, u)
                                if u in extra:
                                    extra[u]()

            mlp("mlp1", w_up, w_down)
            with sp.Fori(0, 4) as i:
                chunk(w_gate, i * 8 + plan["gate"][0], i * NCH)
            for c in range(4):
                chunk(w_ple, plan["ple"][0] + c, c * NCH, n=1, s=c)

            w_x2, w_pw, w_ho, w_wo2 = (pieces(I[n][0]) for n in ("w_in_2", "conv_pw_w_2", "hgrn_out_w_2", "w_out_2"))
            w_up2, w_down2 = pieces(I["mlp_w1_2"][0]), pieces(I["mlp_w2_2"][0])
            c_gate, c_half = 7 * DH, 7 * DH + D

            def loop(w, name, chunks, col, n=8):
                with sp.Fori(0, chunks) as i:
                    chunk(w, i * n + plan[name][0], i * NCH + col, n=n)
            loop(w_x2, "ctx", 6, 0)
            loop(w_x2, "x2", 14, 0)
            loop(w_x2, "gc", 4, c_gate)
            loop(w_pw, "pw", 4, 0, n=4)
            loop(w_x2, "gh", 4, c_half)
            loop(w_ho, "ho", 4, 0, n=4)
            loop(w_wo2, "wo2", 4, 0)
            mlp("mlp2", w_up2, w_down2)
            chunk(w_down2, n_pieces, 0, n=3)

        @block.scalar
        def _(act):
            def split(p, s):
                if isinstance(p, int) and p >= n_pieces:
                    return
                act.wait_ge(landed[s % NSLOT], (p - s % NSLOT) * 4 + 16)
                if not (isinstance(p, int) and p < NSLOT):
                    act.wait_ge(pe_done, p - (NSLOT - 1))
                nc.scalar.activation(whi[:, s % NSLOT], raw[:, s % NSLOT], ACT.Copy).then_inc(hi_done, 1)

            def chunk(p, evac=None, n=8, s=0, extra=()):
                for u in range(n):
                    if u in extra:
                        extra[u]()
                    split(p + (3 + u), s + 3 + u)
                if evac:
                    act.wait_ge(pe_done, p + n)
                    evac()

            def evac_to(dst, col, g, func=ACT.Copy, scale=1.0):
                def f():
                    for th in range(TH):
                        ins = nc.scalar.activation(dst[:, th, bass.ds(col, NCH)], ps[:, bank(g) + th], func, scale=scale)
                    ins.then_inc(acc_free, 1)
                return f

            def norm(k, src, wait_src, gain):
                wait_src(act)
                nc.scalar.activation(xs[:, 0], src[:, 0], ACT.Square, accum_out=stat[:, 0:1]).then_inc(ss_done, 1)
                act.wait_ge(rstd_done, RMS[k] + 1)
                nc.scalar.activation(xs[:, 0], src[:, 0], ACT.Copy, scale=stat[:, 8:9]).then_inc(S["xs", k], 1)
                t0, h0 = TG[k]
                for g in range(KT // 2):
                    act.wait_ge(t_done, t0 + g + 1)
                    for j in range(2):
                        ins = nc.scalar.activation(xhi[:, 2 * g + j], ps[:, TB[(t0 + g) % 2], j * T:(j + 1) * T], ACT.Copy,
                                                   scale=gain[:, 2 * g + j:2 * g + j + 1])
                    ins.then_inc(t_hi, 1)

            def postnorm(k, row, wait_row, gain):
                wait_row(act)
                act.dma_start(gbc[:], gain.partition_broadcast(P)).then_inc(S["gain", k], 16)
                nc.scalar.activation(xs[:, 0], row[:, 0], ACT.Square, accum_out=stat[:, 0:1]).then_inc(ss_done, 1)

            act.dma_start(res[:], rows_of(I["x"][0])).then_inc(x_in, 16)
            act.dma_start(bias_rows, bass.AP(I["rel_pos_bias"].tensor, 0, [[0, GRID], [1, NB]])).then_inc(bias_copied, 16)
            for u in range(3):
                split(u, u)
            act.wait_ge(vec_cols, 1)
            nc.scalar.activation(stat[:, 64:96], cols[:, COL["c_2"]:COL["c_2"] + 32], ACT.Exp, scale=-1.0).then_inc(c_exp, 1)
            norm("norm0", res, lambda e: e.wait_ge(x_in, 16), col("pre_mix_norm"))
            act.wait_ge(bias_copied, 16)
            for r in range(ROWS):
                for h in range(B_H):
                    src = bass.AP(bias_rows.tensor, h * RPB_R * RPB_C + (7 - r) * RPB_C + 15,
                                  [[NB - 1, GRID], [RPB_C, ROWS], [1, GRID]])
                    dst = bm[GRID * (r % 2):GRID * (r % 2) + GRID, r // 2, h].rearrange("p (a b) -> p a b", a=ROWS)
                    act.dma_start(dst, src).then_inc(bias_in, 16)

            p0, g0 = plan["in"]
            with act.Fori(0, 4) as i:
                for c in range(2):
                    chunk(i * 16 + (8 * c + p0), evac_to(proj, i * (2 * NCH) + c * NCH, g0 + c))
            chunk(p0 + 64, evac_to(proj, 8 * NCH, g0 + 8))

            act.wait_ge(pe_done, plan["o"][0])
            act.dma_start(gqk[:, 0:A_Q * HD].rearrange("p (h d) -> p h d", d=HD),
                          bass.AP(I["q_norm"].tensor, 0, [[0, P], [0, A_Q], [1, HD]])).then_inc(gqk_in, 16)
            act.dma_start(gqk[:, A_Q * HD:].rearrange("p (h d) -> p h d", d=HD),
                          bass.AP(I["k_norm"].tensor, 0, [[0, P], [0, A_KV], [1, HD]])).then_inc(gqk_in, 16)
            t0 = TG["attention"][0]

            def turn_out(g):
                act.wait_ge(t_done, t0 + g + 1)
                nc.scalar.activation(qkT[:, 2 * g:2 * g + 2], ps[:, TB[(t0 + g) % 2]].rearrange("p (a b) -> p a b", a=2), ACT.Copy)\
                    .then_inc(t_free, 1)

            def softmax_exp(i):
                act.wait_ge(mx_done, i + 1)
                for th in range(TH):
                    if i < B_H:
                        src, sc = prob[:, i % 2, th], 1.0
                    else:
                        src, sc = ps[:, i % 2, th * T:(th + 1) * T], SCALE
                        if th == 0 and i >= 2:
                            act.wait_ge(pt_done, i - 1)
                    k = 2 * (i % 2) + th
                    ins = nc.scalar.activation(prob[:, i % 2, th], src, ACT.Exp, bias=stat[:, 32 + k:33 + k], scale=sc,
                                               accum_out=stat[:, 36 + k:37 + k])
                ins.then_inc(exp_done, 1)

            def prob_copy(i):
                act.wait_ge(pt_done, i + 1)
                if i >= 2:
                    act.wait_ge(o_done, i - 1)
                nc.scalar.activation(probT[i % 2][:], ps[:, 2 + i % 2].rearrange("p (a b) -> p a b", a=TH), ACT.Copy)\
                    .then_inc(pt_copied, 1)

            def out_hi(i):
                act.wait_ge(o_done, i + 1)
                nc.scalar.activation(xhi[:, HEAD_KT[i]], ps[:, 6 + i % 2, 0:T], ACT.Copy).then_inc(o_hi, 1)

            for g in range(8):
                turn_out(g)
            for i in range(NHEAD + 2):
                if i == B_H:
                    for g in range(8, 13):
                        turn_out(g)
                if 1 <= i <= NHEAD:
                    prob_copy(i - 1)
                if i < NHEAD:
                    softmax_exp(i)
                if i >= 2:
                    out_hi(i - 2)

            p0, g0 = plan["o"]
            with act.Fori(0, 2) as i:
                for c in range(2):
                    chunk(i * 16 + (8 * c + p0), evac_to(yrow, i * (2 * NCH) + c * NCH, g0 + c))
            postnorm("post0", yrow, lambda e: e.wait_ge(acc_free, plan["mlp1"][1] + 2), I["post_mix_norm"][0])
            norm("norm1", res, lambda e: e.wait_ge(S["res", "post0"], 2), col("pre_mlp_norm"))

            def mlp(i, k, u0):
                p0, g0 = plan[k]
                seq, t0 = SEQ, TG[k][0]
                for j, (kind, c) in enumerate(seq):
                    def turned(c=seq[j - 1][1]):
                        for h in range(2):
                            act.wait_ge(t_done, i * 8 + (t0 + 2 * c + h + 1))
                            nc.scalar.activation(hhi[:, 4 * c + 2 * h:4 * c + 2 * h + 2],
                                                 ps[:, TB[(t0 + h) % 2]].rearrange("p (a b) -> p a b", a=2), ACT.Copy)\
                                .then_inc(t_hi, 1)

                    def relu(c=c, j=j):
                        act.wait_ge(sq_done, i * 8 + (2 * (u0 + c) + 2))
                        for th in range(TH):
                            ins = nc.scalar.activation(rrow[:, th], ps[:, bank(g0 + j) + th], ACT.Relu)
                        ins.then_inc(acc_free, 1)
                    chunk(i * (8 * len(seq)) + (p0 + 8 * j), relu if kind == "U" else None,
                          extra={5: turned} if j and seq[j - 1][0] == "U" else {})

            with act.Fori(0, NSB) as i:
                mlp(i, "mlp1", 0)
            postnorm("post1", yrow, lambda e: e.wait_ge(acc_free, plan["gate"][1] + 2), I["post_mlp_norm"][0])
            act.wait_ge(m_mul, mod_ops(0, "mlp2", -1))
            act.dma_start(prow[:], rows_of(I["p"][0, 0])).then_inc(p_in, 16)
            norm("norm2", res, lambda e: e.wait_ge(S["res", "post1"], 2), col("pre_ple_norm"))
            t0 = TG["ple"][0]
            act.wait_ge(t_done, t0 + 1)
            nc.scalar.activation(hhi[:, 0:2], ps[:, TB[t0 % 2]].rearrange("p (a b) -> p a b", a=2), ACT.Copy).then_inc(t_hi, 1)
            p0, g0 = plan["gate"]
            with act.Fori(0, 2) as i:
                for c in range(2):
                    chunk(i * 16 + (8 * c + p0), evac_to(grow, i * (2 * NCH) + c * NCH, g0 + c, ACT.Sigmoid))
            for c in range(4):
                chunk(plan["ple"][0] + c, n=1, s=c)
            postnorm("post2", yrow, lambda e: e.wait_ge(acc_free, plan["ctx"][1] + 2), I["post_ple_norm"][0])

            act.wait_ge(S["res", "post2"], 2)
            act.dma_start(yrow[:], rows_of(I["ctx_2"][0])).then_inc(ctx_in, 16)
            act.dma_start(lg[:].rearrange("p a b c -> p (a b c)"),
                          I["hgrn_lb_logits_2"].rearrange("a b c -> (a b c)").partition_broadcast(P)).then_inc(lg_in, 16)
            act.dma_start(sums[:].rearrange("p a b -> p (a b)"), I["k_sums"]).then_inc(sums_in, 16)

            def norm_mod(k, src, wait_src):
                wait_src(act)
                nc.scalar.activation(xs[:, 0], src[:, 0], ACT.Square, accum_out=stat[:, 0:1]).then_inc(ss_done, 1)
                act.wait_ge(rstd_done, RMS[k] + 1)
                nc.scalar.activation(xs[:, 0], src[:, 0], ACT.Copy, scale=stat[:, 8:9]).then_inc(S["xs", k], 1)
                t0, h0 = TG[k]
                for g in range(KT // 2):
                    act.wait_ge(t_free, t0 + g + 1)
                    nc.scalar.activation(xhi[:, 2 * g:2 * g + 2], tcol[:, g % 2], ACT.Copy).then_inc(t_hi, 1)

            norm_mod("normc", yrow, lambda e: e.wait_ge(ctx_in, 16))
            p0, g0 = plan["ctx"]

            def lb_exps():
                act.wait_ge(lb_diff, 2)
                nc.scalar.activation(lg[:], lg[:], ACT.Exp).then_inc(lb_exp, 1)
            for c in range(6):
                chunk(p0 + 8 * c, evac_to(pctx[:, c // 2], c % 2 * NCH, g0 + c, *((ACT.Copy, 1.0) if c < 2 else (ACT.Exp, -1.0))),
                      extra={5: lb_exps} if c == 0 else {})
            act.wait_ge(ctx_f, 4)
            for d in range(2):
                nc.scalar.activation(lfc[:, d], pctx[:, 1 + d], ACT.Ln).then_inc(ctx_ln, 1)
            for n in range(4):
                act.wait_ge(cs_done, n + 1)
                nc.scalar.activation(dctx[:, n // 2, :, n % 2 * NCH:(n % 2 + 1) * NCH], ps[:, bank(n):bank(n) + 2], ACT.Exp)\
                    .then_inc(cs_exp, 1)
            for n in range(4):
                act.wait_ge(st_done, n + 1)
                nc.scalar.activation(S0[:, n // 2, n % 2 * NCH:(n % 2 + 1) * NCH], ps[:, 6 + n % 2], ACT.Copy).then_inc(st_out, 1)

            norm_mod("norm3", res, lambda e: e.wait_ge(st_out, 4))
            act.wait_ge(S["xs", "norm3"], 2)
            act.dma_start(scratch, res[:]).then_inc(spill, 16)
            act.wait_ge(lb_done, 1)
            act.dma_start(mask_rows[:].rearrange("p a b -> p (a b)"), I["k_masks"]).then_inc(masks_in, 16)
            p0, g0 = plan["x2"]

            def sig_only(dst, col, g):
                def f():
                    for th in range(TH):
                        ins = nc.scalar.activation(dst[:, th, col:col + NCH], ps[:, bank(g) + th], ACT.Sigmoid)
                    ins.then_inc(sig_done, 1)
                return f
            for c in range(14):
                col_, g = c % 2 * NCH, g0 + c
                if c < 2:
                    f = evac_to(rows5[:, RV], col_, g)
                elif c < 6:
                    f = evac_to(rows5[:, RF + (c - 2) // 2], col_, g, ACT.Exp, -1.0)
                elif c < 10:
                    f = sig_only(rows5[:, RQ + (c - 6) // 2], col_, g)
                elif c < 12:
                    if c == 10:
                        act.wait_ge(spill, 16)
                    f = evac_to(urow, col_, g)
                else:
                    f = evac_to(cgrow, col_, g, ACT.Sigmoid)
                chunk(p0 + 8 * c, f)
            t0 = TG["u"][0]
            for g in range(4):
                act.wait_ge(t_done, t0 + g + 1)
                nc.scalar.activation(uT[:, 2 * g:2 * g + 2], ps[:, TB[(t0 + g) % 2]].rearrange("p (a b) -> p a b", a=2), ACT.Copy)\
                    .then_inc(t_free, 1)

            wcol = lambda tap, ct: cols[:, COL["conv_dw_w_2a"] + tap * HH + ct:COL["conv_dw_w_2a"] + tap * HH + ct + 1]
            act.wait_ge(t_free, t0 + 4)
            for ct in range(HH):
                ins = nc.scalar.activation(yT[:, ct], uT[:, ct], ACT.Identity, scale=wcol(TAPS // 2, ct),
                                           bias=cols[:, COL["conv_dw_b_2"] + ct:COL["conv_dw_b_2"] + ct + 1])
            ins.then_inc(tap_done, 1)
            sent = [0]

            def conv(count):
                for n in range(sent[0], min(sent[0] + count, len(TAP_UNITS))):
                    ct, dd = TAP_UNITS[n]
                    if n >= 2:
                        act.wait_ge(conv_done, n - 1)
                    for k in range(2):
                        ins = nc.scalar.activation(tap_part(tcol[:, n % 2, k], ct, dd, False),
                                                   tap_part(uT[:, ct + k], ct, dd, True), ACT.Copy,
                                                   scale=wcol(TAPS // 2 + dd, ct + k))
                    ins.then_inc(tap_done, 1)
                    sent[0] = n + 1

            def exp_unit(n):
                kind, d, m, pair, ne, ns = UNITS[n]
                if ne is None:
                    return
                act.wait_ge(e_done, ne + 1)
                if n >= 2:
                    act.wait_ge(qk_done, n - 1)
                nc.scalar.activation(dec[:, n % 2], ps[:, ne % 2].rearrange("p (a b) -> p a b", a=2), ACT.Exp).then_inc(d_done, 1)

            for hg in range(2):
                cs = slice(hg * GW, (hg + 1) * GW)
                if hg == 0:
                    act.wait_ge(x_f, 4)
                    act.wait_ge(t_done, t0 + 4)
                else:
                    act.wait_ge(e_done, N_E[2 * PER])
                for d in range(2):
                    nc.scalar.activation(lf[:, d], rows5[:, RF + d, :, cs], ACT.Ln).then_inc(lf_done, 1)
                if hg:
                    act.wait_ge(on_done, 2)
                act.dma_start(ngain[:], I["hgrn_norm_g_2"][0, cs].partition_broadcast(P)).then_inc(ng_in, 16)
                t0 = TG["qk%d" % hg][0]
                if hg:
                    act.wait_ge(qk_done, 2 * PER)
                    act.wait_ge(s_done, N_S[2 * PER])
                for g in range(6):
                    act.wait_ge(t_done, t0 + g + 1)
                    dst = (qT, kfT, kbT)[g // 2]
                    nc.scalar.activation(dst[:, g % 2 * 2:g % 2 * 2 + 2], ps[:, TB[(t0 + g) % 2]].rearrange("p (a b) -> p a b", a=2),
                                         ACT.Copy).then_inc(t_free, 1)
                for pair in (2 * hg, 2 * hg + 1):
                    for n in range(pair * PER, (pair + 1) * PER):
                        exp_unit(n)
                        conv(1)
                    act.wait_ge(o2_done, pair + 1)
                    nc.scalar.activation(rows5[:, RQ, :, pair * 2 * HD:(pair + 1) * 2 * HD],
                                         ps[:, 6 + pair % 2].rearrange("p (a b) -> p a b", a=TH), ACT.Copy).then_inc(oc_done, 1)

            g1, b1 = (col(x, HH) for x in ("conv_ln_g_2", "conv_ln_b_2"))

            def ln_means():
                act.wait_ge(ln_sum, 1)
                nc.scalar.activation(lnm[:], ps[:, 6, 0:T], ACT.Copy, scale=1.0 / DH).then_inc(ln_mean, 1)

            def ln_squares():
                act.wait_ge(ln_cent, 1)
                nc.scalar.activation(ysq[:], yT[:], ACT.Square).then_inc(ln_sq, 1)

            def ln_sigmoids():
                act.wait_ge(ln_norm, 1)
                for c in range(HH):
                    nc.scalar.activation(ysg[:, c], yT[:, c], ACT.Sigmoid, bias=b1[:, c:c + 1], scale=g1[:, c:c + 1]).then_inc(ln_s, 1)

            def ln_affine():
                for c in range(HH):
                    nc.scalar.activation(ysq[:, c], yT[:, c], ACT.Identity, bias=b1[:, c:c + 1], scale=g1[:, c:c + 1]).then_inc(ln_z, 1)

            def ln_high():
                act.wait_ge(ln_u, 1)
                nc.scalar.activation(hhi[:, HH:KT], ysq[:], ACT.Copy).then_inc(c_hi, 1)

            def o2_high(g):
                act.wait_ge(c_lo, 1)
                t0 = TG["o2"][0]
                act.wait_ge(t_done, t0 + g + 1)
                nc.scalar.activation(hhi[:, 2 * g:2 * g + 2], ps[:, TB[(t0 + g) % 2]].rearrange("p (a b) -> p a b", a=2), ACT.Copy)                    .then_inc(t_hi, 1)
            p0, g0 = plan["gc"]
            extras = [{4: ln_means, 6: ln_squares}, {6: ln_sigmoids, 7: ln_affine}, {2: ln_high, 6: lambda: o2_high(0), 7: lambda: o2_high(1)},
                      {0: lambda: o2_high(2), 1: lambda: o2_high(3)}]
            for c in range(4):
                chunk(p0 + 8 * c, evac_to(yrow, c * NCH, g0 + c, ACT.Sigmoid), extra=extras[c])

            def pairs_of(name, dst, n=8, func=None, last=False):
                p0, g0 = plan[name]
                with act.Fori(0, 2) as i:
                    for c in range(2):
                        chunk(i * (2 * n) + (n * c + p0), func and evac_to(dst, i * (2 * NCH) + c * NCH, g0 + c, func), n=n)
            pairs_of("pw", None, n=4)
            pairs_of("gh", grow, func=ACT.Sigmoid)
            pairs_of("ho", None, n=4)
            act.wait_ge(on_done, 4)
            act.dma_start(res[:], scratch).then_inc(reload, 16)
            t0, h0 = TG["y"]
            for g in range(8):
                act.wait_ge(t_done, t0 + g + 1)
                nc.scalar.activation(xhi[:, 2 * g:2 * g + 2], ps[:, TB[(t0 + g) % 2]].rearrange("p (a b) -> p a b", a=2), ACT.Copy)\
                    .then_inc(t_hi, 1)
            pairs_of("wo2", yrow, func=ACT.Copy)

            def postnorm_gated(k, n, row, wait_row):
                wait_row(act)
                nc.scalar.activation(xs[:, 0], row[:, 0], ACT.Square, accum_out=stat[:, 0:1]).then_inc(ss_done, 1)
                act.wait_ge(gb_done, n + 1)
                nc.scalar.activation(gbc[:], ps[:, 0:4].rearrange("p a b -> p (a b)"), ACT.Copy).then_inc(S["gain", k], 16)

            act.wait_ge(reload, 16)
            postnorm_gated("post3", 0, yrow, lambda e: e.wait_ge(acc_free, plan["mlp2"][1] + 2))
            norm_mod("norm4", res, lambda e: e.wait_ge(S["res", "post3"], 2))
            with act.Fori(0, NSB) as i:
                mlp(i, "mlp2", 16)
            postnorm_gated("post4", 1, yrow, lambda e: e.wait_ge(acc_free, plan["end"][1] + 2))
            for th in range(TH):
                act.wait_ge(S["res", "post4"], 2)
                act.dma_start(rows_of(out[0])[:, th], res[:, th]).then_inc(out_done, 16)
            act.wait_ge(out_done, 32)

        @block.tensor
        def _(pe):
            def turn(t, parts):
                if t >= 2:
                    pe.wait_ge(t_free, t - 1)
                for c, src in parts:
                    ins = nc.tensor.transpose(ps[:, TB[t % 2], c:c + P], src, ident)
                ins.then_inc(t_done, 1)

            def norm(k):
                pe.wait_ge(S["xs", k], 2)
                for g in range(KT // 2):
                    turn(TG[k][0] + g, [(j * T + th * P, xs[:, th, (2 * g + j) * P:(2 * g + j + 1) * P])
                                        for j in range(2) for th in range(TH)])

            def chunk(p, g, hi, lo, n=8, s=0, par=None, inserts=None, before=None):
                par = g if par is None else par
                pe.wait_ge(acc_free, g + 1)
                for u in range(n):
                    if inserts and u in inserts:
                        inserts[u]()
                    pe.wait_ge(lo_done, p + (u + 1))
                    for th in range(TH):
                        for k in range(2):
                            kt = 2 * u + k
                            for m, (a, b) in enumerate(((hi, whi), (hi, wlo), (lo, whi))):
                                ins = nc.tensor.matmul(ps[:, bank(par) + th], a[:, kt, th * P:(th + 1) * P],
                                                       b[:, (s + u) % NSLOT, k], start=(kt == 0 and m == 0),
                                                       stop=(kt == 2 * n - 1 and m == 2))
                    ins.then_inc(pe_done, 1)

            pe.wait_ge(small_in, 16)
            pe.wait_ge(vec_in, 16 * sum(len(g) for g in VEC_GROUPS))
            c = 0
            for gi, group in enumerate(VEC_GROUPS):
                rows = sum(n for _, n in group)
                ins = nc.tensor.transpose(ps[:, MB, c:c + rows], vecs[0:rows, gi, :], ident[0:rows, 0:rows])
                c += rows
            ins.then_inc(vec_turned, 1)

            norm("norm0")
            pe.wait_ge(t_free, 8)
            p0, g0 = plan["in"]
            with pe.Fori(0, 4) as i:
                for c in range(2):
                    chunk(i * 16 + (8 * c + p0), i * 2 + (g0 + c), xhi, xlo, par=g0 + c)
            chunk(p0 + 64, g0 + 8, xhi, xlo)

            pe.wait_ge(acc_free, plan["o"][1] + 2)
            o_q, o_k = (A_Q + 2 * A_KV) * HD, (A_Q + 2 * A_KV + B_H) * HD
            o_v = o_k + B_H * HD
            t0 = TG["attention"][0]

            def turn_heads(g, a, b):
                turn(t0 + g, [(j * T + th * P, proj[:, th, c:c + HD]) for j, c in enumerate((a, b)) for th in range(TH)])

            def scores(i):
                if i >= 2:
                    pe.wait_ge(sc_free if i - 2 < B_H else exp_done, i - 1)
                q, k = (2 * i, 2 * i + 1) if i < B_H else (16 + i - B_H, 16 + A_Q + (i - B_H) // (A_Q // A_KV))
                for th in range(TH):
                    ins = nc.tensor.matmul(ps[:, i % 2, th * T:(th + 1) * T], qkT[:, q, th * P:(th + 1) * P], qkT[:, k],
                                           start=True, stop=True)
                ins.then_inc(sc_done, 1)

            def prob_turn(i):
                pe.wait_ge(p_done, i + 1)
                if i >= 2:
                    pe.wait_ge(pt_copied, i - 1)
                for kt in range(TH):
                    for th in range(TH):
                        ins = nc.tensor.transpose(ps[:, 2 + i % 2, kt * T + th * P:kt * T + (th + 1) * P],
                                                  prob[:, i % 2, th, kt * P:(kt + 1) * P], ident)
                ins.then_inc(pt_done, 1)

            def values(i):
                pe.wait_ge(pt_copied, i + 1)
                if i >= 2:
                    pe.wait_ge(o_lo, i - 1)
                c = o_v + i * HD if i < B_H else (A_Q + A_KV + (i - B_H) // (A_Q // A_KV)) * HD
                for kt in range(TH):
                    ins = nc.tensor.matmul(ps[:, 6 + i % 2, 0:T], proj[:, kt, c:c + HD], probT[i % 2][:, kt],
                                           start=kt == 0, stop=kt == TH - 1)
                ins.then_inc(o_done, 1)

            for h in range(B_H):
                turn_heads(h, o_q + h * HD, o_k + h * HD)
            pe.wait_ge(t_free, t0 + 8)
            for i in range(NHEAD + 2):
                if i == B_H:
                    pe.wait_ge(rope_done, 4)
                    for g in range(NA // 2):
                        turn_heads(8 + g, 2 * g * HD, (2 * g + 1) * HD)
                    pe.wait_ge(t_free, t0 + 13)
                if i < NHEAD:
                    scores(i)
                if 1 <= i <= NHEAD:
                    prob_turn(i - 1)
                if i >= 2:
                    values(i - 2)
            pe.wait_ge(o_lo, NHEAD)

            p0, g0 = plan["o"]
            with pe.Fori(0, 2) as i:
                for c in range(2):
                    chunk(i * 16 + (8 * c + p0), i * 2 + (g0 + c), xhi, xlo, par=g0 + c)
            norm("norm1")
            pe.wait_ge(t_free, TG["mlp1"][0])

            def mlp(i, k, u0):
                p0, g0 = plan[k]
                seq, t0 = SEQ, TG[k][0]
                for j, (kind, c) in enumerate(seq):
                    def turn_hidden(c=seq[j - 1][1]):
                        pe.wait_ge(sq_done, i * 8 + (2 * (u0 + c) + 4))
                        for h in range(2):
                            pe.wait_ge(t_free, i * 8 + (t0 + 2 * c + h - 1))
                            for a in range(2):
                                for th in range(TH):
                                    f = (2 * h + a) * P
                                    ins = nc.tensor.transpose(ps[:, TB[(t0 + h) % 2], a * T + th * P:a * T + (th + 1) * P],
                                                              sqrow[:, th, f:f + P], ident)
                            ins.then_inc(t_done, 1)

                    def mod_sum(m):
                        pe.wait_ge(m_mul, mod_ops(i, k, 8 * m + 7))
                        n = mod_chunk_of(i, k, m)
                        for v in range(2 if k == "mlp1" and m < MCTX else 1):
                            for b in range(4):
                                ins = nc.tensor.matmul(ps[:, MB, bass.ds(n * 8 + (2 * b + v), 1)], macc[:, v, m % 3, b * P:(b + 1) * P],
                                                       ones[:, 0:1], start=True, stop=True)
                        ins.then_inc(m_red, 1)

                    def hidden_ready(c=c):
                        pe.wait_ge(t_free, i * 8 + (t0 + 8))
                    prev = seq[j - 1][0] if j else None
                    inserts = {3: turn_hidden} if prev == "U" else {}
                    if kind == "D" and c == 0:
                        inserts[5] = hidden_ready
                    for r in range(len(MAT[k][j])):
                        q = j * len(MAT[k][j]) + r
                        if q % 8 == 7:
                            inserts[7] = lambda m=q // 8: mod_sum(m)
                    p = i * (8 * len(seq)) + (p0 + 8 * j)
                    g = i * len(seq) + (g0 + j)
                    st = (xhi, xlo) if kind == "U" else (hhi, hlo)
                    chunk(p, g, *st, par=g0 + j, inserts=inserts)

            with pe.Fori(0, NSB) as i:
                mlp(i, "mlp1", 0)
            norm("norm2")
            pe.wait_ge(p_in, 16)
            turn(TG["ple"][0], [(j * T + th * P, prow[:, th, j * P:(j + 1) * P]) for j in range(2) for th in range(TH)])
            pe.wait_ge(t_free, TG["ple"][0] + 1)
            p0, g0 = plan["gate"]
            with pe.Fori(0, 2) as i:
                for c in range(2):
                    chunk(i * 16 + (8 * c + p0), i * 2 + (g0 + c), xhi, xlo, par=g0 + c)
            p0, g0 = plan["ple"]
            for c in range(4):
                chunk(p0 + c, g0 + c, hhi, hlo, n=1, s=c)

            norm("normc")
            pe.wait_ge(x_lo, 8)

            def straight(name, chunks, n=8, st=(xhi, xlo)):
                p0, g0 = plan[name]
                for c in range(chunks):
                    chunk(p0 + n * c, g0 + c, *st, n=n)

            def looped(name, pairs, n=8, st=(xhi, xlo)):
                p0, g0 = plan[name]
                with pe.Fori(0, pairs) as i:
                    for c in range(2):
                        chunk(i * (2 * n) + (n * c + p0), i * 2 + (g0 + c), *st, n=n, par=g0 + c)
            looped("ctx", 3)
            pe.wait_ge(acc_free, plan["x2"][1] + 2)
            pe.wait_ge(sums_in, 16)
            for n in range(4):
                d, cs = n // 2, slice(n % 2 * NCH, (n % 2 + 1) * NCH)
                pe.wait_ge(ctx_ln, d + 1)
                if n >= 2:
                    pe.wait_ge(cs_exp, n - 1)
                own = sums[:, SUF_EX if d == 0 else PRE_EX]
                far = 0 if d == 0 else 1
                for th in range(TH):
                    ins = nc.tensor.matmul(ps[:, bank(n) + th], own, lfc[:, d, th, cs], start=True, stop=th != far)
                    if th == far:
                        ins = nc.tensor.matmul(ps[:, bank(n) + th], ones, lfc[:, d, 1 - th, cs], start=False, stop=True)
                ins.then_inc(cs_done, 1)
            for n in range(4):
                d = n // 2
                pe.wait_ge(cs_dec, n + 1)
                if n >= 2:
                    pe.wait_ge(st_out, n - 1)
                for h in range(4):
                    c = (n % 2 * 4 + h) * HD
                    for th in range(TH):
                        ins = nc.tensor.matmul(ps[:, 6 + n % 2, h * HD:(h + 1) * HD], dctx[:, d, th, c:c + HD], pctx[:, 0, th, c:c + HD],
                                               start=th == 0, stop=th == TH - 1)
                ins.then_inc(st_done, 1)
            norm("norm3")
            pe.wait_ge(x_lo, 16)
            looped("x2", 7)

            def turn_pair(t, src, kt):
                turn(t, [(j * T + th * P, src[:, th, (kt + j) * P:(kt + j + 1) * P]) for j in range(2) for th in range(TH)])
            pe.wait_ge(u_done, 2)
            for g in range(4):
                turn_pair(TG["u"][0] + g, urow, 2 * g)

            def sums_unit(n):
                kind, d, m, pair, ne, ns = UNITS[n]
                if ne is None:
                    return
                if ne >= 2:
                    pe.wait_ge(d_done, ne - 1)
                for hh in range(2):
                    c = (pair % 2 * 2 + hh) * HD
                    for th in range(TH):
                        o = ps[:, ne % 2, hh * T + th * P:hh * T + (th + 1) * P]
                        w = lf[:, d, th, c:c + HD]
                        if kind == "level":
                            mat, more = LV[m] + d * len(LEVELS), False
                        elif kind == "cross":
                            mat = (SUF_EX, PRE_IN)[th] if d == 0 else (SUF_IN, PRE_EX)[th]
                            more = False
                        else:
                            mat, more = (PRE_IN, SUF_IN)[d], th != d
                        ins = nc.tensor.matmul(o, w, sums[:, mat], start=True, stop=not more)
                        if more:
                            ins = nc.tensor.matmul(o, lf[:, d, 1 - th, c:c + HD], ones, start=False, stop=True)
                ins.then_inc(e_done, 1)

            def score_unit(n):
                kind, d, m, pair, ne, ns = UNITS[n]
                if ns is None:
                    return
                pe.wait_ge(qk_done, n + 1)
                if ns >= 2:
                    pe.wait_ge(s_free, ns - 1)
                for hh in range(2):
                    if kind == "cross":
                        s, t = (0, 1) if d == 0 else (1, 0)
                        ins = nc.tensor.matmul(ps[:, 2 + ns % 2, hh * P:(hh + 1) * P], kD[:, n % 2, hh, s * P:(s + 1) * P],
                                               qD[:, n % 2, hh, t * P:(t + 1) * P], start=True, stop=True)
                        continue
                    for th in range(TH):
                        q = qT[:, pair % 2 * 2 + hh] if kind == "diag" else qD[:, n % 2, hh]
                        ins = nc.tensor.matmul(ps[:, 2 + ns % 2, (hh * 2 + th) * P:(hh * 2 + th + 1) * P],
                                               kD[:, n % 2, hh, th * P:(th + 1) * P], q[:, th * P:(th + 1) * P],
                                               start=True, stop=True)
                ins.then_inc(s_done, 1)

            def out_pair(pair):
                n = (pair + 1) * PER
                pe.wait_ge(qk_done, n)
                pe.wait_ge(s_free, N_S[n] if n < len(UNITS) else n_s)
                if pair >= 2:
                    pe.wait_ge(oc_done, pair - 1)
                for th in range(TH):
                    for hh in range(2):
                        c = (2 * pair + hh) * HD
                        o = ps[:, 6 + pair % 2, (th * 2 + hh) * HD:(th * 2 + hh + 1) * HD]
                        parts = [(qD[:, (n - 2) % 2, hh, th * P:(th + 1) * P], S0[:, 0, c:c + HD]),
                                 (qD[:, (n - 1) % 2, hh, th * P:(th + 1) * P], S0[:, 1, c:c + HD]),
                                 (sc[:, pair % 2, hh, th], rows5[:, RV, th, c:c + HD]),
                                 (cross[:, pair % 2, hh, 1 - th], rows5[:, RV, 1 - th, c:c + HD])]
                        for k, (w, v) in enumerate(parts):
                            ins = nc.tensor.matmul(o, w, v, start=k == 0, stop=k == 3)
                ins.then_inc(o2_done, 1)

            for hg in range(2):
                t0 = TG["qk%d" % hg][0]
                for g in range(6):
                    if g >= 2:
                        pe.wait_ge(k_done, 2 * hg + g // 2)
                    row = (RQ, RF, RF + 1)[g // 2]
                    turn_pair(t0 + g, rows5[:, row], hg * 4 + g % 2 * 2)
                pe.wait_ge(lf_done, 2 * hg + 2)
                pe.wait_ge(t_free, t0 + 6)
                first, last = 2 * hg * PER, 2 * (hg + 1) * PER
                sums_unit(first)
                for n in range(first, last):
                    if n + 1 < last:
                        sums_unit(n + 1)
                    score_unit(n)
                    if (n + 1) % PER == 0:
                        out_pair(n // PER)

            def ln_sums():
                pe.wait_ge(conv_done, len(TAP_UNITS))
                pe.wait_ge(oc_done, 4)
                for c in range(HH):
                    ins = nc.tensor.matmul(ps[:, 6, 0:T], ones, yT[:, c], start=c == 0, stop=c == HH - 1)
                ins.then_inc(ln_sum, 1)

            def ln_variance():
                pe.wait_ge(ln_sq, 1)
                for th in range(TH):
                    for c in range(HH):
                        ins = nc.tensor.matmul(ps[:, 7, th:th + 1], ysq[:, c, th * P:(th + 1) * P], ones[:, 0:1],
                                               start=c == 0, stop=c == HH - 1)
                ins.then_inc(ln_var, 1)

            def ln_spread():
                pe.wait_ge(ln_pow, 1)
                for th in range(TH):
                    ins = nc.tensor.matmul(ps[:, 7, th * P:(th + 1) * P], stat[:, 50 + th:51 + th].to_broadcast([P, P]), ident,
                                           start=True, stop=True)
                ins.then_inc(ln_rows, 1)

            def o2_turn(g):
                pe.wait_ge(on_done, 4)
                turn_pair(TG["o2"][0] + g, rows5[:, RQ], 2 * g)
            p0, g0 = plan["gc"]
            inserts = [{3: ln_sums}, {0: ln_variance, 4: ln_spread}, {5: lambda: o2_turn(0), 6: lambda: o2_turn(1),
                       7: lambda: o2_turn(2)}, {0: lambda: o2_turn(3)}]
            for c in range(4):
                chunk(p0 + 8 * c, g0 + c, xhi, xlo, inserts=inserts[c])
            pe.wait_ge(c_lo, 1)
            looped("pw", 2, n=4, st=(hhi[:, HH:KT], hlo[:, HH:KT]))
            looped("gh", 2)
            pe.wait_ge(t_free, TG["o2"][0] + 4)
            looped("ho", 2, n=4, st=(hhi, hlo))
            pe.wait_ge(merged, 4)
            for g in range(8):
                turn_pair(TG["y"][0] + g, yrow, 2 * g)
            pe.wait_ge(t_free, TG["y"][0] + 8)
            looped("wo2", 2)

            def gate_rows(k, g_end):
                pe.wait_ge(mcol_done, k + 1)
                pe.wait_ge(acc_free, g_end + 2)
                for kt in range(KT):
                    ins = nc.tensor.matmul(ps[:, kt // 4, kt % 4 * P:(kt % 4 + 1) * P], mcol[:, k, kt:kt + 1].to_broadcast([P, P]),
                                           ident, start=True, stop=True)
                ins.then_inc(gb_done, 1)
            gate_rows(3, plan["mlp2"][1])
            norm("norm4")
            pe.wait_ge(x_lo, 24)
            with pe.Fori(0, NSB) as i:
                mlp(i, "mlp2", 16)
            gate_rows(4, plan["end"][1])

        @block.vector
        def _(dve):
            steps = [0]

            def step(ins):
                steps[0] += 1
                ins.then_inc(dve_step, 1)
                dve.wait_ge(dve_step, steps[0])

            def split(p, s):
                if isinstance(p, int) and p >= n_pieces:
                    return
                dve.wait_ge(hi_done, p + 1)
                nc.vector.tensor_tensor(wlo[:, s % NSLOT], raw[:, s % NSLOT], whi[:, s % NSLOT].bitcast(F32), ALU.subtract)\
                    .then_inc(lo_done, 1)

            def chunk(p, evac=None, n=8, s=0, extra=()):
                for u in range(n):
                    if u in extra:
                        extra[u]()
                    split(p + (3 + u), s + 3 + u)
                if evac:
                    dve.wait_ge(pe_done, p + n)
                    evac()

            def mean_square(k, src, wait_src):
                wait_src(dve)
                nc.vector.tensor_tensor_reduce(out=xs[:, 1], in0=src[:, 1], in1=src[:, 1], scale=1.0, scalar=0.0,
                                               op0=ALU.mult, op1=ALU.add, accum_out=stat[:, 1:2]).then_inc(ss_done, 1)
                dve.wait_ge(ss_done, 2 * RMS[k] + 2)
                nc.vector.tensor_scalar(stat[:, 4:6], stat[:, 0:2], 1.0 / D, EPS, ALU.mult, ALU.add).then_inc(ms_done, 1)

            def norm(k, src, wait_src, gain):
                mean_square(k, src, wait_src)
                dve.wait_ge(rstd_done, RMS[k] + 1)
                nc.vector.tensor_scalar(xs[:, 1], src[:, 1], stat[:, 9:10], None, ALU.mult).then_inc(S["xs", k], 1)
                t0, h0 = TG[k]
                for g in range(KT // 2):
                    dve.wait_ge(t_hi, h0 + g + 1)
                    for j in range(2):
                        kt = 2 * g + j
                        ins = nc.vector.scalar_tensor_tensor(out=xlo[:, kt], in0=ps[:, TB[(t0 + g) % 2], j * T:(j + 1) * T],
                                                             scalar=gain[:, kt:kt + 1], in1=xhi[:, kt].bitcast(F32),
                                                             op0=ALU.mult, op1=ALU.subtract)
                    ins.then_inc(t_free, 1)

            def postnorm(k, row, wait_row):
                mean_square(k, row, wait_row)
                dve.wait_ge(rstd_done, RMS[k] + 1)
                dve.wait_ge(S["gain", k], 16)
                for th in range(TH):
                    nc.vector.scalar_tensor_tensor(out=xs[:, th], in0=row[:, th], scalar=stat[:, 8 + th:9 + th], in1=gbc[:],
                                                   op0=ALU.mult, op1=ALU.mult).then_inc(S["scaled", k], 1)
                dve.wait_ge(S["scaled", k], 2)
                nc.vector.tensor_tensor(res[:, 1], res[:, 1], xs[:, 1], ALU.add).then_inc(S["res", k], 1)

            for u in range(3):
                split(u, u)
            dve.wait_ge(vec_turned, 1)
            nc.vector.tensor_copy(cols[:], ps[:, MB]).then_inc(vec_cols, 1)
            norm("norm0", res, lambda e: e.wait_ge(x_in, 16), col("pre_mix_norm"))
            p0, g0 = plan["in"]
            with dve.Fori(0, 4) as i:
                for c in range(2):
                    chunk(i * 16 + (8 * c + p0))
            chunk(p0 + 64)

            dve.wait_ge(acc_free, plan["o"][1] + 2)
            dve.wait_ge(gqk_in, 32)
            dve.wait_ge(early_in, 16)
            for n in range(4):
                th, w = n // 2, (n % 2) * SET * HD
                pj = proj[:, th, w:w + SET * HD]
                ra, rb = rota[:, 0], rota[:, 1]
                step(nc.vector.tensor_tensor(ra, pj, pj, ALU.mult))
                step(nc.vector.tensor_reduce(stat[:, 16:16 + SET], ra.rearrange("p (h d) -> p h d", d=HD), AX_X, ALU.add))
                nc.vector.tensor_scalar(stat[:, 16:16 + SET], stat[:, 16:16 + SET], 1.0 / HD, EPS, ALU.mult, ALU.add)\
                    .then_inc(qk_ss, 1)
                dve.wait_ge(qk_rstd, n + 1)
                h3 = pj.rearrange("p (h d) -> p h d", d=HD)
                step(nc.vector.tensor_tensor(h3, h3, stat[:, 24:24 + SET].unsqueeze(2).to_broadcast([P, SET, HD]), ALU.mult))
                step(nc.vector.tensor_tensor(pj, pj, gqk[:, w:w + SET * HD], ALU.mult))
                nc.vector.tensor_tensor(ra.rearrange("p (h d) -> p h d", d=HD), h3,
                                        rope[:, 0, th].unsqueeze(1).to_broadcast([P, SET, HD]), ALU.mult)
                h4 = pj.rearrange("p (h b s c) -> p h b s c", b=2, s=2, c=HD // 4)
                r4 = rb.rearrange("p (h b s c) -> p h b s c", b=2, s=2, c=HD // 4)
                s4 = rope[:, 1, th].rearrange("p (b s c) -> p b s c", b=2, s=2)
                for s in range(2):
                    ins = nc.vector.tensor_tensor(r4[:, :, :, s], h4[:, :, :, 1 - s],
                                                  s4[:, :, s].unsqueeze(1).to_broadcast([P, SET, 2, HD // 4]), ALU.mult)
                step(ins)
                nc.vector.tensor_tensor(pj, ra, rb, ALU.add).then_inc(rope_done, 1)
                dve.wait_ge(rope_done, n + 1)

            def score_max(i):
                dve.wait_ge(sc_done, i + 1)
                k = 32 + 2 * (i % 2)
                if i < B_H:
                    if i >= 2:
                        dve.wait_ge(pt_done, i - 1)
                    ins = nc.vector.scalar_tensor_tensor(out=prob[:, i % 2], in0=ps[:, i % 2].rearrange("p (a b) -> p a b", a=TH),
                                                         scalar=SCALE, in1=bm[:, :, i], op0=ALU.mult, op1=ALU.add)
                    ins.then_inc(sc_free, 1)
                    dve.wait_ge(sc_free, i + 1)
                    step(nc.vector.tensor_reduce(stat[:, k:k + 2], prob[:, i % 2], AX_X, ALU.max))
                    s = -1.0
                else:
                    step(nc.vector.tensor_reduce(stat[:, k:k + 2], ps[:, i % 2].rearrange("p (a b) -> p a b", a=TH), AX_X, ALU.max))
                    s = -SCALE
                nc.vector.tensor_scalar(stat[:, k:k + 2], stat[:, k:k + 2], s, None, ALU.mult).then_inc(mx_done, 1)

            def normalise(i):
                dve.wait_ge(exp_done, i + 1)
                k = 36 + 2 * (i % 2)
                step(nc.vector.reciprocal(stat[:, k:k + 2], stat[:, k:k + 2]))
                for th in range(TH):
                    ins = nc.vector.tensor_scalar(prob[:, i % 2, th], prob[:, i % 2, th], stat[:, k + th:k + th + 1], None, ALU.mult)
                ins.then_inc(p_done, 1)

            def out_lo(i):
                dve.wait_ge(o_hi, i + 1)
                nc.vector.tensor_tensor(xlo[:, HEAD_KT[i]], ps[:, 6 + i % 2, 0:T], xhi[:, HEAD_KT[i]].bitcast(F32), ALU.subtract)\
                    .then_inc(o_lo, 1)

            dve.wait_ge(bias_done, 1)
            for i in range(NHEAD + 3):
                if 1 <= i <= NHEAD:
                    normalise(i - 1)
                if i < NHEAD:
                    score_max(i)
                if i >= 3:
                    out_lo(i - 3)

            p0, g0 = plan["o"]
            with dve.Fori(0, 2) as i:
                for c in range(2):
                    chunk(i * 16 + (8 * c + p0))
            dve.wait_ge(c_exp, 1)
            cc, ce = cols[:, COL["c_2"]:COL["c_2"] + 32], stat[:, 64:96]
            step(nc.vector.tensor_scalar(ce, ce, 1.0, None, ALU.add))
            step(nc.vector.reciprocal(ce, ce))
            nc.vector.tensor_tensor(ce, ce, cc, ALU.mult).then_inc(silu_done, 1)
            dve.wait_ge(silu_done, 1)

            postnorm("post0", yrow, lambda e: e.wait_ge(acc_free, plan["mlp1"][1] + 2))
            norm("norm1", res, lambda e: e.wait_ge(S["res", "post0"], 2), col("pre_mlp_norm"))
            dve.wait_ge(macc_clear, 1)

            def mod_product(i, k, q):
                dve.wait_ge(m_landed[q % MSLOT], i * (32 * MPER[k]) + (32 * M0[k] + 4 * q + 16 - 4 * (q % MSLOT)))
                if q % 8 == 0:
                    dve.wait_ge(m_red, i * MPER[k] + (M0[k] + q // 8 + (1 if k == "mlp1" else 2)))
                vs = range(2 if k == "mlp1" and q < 8 * MCTX else 1)
                for h in range(2):
                    kt = 2 * (q % 8) + h
                    for v in vs:
                        dve.wait_ge(m_mul, mod_ops(i, k, q - 1) + (len(vs) * (h - 1) + v + 1))
                        a, w, x = macc[:, v, q // 8 % 3], mraw[:, q % MSLOT, h], stat[:, 64 + 16 * v + kt:65 + 16 * v + kt]
                        if kt == 0:
                            ins = nc.vector.tensor_scalar(a, w, x, None, ALU.mult)
                        else:
                            ins = nc.vector.scalar_tensor_tensor(out=a, in0=w, scalar=x, in1=a, op0=ALU.mult, op1=ALU.add)
                        ins.then_inc(m_mul, 1)

            def mlp(i, k):
                p0, g0 = plan[k]
                seq, (t0, h0) = SEQ, TG[k]
                for j, (kind, c) in enumerate(seq):
                    def turned(c=seq[j - 1][1]):
                        for h in range(2):
                            dve.wait_ge(t_hi, i * 8 + (h0 + 2 * c + h + 1))
                            kt = 4 * c + 2 * h
                            nc.vector.tensor_tensor(hlo[:, kt:kt + 2], ps[:, TB[(t0 + h) % 2]].rearrange("p (a b) -> p a b", a=2),
                                                    hhi[:, kt:kt + 2].bitcast(F32), ALU.subtract).then_inc(t_free, 1)

                    def down(c=c, j=j):
                        for th in range(TH):
                            y = yrow[:, th, c * NCH:(c + 1) * NCH]
                            ins = nc.vector.tensor_tensor(y, ps[:, bank(g0 + j) + th], y, ALU.add)
                        ins.then_inc(acc_free, 1)
                    prev = seq[j - 1][0] if j else None
                    chunk(i * (8 * len(seq)) + (p0 + 8 * j), down if kind == "D" else None,
                          extra={**mod_extra(k, j, lambda q: mod_product(i, k, q)), **({TURN_U: turned} if prev == "U" else {})})

            with dve.Fori(0, NSB) as i:
                mlp(i, "mlp1")
            postnorm("post1", yrow, lambda e: e.wait_ge(acc_free, plan["gate"][1] + 2))
            dve.wait_ge(m_red, MPER["mlp1"] * NSB + 2)
            mps = ps[:, MB, 0:8 * N_MCH].rearrange("p (a b) -> p a b", b=2)
            NM, NX = 5 * KT, 2 * KT
            bmod = col("b_mod_2", NMOD * KT)
            nc.vector.tensor_tensor(modT[:, 0:NM, 0], mps[:, 0:NM, 0], bmod[:, 0:NM], ALU.add)
            nc.vector.tensor_tensor(modT[:, 0:NX, 1], mps[:, 0:NX, 1], bmod[:, 0:NX], ALU.add).then_inc(mod_out, 1)
            norm("norm2", res, lambda e: e.wait_ge(S["res", "post1"], 2), col("pre_ple_norm"))
            t0, h0 = TG["ple"]
            dve.wait_ge(t_hi, h0 + 1)
            nc.vector.tensor_tensor(hlo[:, 0:2], ps[:, TB[t0 % 2]].rearrange("p (a b) -> p a b", a=2),
                                    hhi[:, 0:2].bitcast(F32), ALU.subtract).then_inc(t_free, 1)
            p0, g0 = plan["gate"]
            with dve.Fori(0, 2) as i:
                for c in range(2):
                    chunk(i * 16 + (8 * c + p0))
            dve.wait_ge(acc_free, plan["ple"][1] + 2)
            p0, g0 = plan["ple"]
            for c in range(4):
                def gated(c=c):
                    for th in range(TH):
                        y = slice(c * NCH, (c + 1) * NCH)
                        ins = nc.vector.tensor_tensor(yrow[:, th, y], ps[:, bank(g0 + c) + th], grow[:, th, y], ALU.mult)
                    ins.then_inc(acc_free, 1)
                chunk(p0 + c, gated, n=1, s=c)
            postnorm("post2", yrow, lambda e: e.wait_ge(acc_free, plan["ctx"][1] + 2))

            dve.wait_ge(mod_out, 1)
            for n, (part, c, gain) in enumerate(((1, 0, "norm_pre_mix_2"), (1, 1, "norm_pre_mix_2"), (4, 0, "norm_pre_mlp_2"))):
                nc.vector.scalar_tensor_tensor(out=mcol[:, n], in0=modT[:, part * KT:(part + 1) * KT, c], scalar=1.0, in1=col(gain),
                                               op0=ALU.add, op1=ALU.mult).then_inc(mcol_done, 1)
            nc.vector.tensor_tensor(mcol[:, 3], modT[:, 2 * KT:3 * KT, 0], col("norm_post_mix_2"), ALU.mult).then_inc(mcol_done, 1)
            dve.wait_ge(mcol_done, 4)

            def norm_mod(k, src, wait_src, gain, shift):
                mean_square(k, src, wait_src)
                dve.wait_ge(rstd_done, RMS[k] + 1)
                nc.vector.tensor_scalar(xs[:, 1], src[:, 1], stat[:, 9:10], None, ALU.mult).then_inc(S["xs", k], 1)
                t0, h0 = TG[k]

                def low(g):
                    dve.wait_ge(t_hi, h0 + g + 1)
                    nc.vector.tensor_tensor(xlo[:, 2 * g:2 * g + 2], tcol[:, g % 2], xhi[:, 2 * g:2 * g + 2].bitcast(F32), ALU.subtract)\
                        .then_inc(x_lo, 1)
                for g in range(KT // 2):
                    dve.wait_ge(t_done, t0 + g + 1)
                    if g >= 2:
                        dve.wait_ge(x_lo, 8 * MODS.index(k) + g - 1)
                    for j in range(2):
                        kt = 2 * g + j
                        ins = nc.vector.tensor_scalar(tcol[:, g % 2, j], ps[:, TB[(t0 + g) % 2], j * T:(j + 1) * T],
                                                      gain[:, kt:kt + 1], shift[:, kt:kt + 1], ALU.mult, ALU.add)
                    ins.then_inc(t_free, 1)
                    if g:
                        low(g - 1)
                low(KT // 2 - 1)

            norm_mod("normc", yrow, lambda e: e.wait_ge(ctx_in, 16), mcol[:, 1], modT[:, 0:KT, 1])

            def forget(f, d, c, ready, done):
                l = lb[:, d, c:c + NCH].unsqueeze(1).to_broadcast([P, TH, NCH])

                def add_one():
                    dve.wait_ge(acc_free, ready)
                    step(nc.vector.tensor_scalar(f, f, 1.0, None, ALU.add))
                return {2: add_one, 3: lambda: step(nc.vector.reciprocal(f, f)),
                        4: lambda: step(nc.vector.scalar_tensor_tensor(out=f, in0=l, scalar=-1.0, in1=f, op0=ALU.add, op1=ALU.mult)),
                        5: lambda: nc.vector.tensor_tensor(f, l, f, ALU.subtract).then_inc(done, 1)}

            p0, g0 = plan["ctx"]

            def lower_bound():
                l0, l1 = lg[:, :, 0], lg[:, :, 1]

                def total():
                    dve.wait_ge(lb_exp, 1)
                    step(nc.vector.tensor_tensor(l1, l1, l0, ALU.add))

                def clamp():
                    nc.vector.tensor_scalar(lb[:], l0, 2.0 ** -64, None, ALU.max).then_inc(lb_done, 1)
                    dve.wait_ge(lb_done, 1)
                return {2: total, 3: lambda: step(nc.vector.reciprocal(l1, l1)),
                        5: lambda: step(nc.vector.tensor_tensor(l0, l0, l1, ALU.mult)), 7: clamp}

            def ctx_forget(c):
                return forget(pctx[:, c // 2, :, c % 2 * NCH:(c % 2 + 1) * NCH], c // 2 - 1, c % 2 * NCH, g0 + c + 3, ctx_f)
            for c in range(6):
                chunk(p0 + 8 * c, extra=lower_bound() if c == 1 else ctx_forget(c - 1) if c > 2 else {})
            for f in ctx_forget(5).values():
                f()
            for n in range(4):
                d, cs = n // 2, slice(n % 2 * NCH, (n % 2 + 1) * NCH)
                dve.wait_ge(ctx_k, d + 1)
                dve.wait_ge(cs_exp, n + 1)
                nc.vector.tensor_tensor(dctx[:, d, :, cs], dctx[:, d, :, cs], pctx[:, 1 + d, :, cs], ALU.mult).then_inc(cs_dec, 1)

            norm_mod("norm3", res, lambda e: e.wait_ge(st_out, 4), mcol[:, 0], modT[:, 0:KT, 0])
            p0, g0 = plan["x2"]
            for c in range(14):
                col_, g = c % 2 * NCH, g0 + c

                def x_forget(c=c - 1):
                    return forget(rows5[:, RF + (c - 2) // 2, :, c % 2 * NCH:(c % 2 + 1) * NCH], (c - 2) // 2, c % 2 * NCH,
                                  g0 + c + 3, x_f)

                def gate_conv(c=c - 1):
                    dve.wait_ge(acc_free, g0 + c + 3)
                    s = slice(c % 2 * NCH, (c % 2 + 1) * NCH)
                    nc.vector.tensor_tensor(urow[:, :, s], urow[:, :, s], cgrow[:, :, s], ALU.mult).then_inc(u_done, 1)

                def silu(c=c, g=g, col_=col_):
                    row = rows5[:, RQ + (c - 6) // 2, :, col_:col_ + NCH]
                    dve.wait_ge(sig_done, c - 5)
                    ins = nc.vector.scalar_tensor_tensor(out=row, in0=ps[:, bank(g):bank(g) + 2], scalar=SCALE if c < 8 else 1.0,
                                                         in1=row, op0=ALU.mult, op1=ALU.mult)
                    ins.then_inc(acc_free, 1)
                chunk(p0 + 8 * c, silu if 6 <= c < 10 else None,
                      extra=x_forget() if 3 <= c <= 6 else {5: gate_conv} if c == 13 else {})
            gate_conv(13)

            def decay_unit(n):
                kind, d, m, pair, ne, ns = UNITS[n]
                if n >= 2:
                    if UNITS[n - 2][5] is not None:
                        dve.wait_ge(s_done, UNITS[n - 2][5] + 1)
                    else:
                        dve.wait_ge(o2_done, UNITS[n - 2][3] + 1)
                h = slice(pair % 2 * 2, pair % 2 * 2 + 2)
                kT = (kfT, kbT)[d]
                if kind == "diag":
                    nc.vector.tensor_tensor(kD[:, n % 2], kfT[:, h], kbT[:, h], ALU.add).then_inc(qk_done, 1)
                    return
                dve.wait_ge(d_done, ne + 1)
                if kind == "init":
                    nc.vector.tensor_tensor(qD[:, n % 2], qT[:, h], dec[:, n % 2], ALU.mult).then_inc(qk_done, 1)
                    return
                halves = lambda x, i: x.rearrange("p h (b s m) -> p (h b) s m", s=2, m=m)[:, :, i]
                nc.vector.tensor_tensor(halves(qD[:, n % 2], 1 - d), halves(qT[:, h], 1 - d), halves(dec[:, n % 2], 1 - d), ALU.mult)
                nc.vector.tensor_tensor(halves(kD[:, n % 2], d), halves(kT[:, h], d), halves(dec[:, n % 2], d), ALU.mult)\
                    .then_inc(qk_done, 1)

            def keep_unit(n):
                kind, d, m, pair, ne, ns = UNITS[n]
                if ns is None:
                    return
                dve.wait_ge(s_done, ns + 1)
                dve.wait_ge(s_free, ns)
                if kind == "diag" and pair >= 2:
                    dve.wait_ge(o2_done, pair - 1)
                b = ps[:, 2 + ns % 2].rearrange("p (a b) -> p a b", b=P)
                to = sc[:, pair % 2].rearrange("p h t n -> p (h t) n")
                if kind == "diag":
                    ins = nc.vector.tensor_copy(to, b)
                elif kind == "level":
                    ins = nc.vector.copy_predicated(to, masks[:, LV[m] + d * len(LEVELS)].unsqueeze(1).to_broadcast([P, 4, P]), b)
                else:
                    ins = nc.vector.tensor_copy(cross[:, pair % 2, :, d], b[:, 0:2])
                ins.then_inc(s_free, 1)

            def norm_pair(pair):
                dve.wait_ge(oc_done, pair + 1)
                o = rows5[:, RQ, :, pair * 2 * HD:(pair + 1) * 2 * HD]
                g = rows5[:, RG, :, pair * 2 * HD:(pair + 1) * 2 * HD]
                o3 = o.rearrange("p t (h d) -> p t h d", d=HD)
                sq = nsq[:]
                step(nc.vector.tensor_tensor(sq, o, o, ALU.mult))
                step(nc.vector.tensor_reduce(stat[:, 40:44], sq.rearrange("p t (h d) -> p (t h) d", d=HD), AX_X, ALU.add))
                nc.vector.tensor_scalar(stat[:, 40:44], stat[:, 40:44], 1.0 / HD, EPS, ALU.mult, ALU.add).then_inc(on_ms, 1)
                step(nc.vector.tensor_tensor(g, g, ngain[:, pair % 2 * 2 * HD:(pair % 2 + 1) * 2 * HD].unsqueeze(1).to_broadcast([P, TH, 2 * HD]), ALU.mult))
                dve.wait_ge(on_rstd, pair + 1)
                step(nc.vector.tensor_tensor(o3, o3, stat[:, 44:48].rearrange("p (t h) -> p t h", h=2).unsqueeze(3).to_broadcast([P, TH, 2, HD]), ALU.mult))
                nc.vector.tensor_tensor(o, o, g, ALU.mult).then_inc(on_done, 1)

            dve.wait_ge(clr, 2)
            dve.wait_ge(t_free, TG["u"][0] + 4)
            dve.wait_ge(masks_done, 1)
            for hg in range(2):
                dve.wait_ge(t_free, TG["qk%d" % hg][0] + 6)
                first, last = 2 * hg * PER, 2 * (hg + 1) * PER
                for n in range(first, last + 1):
                    if n < last:
                        decay_unit(n)
                    if n > first:
                        keep_unit(n - 1)
                        if n % PER == 6 and n // PER >= 1 and n // PER % 2 == 1:
                            dve.wait_ge(ng_in, 16 * (hg + 1))
                            norm_pair(n // PER - 1)
                dve.wait_ge(ng_in, 16 * (hg + 1))
                norm_pair(2 * hg + 1)
            bc = lambda x: x.unsqueeze(1).to_broadcast([P, HH, T])

            def ln_centre():
                dve.wait_ge(ln_mean, 1)
                dve.wait_ge(conv_done, len(TAP_UNITS))
                nc.vector.tensor_tensor(yT[:], yT[:], bc(lnm[:]), ALU.subtract).then_inc(ln_cent, 1)

            def ln_mean_square():
                dve.wait_ge(ln_var, 1)
                nc.vector.tensor_scalar(stat[:, 48:50], ps[:, 7, 0:2], 1.0 / DH, EPS, ALU.mult, ALU.add).then_inc(ln_ms, 1)

            def ln_scale():
                dve.wait_ge(ln_rows, 1)
                dve.wait_ge(ln_cent, 1)
                nc.vector.tensor_tensor(yT[:], yT[:], bc(ps[:, 7, 0:T]), ALU.mult).then_inc(ln_norm, 1)

            def ln_silu():
                dve.wait_ge(ln_z, HH)
                nc.vector.tensor_tensor(ysq[:], ysq[:], ysg[:], ALU.mult).then_inc(ln_u, 1)

            def ln_low():
                dve.wait_ge(c_hi, 1)
                nc.vector.tensor_tensor(hlo[:, HH:KT], ysq[:], hhi[:, HH:KT].bitcast(F32), ALU.subtract).then_inc(c_lo, 1)

            def o2_low(g):
                t0, h0 = TG["o2"]
                dve.wait_ge(c_lo, 1)
                dve.wait_ge(t_hi, h0 + g + 1)
                nc.vector.tensor_tensor(hlo[:, 2 * g:2 * g + 2], ps[:, TB[(t0 + g) % 2]].rearrange("p (a b) -> p a b", a=2),
                                        hhi[:, 2 * g:2 * g + 2].bitcast(F32), ALU.subtract).then_inc(t_free, 1)
            p0, g0 = plan["gc"]
            extras = [{5: ln_centre}, {1: ln_mean_square, 5: ln_scale}, {1: ln_silu, 3: ln_low, 6: lambda: o2_low(0), 7: lambda: o2_low(1)},
                      {0: lambda: o2_low(2), 1: lambda: o2_low(3)}]
            for c in range(4):
                chunk(p0 + 8 * c, extra=extras[c])

            def low_parts(name, groups, hi, lo):
                t0, h0 = TG[name]
                for g in range(groups):
                    dve.wait_ge(t_hi, h0 + g + 1)
                    nc.vector.tensor_tensor(lo[:, 2 * g:2 * g + 2], ps[:, TB[(t0 + g) % 2]].rearrange("p (a b) -> p a b", a=2),
                                            hi[:, 2 * g:2 * g + 2].bitcast(F32), ALU.subtract).then_inc(t_free, 1)
            def pairs_of(name, n=8):
                p0, g0 = plan[name]
                with dve.Fori(0, 2) as i:
                    for c in range(2):
                        chunk(i * (2 * n) + (n * c + p0), n=n)

            def gated_by(name, dst, add_to=None):
                p0, g0 = plan[name]
                dve.wait_ge(acc_free, g0 + 2)
                for c in range(4):
                    def f(c=c):
                        s = slice(c * NCH, (c + 1) * NCH)
                        nc.vector.tensor_tensor(dst[:, :, s], ps[:, bank(g0 + c):bank(g0 + c) + 2], dst[:, :, s], ALU.mult).then_inc(acc_free, 1)
                        if add_to is not None:
                            dve.wait_ge(acc_free, g0 + c + 3)
                            nc.vector.tensor_tensor(add_to[:, :, s], add_to[:, :, s], dst[:, :, s], ALU.add).then_inc(merged, 1)
                    chunk(p0 + 4 * c, f, n=4)
            gated_by("pw", yrow)
            pairs_of("gh")
            gated_by("ho", grow, yrow)
            low_parts("y", 8, xhi, xlo)
            pairs_of("wo2")
            dve.wait_ge(reload, 16)
            postnorm("post3", yrow, lambda e: e.wait_ge(acc_free, plan["mlp2"][1] + 2))
            norm_mod("norm4", res, lambda e: e.wait_ge(S["res", "post3"], 2), mcol[:, 2], modT[:, 3 * KT:4 * KT, 0])
            dve.wait_ge(macc_clear, 2)
            with dve.Fori(0, NSB) as i:
                mlp(i, "mlp2")
            dve.wait_ge(m_red, N_MCH + 2)
            step(nc.vector.tensor_tensor(modT[:, NM:, 0], mps[:, NM:, 0], bmod[:, NM:], ALU.add))
            nc.vector.tensor_tensor(mcol[:, 4], modT[:, NM:, 0], col("norm_post_mlp_2"), ALU.mult).then_inc(mcol_done, 1)
            postnorm("post4", yrow, lambda e: e.wait_ge(acc_free, plan["end"][1] + 2))

        @block.gpsimd
        def _(pool):
            half = stat[:, 128:144]
            nc.gpsimd.memset(half, -0.5).then_inc(half_set, 1)
            for n in range(2):
                nc.gpsimd.memset(stat[:, 200 + n:201 + n], 0.0).then_inc(acc_free, 1)
                nc.gpsimd.memset(stat[:, 202 + n:203 + n], 0.0).then_inc(m_red, 1)
                nc.gpsimd.memset(stat[:, 204 + n:205 + n], 0.0).then_inc(sq_done, 1)
            nc.gpsimd.memset(stat[:, 206:207], 0.0).then_inc(m_mul, 16)

            def rstd(k):
                pool.wait_ge(ms_done, RMS[k] + 1)
                nc.gpsimd.tensor_tensor(stat[:, 8:10], stat[:, 4:6], stat[:, 128:130], ALU.pow).then_inc(rstd_done, 1)

            def add_half(k):
                pool.wait_ge(S["scaled", k], 1)
                nc.gpsimd.tensor_tensor(res[:, 0], res[:, 0], xs[:, 0], ALU.add).then_inc(S["res", k], 1)

            pool.wait_ge(half_set, 1)
            rstd("norm0")
            pool.wait_ge(bias_in, 16 * ROWS * B_H)
            pool.wait_ge(early_in, 16)
            b3 = bm[:].rearrange("p t h (a b) -> p (t h a) b", b=GRID)
            nc.gpsimd.tensor_tensor(b3, b3, colmask.unsqueeze(1).to_broadcast([P, TH * B_H * ROWS, GRID]), ALU.add)\
                .then_inc(bias_done, 1)
            for n in range(4):
                pool.wait_ge(qk_ss, n + 1)
                nc.gpsimd.tensor_tensor(stat[:, 24:24 + SET], stat[:, 16:16 + SET], stat[:, 128:128 + SET], ALU.pow)\
                    .then_inc(qk_rstd, 1)
            rstd("post0")
            add_half("post0")
            rstd("norm1")
            pool.wait_ge(S["res", "post0"], 2)
            nc.gpsimd.memset(yrow[:], 0.0).then_inc(macc_clear, 1)

            def mlp(i, k):
                g0 = plan[k][1]
                for j in range(len(SEQ)):
                    if j and SEQ[j - 1][0] == "U":
                        c = SEQ[j - 1][1]
                        for th in range(TH):
                            pool.wait_ge(acc_free, i * len(SEQ) + (g0 + j + 2))
                            pool.wait_ge(t_done, i * 8 + (TG[k][0] + 2 * c))
                            nc.gpsimd.tensor_tensor(sqrow[:, th], rrow[:, th], rrow[:, th], ALU.mult).then_inc(sq_done, 1)

            with pool.Fori(0, NSB) as i:
                mlp(i, "mlp1")
            rstd("post1")
            add_half("post1")
            rstd("norm2")
            rstd("post2")
            add_half("post2")

            rstd("normc")
            pool.wait_ge(lg_in, 16)
            l0, l1 = lg[:, :, 0], lg[:, :, 1]
            nc.gpsimd.tensor_tensor(l1, l1, l0, ALU.subtract).then_inc(pool_own, 1)
            pool.wait_ge(pool_own, 1)
            nc.gpsimd.tensor_scalar(l0, l1, -1.0, 0.0, ALU.mult, ALU.min).then_inc(lb_diff, 1)
            pool.wait_ge(lb_diff, 1)
            nc.gpsimd.tensor_scalar(l1, l1, 0.0, None, ALU.min).then_inc(lb_diff, 1)
            for d in range(2):
                pool.wait_ge(ctx_ln, d + 1)
                nc.gpsimd.tensor_scalar(pctx[:, 1 + d], pctx[:, 1 + d], -1.0, 1.0, ALU.mult, ALU.add).then_inc(ctx_k, 1)
            rstd("norm3")
            pool.wait_ge(masks_in, 16)
            nc.gpsimd.tensor_copy(masks[:], mask_rows[:]).then_inc(masks_done, 1)
            pool.wait_ge(x_f, 4)
            nc.gpsimd.memset(kD[:], 0.0).then_inc(clr, 1)
            nc.gpsimd.memset(qD[:], 0.0).then_inc(clr, 1)
            added = [0]

            def conv(upto):
                for n in range(added[0], min(upto, len(TAP_UNITS))):
                    ct, dd = TAP_UNITS[n]
                    pool.wait_ge(tap_done, n + 2)
                    if TAP_LAST[n] is not None:
                        pool.wait_ge(conv_done, TAP_LAST[n] + 1)
                    two = [tap_two(x, ct, dd) for x in (yT[:, ct:ct + 2], tcol[:, n % 2])]
                    nc.gpsimd.tensor_tensor(two[0], two[0], two[1], ALU.add).then_inc(conv_done, 1)
                    added[0] = n + 1
            for hg in range(2):
                for d in range(2):
                    pool.wait_ge(lf_done, 2 * hg + d + 1)
                    f = rows5[:, RF + d, :, hg * GW:(hg + 1) * GW]
                    nc.gpsimd.tensor_scalar(f, f, -1.0, 1.0, ALU.mult, ALU.add).then_inc(k_done, 1)
                for pair in (2 * hg, 2 * hg + 1):
                    conv((pair + 1) * PER + (4 if pair % 2 == 0 else -1))
                    pool.wait_ge(on_ms, pair + 1)
                    nc.gpsimd.tensor_tensor(stat[:, 44:48], stat[:, 40:44], stat[:, 128:132], ALU.pow).then_inc(on_rstd, 1)
            conv(len(TAP_UNITS))
            pool.wait_ge(ln_ms, 1)
            nc.gpsimd.tensor_tensor(stat[:, 50:52], stat[:, 48:50], stat[:, 128:130], ALU.pow).then_inc(ln_pow, 1)
            rstd("post3")
            add_half("post3")
            rstd("norm4")
            pool.wait_ge(S["res", "post3"], 2)
            nc.gpsimd.memset(yrow[:], 0.0).then_inc(macc_clear, 1)
            with pool.Fori(0, NSB) as i:
                mlp(i, "mlp2")
            rstd("post4")
            add_half("post4")


INPUTS = ["x", "p", "pre_mix_norm", "w_in", "q_norm", "k_norm", "rel_pos_bias", "w_o", "post_mix_norm", "pre_mlp_norm",
          "w_up", "w_down", "post_mlp_norm", "pre_ple_norm", "w_ple_gate", "w_ple_proj", "post_ple_norm", "c_2", "ctx_2",
          "c_ctx_2", "w_mod_2", "b_mod_2", "norm_pre_mix_2", "norm_post_mix_2", "norm_pre_mlp_2", "norm_post_mlp_2",
          "w_in_2", "conv_dw_w_2", "conv_dw_b_2", "conv_ln_g_2", "conv_ln_b_2", "conv_pw_w_2", "hgrn_lb_logits_2",
          "hgrn_norm_g_2", "hgrn_out_w_2", "w_out_2", "mlp_w1_2", "mlp_w2_2"]


def kernel(**inputs):
    import concourse.bacc as bacc
    from concourse.bass_utils import run_bass_kernel_spmd

    nc = bacc.Bacc("TRN2", target_bir_lowering=False, num_devices=1)
    arrays = {name: np.ascontiguousarray(inputs[name]) for name in INPUTS}
    arrays.update(shape_constants())
    I = {name: nc.dram_tensor(name, a.shape, mybir.dt.from_np(a.dtype), kind="ExternalInput").ap()
         for name, a in arrays.items()}
    out = nc.dram_tensor("out", (1, T, D), F32, kind="ExternalOutput").ap()
    build(nc, I, out)
    result = run_bass_kernel_spmd(nc, [arrays], core_ids=[0])
    return result.results[0]["out"]
```
